# Optimizing a Trainium2 kernel written in Bass

```python
import math
import jax, jax.numpy as jnp
from jax import lax
import numpy as np

D_MODEL = 1024
BATCH = 1
SEQ = 256
DEPTH = 2

CTX_LEN = 256
GRID_W = 64
Q_BLOCK = 128
ROPE_BASE = 10000.0
NORM_EPS = 1e-6

MLA_HEADS = 8
MLA_NOPE = 64
MLA_ROPE = 32
MLA_V = 64
Q_LORA = 256
KV_LORA = 128
MLA_WIDTH = MLA_HEADS * MLA_V

CONV_CH = 512
CONV_WIDTH = 31

DIFF_HEADS = 4
DIFF_HD = 64
DIFF_WIDTH = DIFF_HEADS * 2 * DIFF_HD

N_BRANCH = 3
IN_SPLITS = (Q_LORA, KV_LORA, MLA_ROPE, 2 * CONV_CH, DIFF_WIDTH, DIFF_WIDTH, DIFF_WIDTH, N_BRANCH * D_MODEL)
IN_COLS = Q_LORA + KV_LORA + MLA_ROPE + 2 * CONV_CH + 3 * DIFF_WIDTH + N_BRANCH * D_MODEL

N_GROUPS = 4
EXPERTS_PER_GROUP = 8
N_EXPERTS = N_GROUPS * EXPERTS_PER_GROUP
TOP_K_IN_GROUP = 2
EXPERT_FF = 256

kernel_name = 'hybrid_mla_conformer_diffattn_hmoe_block'

def rms_norm(x, g):
    xf = x.astype(jnp.float32)
    y = xf * lax.rsqrt(jnp.mean(xf * xf, axis=-1, keepdims=True) + NORM_EPS)
    return (y * g.astype(jnp.float32)).astype(x.dtype)

def layer_norm(x, g, b):
    xf = x.astype(jnp.float32)
    mu = jnp.mean(xf, axis=-1, keepdims=True)
    var = jnp.mean(jnp.square(xf - mu), axis=-1, keepdims=True)
    y = (xf - mu) * lax.rsqrt(var + NORM_EPS) * g.astype(jnp.float32) + b.astype(jnp.float32)
    return y.astype(x.dtype)

def split_cols(p):
    idx = np.cumsum(np.array(IN_SPLITS))[:-1].tolist()
    return jnp.split(p, idx, axis=-1)

def rope_tables(row, col, rot_dim):
    n = rot_dim // 4
    inv = ROPE_BASE ** (-jnp.arange(n, dtype=jnp.float32) / n)
    ang = jnp.concatenate([row[:, None] * inv, col[:, None] * inv], axis=-1)
    return jnp.cos(ang), jnp.sin(ang)

def rope_2d(x, rope):
    cos, sin = rope
    half = x.shape[-1] // 2
    shape = (x.shape[1],) + (1,) * (x.ndim - 3) + (half,)
    cos = cos.reshape(shape)
    sin = sin.reshape(shape)
    x1, x2 = x[..., :half], x[..., half:]
    return jnp.concatenate([x1 * cos - x2 * sin, x1 * sin + x2 * cos], axis=-1).astype(x.dtype)

def attend(q, k, v, scale):
    s = jnp.einsum('bqhd,bkhd->bhqk', q, k).astype(jnp.float32) * scale
    p = jax.nn.softmax(s, axis=-1).astype(v.dtype)
    return jnp.einsum('bhqk,bkhe->bqhe', p, v)

def diff_attend(q, k, v, lam, scale):
    s = jnp.einsum('bqhmd,bkhmd->bhmqk', q, k).astype(jnp.float32) * scale
    p = jax.nn.softmax(s, axis=-1)
    p = p[:, :, 0] - lam * p[:, :, 1]
    return jnp.einsum('bhqk,bkhe->bqhe', p.astype(v.dtype), v)

def sweep_query_blocks(fn, q):
    b, s = q.shape[:2]
    nb = s // Q_BLOCK
    qb = jnp.moveaxis(q.reshape(b, nb, Q_BLOCK, *q.shape[2:]), 1, 0)
    out = jnp.moveaxis(lax.map(fn, qb), 0, 1)
    return out.reshape(b, s, *out.shape[3:])

def mla_qkv(c_q, c_kv, k_r, q_norm_g, w_uq, kv_norm_g, w_ukv, rope):
    b, s = c_q.shape[:2]
    q = (rms_norm(c_q, q_norm_g) @ w_uq).reshape(b, s, MLA_HEADS, MLA_NOPE + MLA_ROPE)
    kv = (rms_norm(c_kv, kv_norm_g) @ w_ukv).reshape(b, s, MLA_HEADS, MLA_NOPE + MLA_V)
    q_nope, q_rope = q[..., :MLA_NOPE], q[..., MLA_NOPE:]
    k_nope, v = kv[..., :MLA_NOPE], kv[..., MLA_NOPE:]
    k_r = k_r[:, :, None, :]
    if rope is not None:
        q_rope = rope_2d(q_rope, rope)
        k_r = rope_2d(k_r, rope)
    q = jnp.concatenate([q_nope, q_rope], axis=-1)
    k = jnp.concatenate([k_nope, jnp.broadcast_to(k_r, (b, s, MLA_HEADS, MLA_ROPE))], axis=-1)
    return q, k, v

def diff_qkv(q, k, v, rope):
    b, s = q.shape[:2]
    q = q.reshape(b, s, DIFF_HEADS, 2, DIFF_HD)
    k = k.reshape(b, s, DIFF_HEADS, 2, DIFF_HD)
    v = v.reshape(b, s, DIFF_HEADS, 2 * DIFF_HD)
    if rope is not None:
        q = rope_2d(q, rope)
        k = rope_2d(k, rope)
    return q, k, v

def project_branches(h, w_in, q_norm_g, w_uq, kv_norm_g, w_ukv, rope_a, rope_d):
    cq, ckv, kr, glu, dq, dk, dv, gates = split_cols(h @ w_in)
    qa, ka, va = mla_qkv(cq, ckv, kr, q_norm_g, w_uq, kv_norm_g, w_ukv, rope_a)
    qd, kd, vd = diff_qkv(dq, dk, dv, rope_d)
    return qa, ka, va, qd, kd, vd, glu, gates

def conformer_conv(glu_in, conv_w, conv_b, ln_g, ln_b):
    a, g = jnp.split(glu_in, 2, axis=-1)
    u = a * jax.nn.sigmoid(g)
    pad = CONV_WIDTH // 2
    u = lax.conv_general_dilated(u, conv_w[:, None, :].astype(u.dtype), (1,), [(pad, pad)],
                                 dimension_numbers=('NWC', 'WIO', 'NWC'),
                                 feature_group_count=CONV_CH) + conv_b
    return jax.nn.silu(layer_norm(u, ln_g, ln_b))

def merge_branches(gates, o_mla, o_conv, o_diff, w_o_mla, w_o_conv, w_o_diff, w_out):
    g = jax.nn.sigmoid(gates).reshape(*gates.shape[:-1], N_BRANCH, D_MODEL)
    y = (g[..., 0, :] * (o_mla @ w_o_mla) + g[..., 1, :] * (o_conv @ w_o_conv)
         + g[..., 2, :] * (o_diff @ w_o_diff))
    return y @ w_out

def hier_moe(h, w_rg, b_rg, w_re, b_re, w_gate, w_up, w_down):
    b, t = h.shape[:2]
    g_logits = (h @ w_rg + b_rg).astype(jnp.float32)
    g_prob = jax.nn.softmax(g_logits, axis=-1)
    g_sel = jnp.argmax(g_logits, axis=-1)
    p_g = jnp.take_along_axis(g_prob, g_sel[..., None], axis=-1)
    e_logits = (h @ w_re + b_re).astype(jnp.float32).reshape(b, t, N_GROUPS, EXPERTS_PER_GROUP)
    e_in = jnp.take_along_axis(e_logits, g_sel[..., None, None], axis=-2)[..., 0, :]
    top_v, top_i = lax.top_k(e_in, TOP_K_IN_GROUP)
    w = jax.nn.softmax(top_v, axis=-1) * p_g
    eid = g_sel[..., None] * EXPERTS_PER_GROUP + top_i
    combine = jnp.einsum('btk,btke->bte', w, jax.nn.one_hot(eid, N_EXPERTS, dtype=jnp.float32))
    combine = combine.astype(h.dtype).reshape(b, t, N_GROUPS, EXPERTS_PER_GROUP)
    y = jnp.zeros(h.shape, h.dtype)
    for g in range(N_GROUPS):
        sl = slice(g * EXPERTS_PER_GROUP, (g + 1) * EXPERTS_PER_GROUP)
        a = jnp.einsum('btd,edf->btef', h, w_gate[sl])
        u = jnp.einsum('btd,edf->btef', h, w_up[sl])
        hid = jax.nn.silu(a) * u * combine[:, :, g, :, None]
        y = y + jnp.einsum('btef,efd->btd', hid, w_down[sl])
    return y

def hybrid_layer(xl, xc, c, c_ctx, layer_idx, update_ctx, rope_a, rope_d,
                 w_ada, b_ada, norm1_g, w_in, q_norm_g, w_uq, kv_norm_g, w_ukv,
                 conv_w, conv_b, conv_ln_g, conv_ln_b, lam_q1, lam_k1, lam_q2, lam_k2, diff_subln_g,
                 w_o_mla, w_o_conv, w_o_diff, w_out, norm2_g, w_rg, b_rg, w_re, b_re,
                 w_gate, w_up, w_down):
    b, s = xl.shape[:2]
    lam_init = 0.8 - 0.6 * math.exp(-0.3 * layer_idx)
    scale_a = 1.0 / math.sqrt(MLA_NOPE + MLA_ROPE)
    scale_d = 1.0 / math.sqrt(DIFF_HD)
    sh1_l, sc1_l, g1_l, sh2_l, sc2_l, g2_l = jnp.split((jax.nn.silu(c) @ w_ada + b_ada)[:, None, :], 6, axis=-1)
    sh1_c, sc1_c, g1_c, sh2_c, sc2_c, g2_c = jnp.split((jax.nn.silu(c_ctx) @ w_ada + b_ada)[None, None, :], 6, axis=-1)

    hl = rms_norm(xl, norm1_g) * (1 + sc1_l) + sh1_l
    hc = rms_norm(xc, norm1_g) * (1 + sc1_c) + sh1_c
    qa_c, ka_c, va_c, qd_c, kd_c, vd_c, glu_c, gates_c = project_branches(
        hc, w_in, q_norm_g, w_uq, kv_norm_g, w_ukv, None, None)
    qa_l, ka_l, va_l, qd_l, kd_l, vd_l, glu_l, gates_l = project_branches(
        hl, w_in, q_norm_g, w_uq, kv_norm_g, w_ukv, rope_a, rope_d)

    lf = lambda p: p.astype(jnp.float32)
    lam = (jnp.exp(jnp.sum(lf(lam_q1) * lf(lam_k1))) - jnp.exp(jnp.sum(lf(lam_q2) * lf(lam_k2)))
           + lam_init)

    def diff_post(o):
        return (rms_norm(o, diff_subln_g) * (1.0 - lam_init)).reshape(*o.shape[:2], DIFF_WIDTH)

    ka_all = jnp.concatenate([ka_c, ka_l], axis=1)
    va_all = jnp.concatenate([va_c, va_l], axis=1)
    kd_all = jnp.concatenate([kd_c, kd_l], axis=1)
    vd_all = jnp.concatenate([vd_c, vd_l], axis=1)
    o_mla_l = sweep_query_blocks(lambda qb: attend(qb, ka_all, va_all, scale_a), qa_l).reshape(b, s, MLA_WIDTH)
    o_diff_l = diff_post(sweep_query_blocks(lambda qb: diff_attend(qb, kd_all, vd_all, lam, scale_d), qd_l))
    o_conv_l = conformer_conv(glu_l, conv_w, conv_b, conv_ln_g, conv_ln_b)
    xl_new = xl + g1_l * merge_branches(gates_l, o_mla_l, o_conv_l, o_diff_l, w_o_mla, w_o_conv, w_o_diff, w_out)
    h2 = rms_norm(xl_new, norm2_g) * (1 + sc2_l) + sh2_l
    xl_new = xl_new + g2_l * hier_moe(h2, w_rg, b_rg, w_re, b_re, w_gate, w_up, w_down)

    if update_ctx:
        o_mla_c = attend(qa_c, ka_c, va_c, scale_a).reshape(b, xc.shape[1], MLA_WIDTH)
        o_diff_c = diff_post(diff_attend(qd_c, kd_c, vd_c, lam, scale_d))
        o_conv_c = conformer_conv(glu_c, conv_w, conv_b, conv_ln_g, conv_ln_b)
        xc = xc + g1_c * merge_branches(gates_c, o_mla_c, o_conv_c, o_diff_c, w_o_mla, w_o_conv, w_o_diff, w_out)
        h2c = rms_norm(xc, norm2_g) * (1 + sc2_c) + sh2_c
        xc = xc + g2_c * hier_moe(h2c, w_rg, b_rg, w_re, b_re, w_gate, w_up, w_down)
    return xl_new, xc

def setup_inputs(seed: int = 0) -> dict:
    key = jax.random.key(seed)
    ks = iter(jax.random.split(key, 48))
    f32 = jnp.float32

    def nrm(shape, scale):
        return jax.random.normal(next(ks), shape, f32) * scale

    L, D = DEPTH, D_MODEL
    return {
        'x': nrm((BATCH, SEQ, D), 1.0),
        'c': nrm((BATCH, D), 1.0),
        'ctx': nrm((BATCH, CTX_LEN, D), 1.0),
        'c_ctx': nrm((D,), 1.0),
        'w_ada': nrm((L, D, 6 * D), 0.5 * D ** -0.5),
        'b_ada': nrm((L, 6 * D), 0.02),
        'norm1_g': 1.0 + nrm((L, D), 0.02),
        'w_in': nrm((L, D, IN_COLS), D ** -0.5),
        'q_norm_g': 1.0 + nrm((L, Q_LORA), 0.02),
        'w_uq': nrm((L, Q_LORA, MLA_HEADS * (MLA_NOPE + MLA_ROPE)), Q_LORA ** -0.5),
        'kv_norm_g': 1.0 + nrm((L, KV_LORA), 0.02),
        'w_ukv': nrm((L, KV_LORA, MLA_HEADS * (MLA_NOPE + MLA_V)), KV_LORA ** -0.5),
        'conv_w': nrm((L, CONV_WIDTH, CONV_CH), CONV_WIDTH ** -0.5),
        'conv_b': nrm((L, CONV_CH), 0.02),
        'conv_ln_g': 1.0 + nrm((L, CONV_CH), 0.02),
        'conv_ln_b': nrm((L, CONV_CH), 0.02),
        'lam_q1': nrm((L, DIFF_HD), 0.1),
        'lam_k1': nrm((L, DIFF_HD), 0.1),
        'lam_q2': nrm((L, DIFF_HD), 0.1),
        'lam_k2': nrm((L, DIFF_HD), 0.1),
        'diff_subln_g': 1.0 + nrm((L, 2 * DIFF_HD), 0.02),
        'w_o_mla': nrm((L, MLA_WIDTH, D), MLA_WIDTH ** -0.5),
        'w_o_conv': nrm((L, CONV_CH, D), CONV_CH ** -0.5),
        'w_o_diff': nrm((L, DIFF_WIDTH, D), DIFF_WIDTH ** -0.5),
        'w_out': nrm((L, D, D), D ** -0.5),
        'norm2_g': 1.0 + nrm((L, D), 0.02),
        'w_rg': nrm((L, D, N_GROUPS), D ** -0.5),
        'b_rg': nrm((L, N_GROUPS), 0.01),
        'w_re': nrm((L, D, N_EXPERTS), D ** -0.5),
        'b_re': nrm((L, N_EXPERTS), 0.01),
        'w_gate': nrm((L, N_EXPERTS, D, EXPERT_FF), D ** -0.5),
        'w_up': nrm((L, N_EXPERTS, D, EXPERT_FF), D ** -0.5),
        'w_down': nrm((L, N_EXPERTS, EXPERT_FF, D), EXPERT_FF ** -0.5),
        'final_g': 1.0 + nrm((D,), 0.02),
    }

def reference(x, c, ctx, c_ctx, w_ada, b_ada, norm1_g, w_in, q_norm_g, w_uq, kv_norm_g, w_ukv,
              conv_w, conv_b, conv_ln_g, conv_ln_b, lam_q1, lam_k1, lam_q2, lam_k2, diff_subln_g,
              w_o_mla, w_o_conv, w_o_diff, w_out, norm2_g, w_rg, b_rg, w_re, b_re,
              w_gate, w_up, w_down, final_g):
    s = x.shape[1]
    rows = s // GRID_W
    row = jnp.repeat(jnp.arange(rows, dtype=jnp.float32), GRID_W)
    col = jnp.tile(jnp.arange(GRID_W, dtype=jnp.float32), rows)
    rope_a = rope_tables(row, col, MLA_ROPE)
    rope_d = rope_tables(row, col, DIFF_HD)
    xl, xc = x, ctx
    for l in range(DEPTH):
        xl, xc = hybrid_layer(
            xl, xc, c, c_ctx, l, l < DEPTH - 1, rope_a, rope_d,
            w_ada[l], b_ada[l], norm1_g[l], w_in[l], q_norm_g[l], w_uq[l], kv_norm_g[l], w_ukv[l],
            conv_w[l], conv_b[l], conv_ln_g[l], conv_ln_b[l], lam_q1[l], lam_k1[l], lam_q2[l], lam_k2[l],
            diff_subln_g[l], w_o_mla[l], w_o_conv[l], w_o_diff[l], w_out[l], norm2_g[l],
            w_rg[l], b_rg[l], w_re[l], b_re[l], w_gate[l], w_up[l], w_down[l])
    return rms_norm(xl, final_g)


_drawn_inputs = setup_inputs


def setup_inputs(seed=0):
    import zlib

    import numpy as np

    out = dict(_drawn_inputs(seed))
    spreads = {}
    factors = {'norm1_g': 8.0,
     'q_norm_g': 8.0,
     'kv_norm_g': 8.0,
     'conv_b': 6.884,
     'conv_ln_g': 8.0,
     'conv_ln_b': 6.509,
     'lam_k1': 3.659,
     'lam_q2': 4.686,
     'lam_k2': 8.0,
     'diff_subln_g': 7.001,
     'norm2_g': 3.168,
     'b_rg': 8.0,
     'b_re': 6.344,
     'final_g': 2.843}
    for name, (base, spread) in spreads.items():
        noise = np.random.default_rng([zlib.crc32(name.encode()), seed]).standard_normal(out[name].shape)
        drawn = base * np.exp(spread * noise) if base else spread * noise
        out[name] = __import__('jax').numpy.asarray(drawn.astype(out[name].dtype))
    for name, factor in factors.items():
        out[name] = (out[name] * factor).astype(out[name].dtype)
    return out
```

```python
import math
from contextlib import ExitStack

import numpy as np
import concourse.bass as bass
from concourse import mybir

D = 1024
KD = D // 128
SEQ, CTX = 256, 256
T = CTX + SEQ
DEPTH = 2
GRID_W = 64
ROPE_BASE = 10000.0
EPS = 1e-6
HA, NOPE, ROPE, VA = 8, 64, 32, 64
QL, KVL = 256, 128
CC, CW = 512, 31
HD, DH = 4, 64
NG, EG, FF = 4, 8, 256
NE = NG * EG
CT = CC // 128
PAD = CW // 2
UP = 256 + 2 * PAD
LW = QL + KVL + ROPE
SLOT = 4608
NRING = 3
NADA = 12
OVER = 15
NBLK = 48
SCALE_A = 1.0 / math.sqrt(NOPE + ROPE)
SCALE_D = 1.0 / math.sqrt(DH)
ROUND = 12582912.0

VEC = {}
_at = 0
for _n, _w in (("norm1_g", KD), ("norm2_g", KD), ("b_ada", 48), ("q_g", 2), ("kv_g", 1), ("conv_w", CT * CW),
               ("conv_b", CT), ("ln_g", CT), ("ln_b", CT), ("sub_g", 1), ("lams", 4 * DH), ("b_r", NG + NE)):
    VEC[_n] = (_at, _at + _w)
    _at += _w
NV = _at

CON = {}
_at = 0
for _n, _w in (("ident", 128), ("cos_d", SEQ), ("sin_d", SEQ), ("cos_a", SEQ), ("sin_a", SEQ)):
    CON[_n] = (_at, _at + _w)
    _at += _w
NC = _at
RCON = {}
_at = 0
for _n, _w in (("tri", 128), ("desc4", NG), ("desc32", NE), ("expert", NE), ("nth", OVER), ("token", 4)):
    RCON[_n] = (_at, _at + _w)
    _at += _w
NRC = _at


def build(nc, a):
    f32, i32 = mybir.dt.float32, mybir.dt.int32
    ALU, ACT, AX = mybir.AluOpType, mybir.ActivationFunctionType, mybir.AxisListType
    MUL, ADD, SUB = ALU.mult, ALU.add, ALU.subtract
    ctx = ExitStack()

    def sb(name, shape, dt=f32):
        return ctx.enter_context(nc.sbuf_tensor(name, shape, dt))

    def sem(name):
        return ctx.enter_context(nc.semaphore(name))

    def grid(ap, n):
        return ap.rearrange("p (n m) -> p n m", n=n)

    with ctx:
        x = grid(sb("x", [128, KD * T])[:, :], KD)
        h = grid(sb("h", [128, KD * T])[:, :], KD)
        arena = sb("arena", [128, 20720])
        ring = grid(sb("ring", [128, NRING * SLOT])[:, :], NRING)
        qa = grid(arena[:, 0:4096], HA)
        oa = grid(arena[:, 0:4096], HA)[:, 0:8:2, :]
        va = grid(arena[:, 4096:6144], 4)
        qd = grid(arena[:, 6144:8192], HD)
        kd = grid(arena[:, 8192:10240], HD)
        vd = grid(arena[:, 10240:12288], 4)
        ka = grid(arena[:, 12288:16384], HA)
        yt = grid(arena[:, 12288:16384], KD)
        up = arena[:, 16384:16384 + CT * 2 * UP].rearrange("p (c s u) -> p c s u", c=CT, s=2)
        cv = grid(arena[:, 18672:20720], CT)
        lora = grid(sb("lora", [128, 4 * T])[:, :], 4)
        P = grid(sb("P", [128, 4 * 512])[:, :], 4)
        PT = grid(sb("PT", [128, 2 * 512])[:, :], 2)
        con = sb("con", [128, NC])
        vec = grid(sb("vec", [128, 2 * NV])[:, :], 2)
        ones = sb("ones", [128, 128])
        fing = sb("fing", [128, KD])
        silc = sb("silc", [128, 2 * KD * 2])
        ada = [grid(sb(f"ada{l}", [128, 96])[:, :], 48) for l in range(2)]
        mod = [grid(sb(f"mod{l}", [128, 3 * KD * 2])[:, :], 3 * KD) for l in range(2)]
        st = sb("st", [128, 64])
        am = sb("am", [128, 96])
        small = sb("small", [128, 16])
        wr = grid(sb("wr", [128, KD * (NG + NE)])[:, :], KD)
        wd = grid(arena[:, 0:8192], 4)
        gu = [ring[:, 0, 0:4096], ring[:, 1, 0:4096], ring[:, 2, 0:4096], arena[:, 8192:12288]]
        m0 = 12288
        xg = grid(arena[:, m0:m0 + 2048], 2)
        yy = grid(arena[:, m0 + 2048:m0 + 4096], 2)
        stage = grid(arena[:, m0:m0 + 4096], 4)
        xgt = grid(arena[:, m0 + 4096:m0 + 5120], 2)
        gt = grid(arena[:, m0 + 5120:m0 + 5376], 2)
        hid = grid(arena[:, m0 + 5376:m0 + 5632], 2)
        rt = sb("routing", [128, 1824])[:, :]
        rat = [0]

        def rtile(n, dt=f32):
            rat[0] += n
            assert rat[0] <= 1824, rat[0]
            t = rt[:, rat[0] - n:rat[0]]
            return t if dt == f32 else t.bitcast(dt)

        rcon = rtile(NRC)
        lg = grid(rtile(4 * 36), 4)
        g4 = [grid(rtile(16), 4) for _ in range(3)]
        bigs = rtile(8 * 128)
        big = [grid(bigs[:, 128 * n_:128 * n_ + 128], 4) for n_ in range(8)]
        col = [rtile(4) for _ in range(10)]
        c32 = [rtile(32) for _ in range(6)]
        cmp15 = grid(bigs[:, 0:OVER * NE], OVER)
        ov15 = rtile(16)
        icol = rtile(4, i32)
        sl = grid(rtile(8, i32), 2)
        tok = rtile(4, i32)
        meta = [rtile(16, i32) for _ in range(2)]
        idx = rtile(NBLK, i32)
        zero = rtile(NBLK, i32)

        PS = [ctx.enter_context(nc.psum_tensor(f"bank{i}", [128, 512], f32)) for i in range(8)]
        BANK = {"a": PS[0], "d": PS[1]}

        CAP = [T // 8, SEQ // 8]
        h2d = [nc.dram_tensor(f"h2_{l}", [8 * CAP[l], D], f32).ap() for l in range(2)]
        yd = [nc.dram_tensor(f"y_{l}", [CAP[l] * NBLK, D], f32).ap() for l in range(2)]
        td = [nc.dram_tensor(f"tok_{l}", [CAP[l] * NBLK, 1], i32).ap() for l in range(2)]

        full = {"a": sem("act_tile_full"), "d": sem("dve_tile_full")}
        empty = {"a": sem("act_tile_empty"), "d": sem("dve_tile_empty")}
        number = {"a": {}, "d": {}}
        ring_ready = [sem(f"ring_ready{s}") for s in range(NRING)]
        unit_end = {}
        loaded = sem("inputs_loaded")
        x_loaded, router_loaded, table_zero = sem("x_loaded"), sem("router_loaded"), sem("table_zero")
        hid_half, zeroed = sem("hid_half"), sem("zeroed")
        y_zeroed = sem("y_zeroed")
        passed = sem("waits_passed")
        lam_sums, lam_exps = sem("lam_sums"), sem("lam_exps")
        consts_set = sem("consts_set")
        silc_tanh, silc_ready = sem("silc_tanh"), sem("silc_ready")
        dve_step, pool_step = sem("dve_step"), sem("pool_step")
        out_ready, out_stored = sem("out_ready"), sem("out_stored")
        NAMES = ["sq_ready", "stat_ready", "recip_ready", "modded", "shifted",
                 "conv_v", "conv_sq", "conv_scaled", "conv_half", "conv_tanh", "conv_out",
                 "rope_part", "rope_pool", "kr_ready", "kr_copied", "pads_zero", "scores", "scores_max", "exp_ready",
                 "probs_ready", "pt_full", "pt_ready", "pv_full", "attn_out", "merge_part", "yt_ready", "g1_ready", "out_part",
                 "h2_stored", "gexp_in", "gexp", "mask_ready", "slots_ready", "scattered", "idx_loaded", "icol_ready",
                 "xg_ready0", "xg_ready1", "xgt_full", "xgt_ready", "gu_ready0", "gu_ready1", "gu_ready2", "gu_ready3",
                 "wd_ready0", "wd_ready1", "wd_ready2", "wd_ready3", "gu_full", "gtanh", "hid_ready",
                 "y_full", "y_act", "y_dve", "y_stored0", "y_stored1", "yg_ready0", "yg_ready1", "yg_mixed",
                 "ov_w", "ov_icol", "ov_xg", "ov_pe", "ov_act", "ov_dve", "ov_stored"]
        S = [{n: sem(f"{n}_{l}") for n in NAMES} for l in range(DEPTH)]

        def sqt(k):
            return P[:, k, :] if k < 4 else lora[:, k - 4, :]

        def attn_units(l):
            tiles = range(0 if l == 0 else 2, 4)
            seen = [CTX if t < CTX // 128 else T for t in range(4)]
            return ([(i, t, seen[t]) for i in range(HA) for t in tiles],
                    [(i, t, seen[t]) for i in range(HD) for t in tiles])

        def wait_apart(eng, sm, value):
            eng.wait_ge(sm, value)
            eng.sem_inc(passed, 1)

        def con_at(n):
            return con[:, CON[n][0]:CON[n][1]]

        def vec_at(l, n):
            return vec[:, l, VEC[n][0]:VEC[n][1]]

        def rcon_at(n):
            return rcon[:, RCON[n][0]:RCON[n][1]]

        ident = con_at("ident")

        units = [("ada", 0, u) for u in range(4)]
        more = [("ada", 0, u) for u in range(4, NADA)] + [("ada", 1, u) for u in range(NADA)]
        for l in range(DEPTH):
            for kind, n in (("lora", 1), ("glu", 2), ("dq", 1), ("ukv", 1), ("dk", 1), ("dv", 1), ("merge", KD), ("out", 2)):
                for i in range(n):
                    units.append((kind, l, i))
                    take = 2 if kind != "out" else 4
                    if l == 0:
                        units += more[:take]
                        del more[:take]
        assert not more
        unit_no = {u: i for i, u in enumerate(units)}
        first_of_layer1 = unit_no[("lora", 1, 0)]

        block = ctx.enter_context(nc.Block())

        @block.tensor
        def _(pe):
            made = {}

            def begin(b, name):
                n = len(number[b]) + 1
                made["a"], made["d"] = int(b == "a"), int(b == "d")
                assert (name not in number[b])
                number[b][name] = n
                if n > 1:
                    pe.wait_ge(empty[b], n - 1)
                return BANK[b]

            def end(b, ins):
                ins.then_inc(full[b], 1)

            def unit(key):
                n = unit_no[key]
                pe.wait_ge(ring_ready[n % NRING], 16 * (n // NRING + 1))
                return ring[:, n % NRING, :]

            def mm(out, w, rhs, start, stop):
                return nc.tensor.matmul(out, w, rhs, start=start, stop=stop)

            def ada_units(after):
                n = unit_no[after] + 1
                while n < len(units) and units[n][0] == "ada":
                    ada_unit(units[n])
                    n += 1

            def ada_unit(key):
                _, la, u = key
                w = grid(unit(key)[:, 0:4096], KD)
                ps = begin("d", ("ada", la, u))
                for m in range(4):
                    for k in range(KD):
                        last = mm(ps[:, 2 * m:2 * m + 2], w[:, k, 128 * m:128 * m + 128],
                                  silc[:, 2 * k:2 * k + 2], k == 0, k == KD - 1)
                end("d", last)
                used(key)

            def used(key):
                b = max("ad", key=lambda n_: made[n_])
                unit_end[key] = (b, len(number[b]))

            def column_tile(b, name, w, q0, cols=128, kk=KD, src=None):
                ps = begin(b, name)
                for k in range(kk):
                    last = mm(ps[0:cols, 0:T - q0], w(k), src[:, k, q0:T], k == 0, k == kk - 1)
                end(b, last)

            def row_stats(name, parts):
                ps = begin("a", name)
                for c, (src, t) in enumerate(parts):
                    for j, s_ in enumerate(src):
                        last = mm(ps[:, c:c + 1], s_[:, t * 128:t * 128 + 128], ones[:, 0:1],
                                  j == 0, j == len(src) - 1)
                end("a", last)

            def spread(name, cols, q0=0):
                ps = begin("d", name)
                for t, c in cols:
                    last = mm(ps[:, t * 128:t * 128 + 128], st[:, c:c + 1].to_broadcast([128, 128]), ident, True, True)
                end("d", last)

            def norm_stats(l, which, t0, seen):
                pe.wait_ge(S[l]["sq_ready"], seen)
                row_stats((which, l), [([sqt(k) for k in range(KD)], t) for t in range(t0, 4)])

            pe.wait_ge(loaded, 16 * 5)
            pe.wait_ge(consts_set, 2)
            pe.wait_ge(silc_ready, 1)
            for u in range(4):
                ada_unit(("ada", 0, u))

            for l in range(DEPTH):
                s = S[l]
                q0 = 0 if l == 0 else CTX
                qt0 = q0 // 128
                norm_stats(l, "n1", 0, KD)
                pe.wait_ge(s["recip_ready"], 1)
                spread(("n1b", l), [(t, t) for t in range(4)])
                pe.wait_ge(s["shifted"], 2 * KD)
                w = grid(unit(("lora", l, 0))[:, 0:KD * LW], KD)
                for i, (b, c0, cols, qq) in enumerate((("a", 0, 128, q0), ("d", 128, 128, q0),
                                                      ("a", 256, 128, 0), ("d", 384, 32, 0))):
                    column_tile(b, ("lora", l, i), lambda k: w[:, k, c0:c0 + cols], qq, cols, KD, h)
                used(("lora", l, 0))
                ada_units(("lora", l, 0))
                for j in range(2):
                    w = unit(("glu", l, j))[:, 0:4096].rearrange("p (k n m) -> p k n m", k=KD, n=4)
                    for i in range(2):
                        column_tile("a", ("gluG", l, 2 * j + i), lambda k: w[:, k, 2 * i + 1, :], q0, 128, KD, h)
                        column_tile("d", ("gluA", l, 2 * j + i), lambda k: w[:, k, 2 * i, :], q0, 128, KD, h)
                    used(("glu", l, j))
                    ada_units(("glu", l, j))
                    if j == 0:
                        pe.wait_ge(s["stat_ready"], 1)
                        row_stats(("loraS", l), [([P[:, 0], P[:, 1]], t) for t in range(qt0, 4)]
                                  + [([P[:, 2]], t) for t in range(4)])
                pe.wait_ge(s["recip_ready"], 2)
                spread(("loraQ", l), [(t, 8 + t - qt0) for t in range(qt0, 4)])
                spread(("loraK", l), [(t, 8 + 4 - qt0 + t) for t in range(4)])
                w = grid(unit(("dq", l, 0))[:, 0:4096], KD)
                for i in range(HD):
                    column_tile("ad"[i % 2], ("dq", l, i), lambda k: w[:, k, 128 * i:128 * i + 128], q0, 128, KD, h)
                used(("dq", l, 0))
                ada_units(("dq", l, 0))
                pe.wait_ge(empty["d"], number["d"][("loraK", l)])
                w = unit(("ukv", l, 0))
                wq, wkv = grid(w[:, 0:1536], 2), w[:, 1536:2560]
                for i in range(HA):
                    column_tile("ad"[i % 2], ("uq", l, i), lambda k: wq[:, k, 96 * i:96 * i + 96], q0, 96, 2, lora)
                for i in range(HA):
                    column_tile("ad"[i % 2], ("uk", l, i), lambda k: wkv[:, 128 * i:128 * i + 64], 0, 64, 1, lora[:, 2:3])
                for t in range(4):
                    b = "ad"[t % 2]
                    ps = begin(b, ("uv", l, t))
                    end(b, mm(ps[:, :], lora[:, 2, t * 128:t * 128 + 128],
                              wkv.rearrange("p (h n) -> p h n", h=HA)[:, :, NOPE:], True, True))
                used(("ukv", l, 0))
                ada_units(("ukv", l, 0))
                w = grid(unit(("dk", l, 0))[:, 0:4096], KD)
                for i in range(HD):
                    column_tile("ad"[i % 2], ("dk", l, i), lambda k: w[:, k, 128 * i:128 * i + 128], 0, 128, KD, h)
                used(("dk", l, 0))
                ada_units(("dk", l, 0))
                w = grid(unit(("dv", l, 0))[:, 0:4096], KD)
                for t in range(4):
                    b = "ad"[t % 2]
                    ps = begin(b, ("dv", l, t))
                    for k in range(KD):
                        last = mm(ps[:, :], h[:, k, t * 128:t * 128 + 128], w[:, k, :], k == 0, k == KD - 1)
                    end(b, last)
                used(("dv", l, 0))
                ada_units(("dv", l, 0))
                pe.wait_ge(s["conv_v"], 1)
                row_stats(("lnM", l), [([cv[:, c] for c in range(CT)], t) for t in range(qt0, 4)])
                pe.wait_ge(empty["a"], number["a"][("lnM", l)])
                spread(("lnMb", l), [(t, 16 + t - qt0) for t in range(qt0, 4)])
                pe.wait_ge(s["conv_sq"], CT)
                row_stats(("lnV", l), [([P[:, c] for c in range(CT)], t) for t in range(qt0, 4)])
                pe.wait_ge(s["recip_ready"], 3)
                spread(("lnVb", l), [(t, 24 + t - qt0) for t in range(qt0, 4)])

                AU, DU = attn_units(l)
                n_all = len(AU) + len(DU)
                for b in "ad":
                    pe.wait_ge(empty[b], len(number[b]))
                pe.wait_ge(s["rope_pool"], 3)
                pe.wait_ge(s["kr_copied"], 1)

                def scores_a(u):
                    i, t, nk = AU[u]
                    if u >= 4:
                        pe.wait_ge(s["exp_ready"], u - 3)
                    mm(PS[2 + u % 4][:, 0:nk], qa[0:96, i, t * 128:t * 128 + 128], ka[0:96, i, 0:nk], True, True) \
                        .then_inc(s["scores"], 1)

                def scores_d(u):
                    i, t, nk = DU[u]
                    g = len(AU) + 2 * u
                    pe.wait_ge(s["exp_ready"], len(AU) if u < 2 else g - 2)
                    for m in range(2):
                        mm(PS[2 + 2 * (u % 2) + m][:, 0:nk], qd[64 * m:64 * m + 64, i, t * 128:t * 128 + 128],
                           kd[64 * m:64 * m + 64, i, 0:nk], True, True).then_inc(s["scores"], 1)

                def turn(g, src, nk):
                    pe.wait_ge(s["probs_ready"], g + 1)
                    if g >= 1:
                        pe.wait_ge(s["pt_ready"], g)
                    for kt in range(nk // 128):
                        last = nc.tensor.transpose(PS[6][:, kt * 128:kt * 128 + 128],
                                                   src[:, kt * 128:kt * 128 + 128], ident)
                    last.then_inc(s["pt_full"], 1)

                def values(g, lhs, out, nk):
                    pe.wait_ge(s["pt_ready"], g + 1)
                    if g >= 1:
                        pe.wait_ge(s["attn_out"], g)
                    for kt in range(nk // 128):
                        last = mm(out, lhs(kt), PT[:, g % 2, kt * 128:kt * 128 + 128], kt == 0, kt == nk // 128 - 1)
                    last.then_inc(s["pv_full"], 1)

                def values_a(u):
                    i, t, nk = AU[u]
                    r = 64 * (i % 2)
                    values(u, lambda kt: va[:, kt, 64 * i:64 * i + 64], PS[7][r:r + 64, 0:128], nk)

                def values_d(u):
                    i, t, nk = DU[u]
                    values(len(AU) + u, lambda kt: vd[:, kt, 128 * i:128 * i + 128], PS[7][:, 0:128], nk)

                scores_a(0)
                scores_a(1)
                for u in range(len(AU)):
                    if u + 2 < len(AU):
                        scores_a(u + 2)
                    turn(u, P[:, u % 4], AU[u][2])
                    if u >= 1:
                        values_a(u - 1)
                scores_d(0)
                values_a(len(AU) - 1)
                for u in range(len(DU)):
                    if u + 1 < len(DU):
                        scores_d(u + 1)
                    turn(len(AU) + u, P[:, 2 * (u % 2)], DU[u][2])
                    if u >= 1:
                        values_d(u - 1)
                values_d(len(DU) - 1)
                pe.wait_ge(s["stat_ready"], 1 + HD)
                row_stats(("dn", l), [([P[:, i]], t) for i in range(HD) for t in range(qt0, 4)])
                pe.wait_ge(s["recip_ready"], 4)
                for i in range(HD):
                    spread(("dnb", l, i), [(t, 32 + i * (4 - qt0) + t - qt0) for t in range(qt0, 4)])
                pe.wait_ge(empty["d"], number["d"][("dnb", l, HD - 1)])
                pe.wait_ge(s["conv_out"], CT)
                for c in range(KD):
                    w = unit(("merge", l, c))
                    wg = w[:, 0:3072].rearrange("p (k n m) -> p k n m", k=KD, n=3)
                    wo = grid(w[:, 3072:4608], 12)
                    for b in range(3):
                        column_tile("a", ("gate", l, c, b), lambda k: wg[:, k, b, :], q0, 128, KD, h)
                        column_tile("d", ("branch", l, c, b), lambda k: wo[:, 4 * b + k, :], q0, 128, 4, (oa, cv, qd)[b])
                    used(("merge", l, c))
                    ada_units(("merge", l, c))
                pe.wait_ge(s["yt_ready"], KD)
                for c in range(KD):
                    if c % 4 == 0:
                        w = unit(("out", l, c // 4))[:, 0:4096].rearrange("p (k n m) -> p k n m", k=KD, n=4)
                    column_tile("ad"[c % 2], ("out", l, c), lambda k: w[:, k, c % 4, :], q0, 128, KD, yt)
                    if c % 4 == 3:
                        used(("out", l, c // 4))
                        ada_units(("out", l, c // 4))
                norm_stats(l, "n2", qt0, 2 * KD)
                pe.wait_ge(s["recip_ready"], 5)
                spread(("n2b", l), [(t, 48 + t - qt0) for t in range(qt0, 4)])
                pe.wait_ge(s["shifted"], 2 * KD + (2 if l == 0 else 1) * KD)
                pe.wait_ge(router_loaded, 16 * (l + 1))
                ps = begin("d", ("router", l))
                for t in range(qt0, 4):
                    for k in range(KD):
                        last = mm(ps[:, (t - qt0) * 36:(t - qt0) * 36 + 36], h[:, k, t * 128:t * 128 + 128],
                                  wr[:, k, :], k == 0, k == KD - 1)
                end("d", last)
                for t in range(qt0, 4):
                    for half in range(2):
                        b = "ad"[half]
                        ps = begin(b, ("h2", l, t, half))
                        for k in range(4):
                            last = nc.tensor.transpose(ps[:, k * 128:k * 128 + 128],
                                                       h[:, 4 * half + k, t * 128:t * 128 + 128], ident)
                        end(b, last)
                TT = 4 - qt0
                pe.wait_ge(s["mask_ready"], 1)
                ps = begin("d", ("rank", l))
                for t in range(TT):
                    for j in range(t + 1):
                        mm(ps[:, t * 32:t * 32 + 32], ones[:, :] if j < t else rcon_at("tri"), big[4][:, j, :], j == 0, j == t)
                for j in range(TT):
                    last = mm(ps[:, 128:160], ones[:, :], big[4][:, j, :], j == 0, j == TT - 1)
                end("d", last)

                C = (T - q0) // 8

                def gather_turn(par, full_sem):
                    for k in range(KD):
                        last = nc.tensor.transpose(PS[2 + par][:, k * C:k * C + C], xg[0:C, par, k * 128:k * 128 + 128],
                                                   ident[0:C, 0:C])
                    last.then_inc(full_sem, 1)

                def up_products(par, slot, full_sem):
                    w = slot.rearrange("p (g k n m) -> p g k n m", g=2, k=KD, n=2)
                    for g in range(2):
                        for n in range(2):
                            for k in range(KD):
                                last = mm(PS[4 + par][:, (2 * g + n) * C:(2 * g + n) * C + C], w[:, g, k, n, :],
                                          xgt[:, par, k * C:k * C + C], k == 0, k == KD - 1)
                    last.then_inc(full_sem, 1)

                def down_products(par, slot, full_sem):
                    w = grid(slot, 2)
                    for n in range(2):
                        for k in range(2):
                            last = mm(PS[6 + n][0:C, :], hid[:, par, k * C:k * C + C], w[:, k, n * 512:n * 512 + 512],
                                      k == 0, k == 1)
                    last.then_inc(full_sem, 1)

                def do_turn(j, i):
                    wait_apart(pe, s[f"xg_ready{j % 2}"], i * 32 + 16 * (j // 2 + 1))
                    if not (isinstance(i, int) and 4 * i + j < 2):
                        wait_apart(pe, s["xgt_ready"], i * 4 + j - 1)
                    gather_turn(j % 2, s["xgt_full"])

                def do_up(j, i):
                    pe.wait_ge(s[f"gu_ready{j}"], i * 32 + 32)
                    pe.wait_ge(s["xgt_ready"], i * 4 + j + 1)
                    if not (isinstance(i, int) and 4 * i + j < 2):
                        pe.wait_ge(s["hid_ready"], i * 4 + j - 1)
                    up_products(j % 2, gu[j], s["gu_full"])

                def do_down(j, i):
                    pe.wait_ge(s[f"wd_ready{j}"], i * 16 + 16)
                    pe.wait_ge(s["hid_ready"], i * 4 + j + 1)
                    if not (isinstance(i, int) and 4 * i + j < 1):
                        pe.wait_ge(s["y_act"], i * 4 + j)
                        pe.wait_ge(s["y_dve"], i * 4 + j)
                    down_products(j % 2, wd[:, j, :], s["y_full"])

                def group(i, first, last):
                    for j in range(4):
                        do_up(j, i)
                        if not (last and j == 3):
                            jn, inn = (j + 1, i) if j < 3 else (0, i + 1)
                            do_turn(jn, inn)
                        if not (first and j == 0):
                            jp, ip = (j - 1, i) if j > 0 else (3, i - 1)
                            do_down(jp, ip)

                do_turn(0, 0)
                group(0, True, False)
                with pe.Fori(1, NE // 4 - 1) as i:
                    group(i, False, False)
                group(NE // 4 - 1, False, True)
                do_down(3, NE // 4 - 1)
                nx = pe.value_load(meta[l][0:1, 15:16], min_val=0, max_val=OVER)
                with pe.If(nx > 0):
                    with pe.Fori(0, OVER) as j:
                        with pe.If(nx > j):
                            wait_apart(pe, s["ov_xg"], 16 * j + 16)
                            gather_turn(0, s["ov_pe"])
                            pe.wait_ge(s["ov_w"], 48 * j + 48)
                            pe.wait_ge(s["ov_act"], 3 * j + 1)
                            up_products(0, gu[3], s["ov_pe"])
                            pe.wait_ge(s["ov_dve"], 3 * j + 2)
                            down_products(0, wd[:, 3, :], s["ov_pe"])
                for t in range(qt0, 4):
                    pe.wait_ge(s["yg_mixed"], t - qt0 + 1)
                    for half in range(2):
                        ps = begin("d", ("mix", l, t, half))
                        for k in range(4):
                            last = nc.tensor.transpose(ps[:, k * 128:k * 128 + 128],
                                                       xg[:, (t - qt0) % 2, (4 * half + k) * 128:(4 * half + k) * 128 + 128],
                                                       ident)
                        end("d", last)
            s = S[1]
            norm_stats(1, "nf", 2, 3 * KD)
            pe.wait_ge(s["recip_ready"], 6)
            spread(("nfb", 1), [(t, 52 + t - 2) for t in range(2, 4)])

        @block.scalar
        def _(act):
            A, Dn = number["a"], number["d"]
            own = [0]

            def f(out, in_, fn, **kw):
                return nc.scalar.activation(out, in_, fn, **kw)

            eps = small[:, 0:1]

            def take(key):
                act.wait_ge(full["a"], A[key])

            def give(ins):
                ins.then_inc(empty["a"], 1)

            def squares(s, t0, last):
                for k in range(KD):
                    f(sqt(k)[:, t0 * 128:T], x[:, k, t0 * 128:T], ACT.Square).then_inc(s["sq_ready"], 1)

            def root(key, c0, n, scale, psc=0, done=True):
                ins = f(st[:, c0:c0 + n], PS[0][:, psc:psc + n], ACT.Sqrt, scale=scale, bias=eps)
                if done:
                    give(ins)

            def shifts(s, l, name, segs, col0, base):
                n = 0
                for k in range(KD):
                    for v, t0, t1 in segs:
                        n += 1
                        if n < KD * len(segs):
                            act.wait_ge(s["modded"], base + n)
                        else:
                            act.wait_ge(empty["d"], Dn[name])
                        f(h[:, k, t0:t1], h[:, k, t0:t1], ACT.Identity, bias=ada[l][:, col0 + k, v:v + 1]) \
                            .then_inc(s["shifted"], 1)

            BOTH = [(1, 0, CTX), (0, CTX, T)]
            act.wait_ge(loaded, 16 * 5)
            f(silc[:, 0:16], silc[:, 16:32], ACT.Tanh, scale=0.5).then_inc(silc_tanh, 1)
            act.wait_ge(lam_sums, 1)
            f(small[:, 5:9], small[:, 1:5], ACT.Exp).then_inc(lam_exps, 1)
            act.wait_ge(consts_set, 2)
            act.wait_ge(x_loaded, 16)
            for l in range(DEPTH):
                s = S[l]
                q0 = 0 if l == 0 else CTX
                qt0, NQ = q0 // 128, T - q0
                nt = 4 - qt0
                SEGS = BOTH if l == 0 else BOTH[1:]
                if l == 1:
                    act.wait_ge(empty["d"], Dn[("mix", 0, 3, 1)])
                squares(s, 0, None)
                take(("n1", l))
                root(("n1", l), 0, 4, 1.0 / D)
                shifts(s, l, ("n1b", l), BOTH, 0, 0)
                for i, p in ((0, 0), (2, 2)):
                    take(("lora", l, i))
                    t0 = q0 if i == 0 else 0
                    f(lora[:, i, t0:T], PS[0][:, 0:T - t0], ACT.Copy)
                    give(f(P[:, p, t0:T], PS[0][:, 0:T - t0], ACT.Square))
                    if i == 0:
                        act.wait_ge(empty["d"], Dn[("lora", l, 1)])
                        f(P[:, 1, q0:T], lora[:, 1, q0:T], ACT.Square)
                f(small[:, 15:16], small[:, 15:16], ACT.Copy).then_inc(s["stat_ready"], 1)
                for j in range(CT):
                    take(("gluG", l, j))
                    if j >= 2:
                        act.wait_ge(empty["d"], Dn[("gluA", l, j - 2)])
                    give(f(PT[:, j % 2, q0:T], PS[0][:, 0:NQ], ACT.Tanh, scale=0.5))
                    if j == 1:
                        take(("loraS", l))
                        root(None, 8, nt, 1.0 / QL, 0, False)
                        root(None, 8 + nt, 4, 1.0 / KVL, nt)
                for i in range(0, HD, 2):
                    take(("dq", l, i))
                    give(f(qd[:, i, q0:T], PS[0][:, 0:NQ], ACT.Copy))
                act.wait_ge(y_zeroed, 16 * DEPTH)
                for i in range(0, HA, 2):
                    take(("uq", l, i))
                    give(f(qa[0:96, i, q0:T], PS[0][0:96, 0:NQ], ACT.Copy))
                for i in range(0, HA, 2):
                    take(("uk", l, i))
                    give(f(ka[0:64, i, :], PS[0][0:64, :], ACT.Copy))
                for t in range(0, 4, 2):
                    take(("uv", l, t))
                    give(f(va[:, t, :], PS[0][:, :], ACT.Copy))
                for i in range(0, HD, 2):
                    take(("dk", l, i))
                    give(f(kd[:, i, :], PS[0][:, :], ACT.Copy))
                for t in range(0, 4, 2):
                    take(("dv", l, t))
                    give(f(vd[:, t, :], PS[0][:, :], ACT.Copy))
                take(("lnM", l))
                give(f(st[:, 16:16 + nt], PS[0][:, 0:nt], ACT.Copy, scale=1.0 / CC))
                act.wait_ge(empty["d"], Dn[("lnMb", l)])
                act.wait_ge(s["rope_pool"], 3)
                for c in range(CT):
                    f(P[:, c, q0:T], cv[:, c, q0:T], ACT.Square).then_inc(s["conv_sq"], 1)
                take(("lnV", l))
                root(None, 24, nt, 1.0 / CC)
                for c in range(CT):
                    if c < CT - 1:
                        act.wait_ge(s["conv_scaled"], c + 1)
                    else:
                        act.wait_ge(empty["d"], Dn[("lnVb", l)])
                    f(cv[:, c, q0:T], cv[:, c, q0:T], ACT.Identity, scale=0.5, bias=vec_at(l, "ln_b")[:, c:c + 1]) \
                        .then_inc(s["conv_half"], 1)
                    act.wait_ge(s["conv_half"], c + 1)
                    f(P[:, c, q0:T], cv[:, c, q0:T], ACT.Tanh).then_inc(s["conv_tanh"], 1)
                act.wait_ge(s["conv_out"], CT)
                AU, DU = attn_units(l)
                nA = len(AU)

                def exp_a(u):
                    i, t, nk = AU[u]
                    c = 8 * (u % 8)
                    act.wait_ge(s["scores_max"], u + 1)
                    if u >= 4:
                        act.wait_ge(s["pt_full"], u - 3)
                    f(P[:, u % 4, 0:nk], PS[2 + u % 4][:, 0:nk], ACT.Exp, scale=SCALE_A, bias=am[:, c + 2:c + 3],
                      accum_out=am[:, c + 4:c + 5]).then_inc(s["exp_ready"], 1)

                def exp_d(u):
                    i, t, nk = DU[u]
                    c = 8 * ((nA + u) % 8)
                    act.wait_ge(s["scores_max"], nA + u + 1)
                    act.wait_ge(s["pt_full"], nA + max(u - 1, 0))
                    for m in range(2):
                        f(P[:, 2 * (u % 2) + m, 0:nk], PS[2 + 2 * (u % 2) + m][:, 0:nk], ACT.Exp, scale=SCALE_D,
                          bias=am[:, c + 2 + m:c + 3 + m], accum_out=am[:, c + 4 + m:c + 5 + m]) \
                            .then_inc(s["exp_ready"], 1)

                def pt_copy(g, nk):
                    act.wait_ge(s["pt_full"], g + 1)
                    if g >= 2:
                        act.wait_ge(s["pv_full"], g - 1)
                    f(PT[:, g % 2, 0:nk], PS[6][:, 0:nk], ACT.Copy).then_inc(s["pt_ready"], 1)

                exp_a(0)
                exp_a(1)
                for u in range(nA):
                    if u + 2 < nA:
                        exp_a(u + 2)
                    pt_copy(u, AU[u][2])
                exp_d(0)
                for u in range(len(DU)):
                    if u + 1 < len(DU):
                        exp_d(u + 1)
                    pt_copy(nA + u, DU[u][2])
                act.wait_ge(s["attn_out"], nA + len(DU))
                for i in range(HD):
                    f(P[:, i, q0:T], qd[:, i, q0:T], ACT.Square).then_inc(s["stat_ready"], 1)
                take(("dn", l))
                root(None, 32, HD * nt, 1.0 / (2 * DH))
                for n in range(3 * KD):
                    c, b = divmod(n, 3)
                    take(("gate", l, c, b))
                    if n >= 2:
                        act.wait_ge(empty["d"], Dn[("branch", l, (n - 2) // 3, (n - 2) % 3)])
                    give(f(P[:, n % 2, q0:T], PS[0][:, 0:NQ], ACT.Tanh, scale=0.5))
                act.wait_ge(s["g1_ready"], 1)
                for c in range(0, KD, 2):
                    take(("out", l, c))
                    j = (c // 2) % 2
                    if c >= 4:
                        act.wait_ge(s["out_part"], c // 2 - 1)
                    for v, t0, t1 in SEGS:
                        ins = f(P[:, j, t0:t1], PS[0][:, t0 - q0:t1 - q0], ACT.Copy,
                                scale=mod[l][:, 2 * KD + c, v:v + 1])
                    give(ins)
                act.wait_ge(s["out_part"], KD // 2)
                act.wait_ge(empty["d"], Dn[("out", l, KD - 1)])
                squares(s, qt0, None)
                take(("n2", l))
                root(None, 48, nt, 1.0 / D)
                shifts(s, l, ("n2b", l), SEGS, 3 * KD, 2 * KD - 1)
                for t in range(nt):
                    take(("h2", l, qt0 + t, 0))
                    give(f(stage[:, t, 0:512], PS[0][:, :], ACT.Copy))
                    act.wait_ge(empty["a"], A[("h2", l, qt0 + t, 0)])
                    act.wait_ge(empty["d"], Dn[("h2", l, qt0 + t, 1)])
                    act.dma_start(h2d[l][t * 128:t * 128 + 128, :], stage[:, t, :]).then_inc(s["h2_stored"], 16)
                act.wait_ge(s["gexp_in"], 1)
                f(g4[1][:, 0:nt, :], g4[0][:, 0:nt, :], ACT.Exp)
                f(col[5][:, 0:nt], col[4][:, 0:nt], ACT.Exp).then_inc(s["gexp"], 1)
                C = NQ // 8
                yrow = yd[l].rearrange("(r b) d -> r b d", b=NBLK)

                def xgt_copy(j, i):
                    act.wait_ge(s["xgt_full"], i * 4 + j + 1)
                    if not (isinstance(i, int) and 4 * i + j < 2):
                        act.wait_ge(s["gu_full"], i * 4 + j - 1)
                    f(xgt[:, j % 2, 0:KD * C], PS[2 + j % 2][:, 0:KD * C], ACT.Copy).then_inc(s["xgt_ready"], 1)

                def gate_tanh(j, i):
                    act.wait_ge(s["gu_full"], i * 4 + j + 1)
                    if not (isinstance(i, int) and 4 * i + j < 2):
                        act.wait_ge(s["hid_ready"], i * 4 + j - 1)
                    f(gt[:, j % 2, 0:2 * C], PS[4 + j % 2][:, 0:2 * C], ACT.Tanh, scale=0.5).then_inc(s["gtanh"], 1)

                def y_out(j, i):
                    p = j % 2
                    act.wait_ge(s["y_full"], i * 4 + j + 1)
                    if not (isinstance(i, int) and 4 * i + j < 2):
                        act.wait_ge(s[f"y_stored{p}"], i * 32 + 16 * (j // 2))
                    f(yy[0:C, p, 0:512], PS[6][0:C, :], ACT.Copy).then_inc(s["y_act"], 1)
                    act.wait_ge(s["y_act"], i * 4 + j + 1)
                    act.wait_ge(s["y_dve"], i * 4 + j + 1)
                    act.dma_start(yrow[0:C, bass.ds(i * 4 + j, 1), :], yy[0:C, p:p + 1, :]) \
                        .then_inc(s[f"y_stored{p}"], 16)

                def group(i, first, last):
                    for j in range(4):
                        gate_tanh(j, i)
                        if not (last and j == 3):
                            xgt_copy((j + 1) % 4, i + (j + 1) // 4)
                        if not (first and j == 0):
                            y_out((j - 1) % 4, i - (j == 0))

                xgt_copy(0, 0)
                group(0, True, False)
                with act.Fori(1, NE // 4 - 1) as i:
                    group(i, False, False)
                group(NE // 4 - 1, False, True)
                y_out(3, NE // 4 - 1)
                nx = act.value_load(meta[l][0:1, 15:16], min_val=0, max_val=OVER)
                with act.If(nx > 0):
                    act.wait_ge(s["y_stored0"], 16 * NE // 2)
                    with act.Fori(0, OVER) as j:
                        with act.If(nx > j):
                            act.wait_ge(s["ov_pe"], 3 * j + 1)
                            f(xgt[:, 0, 0:KD * C], PS[2][:, 0:KD * C], ACT.Copy).then_inc(s["ov_act"], 1)
                            act.wait_ge(s["ov_pe"], 3 * j + 2)
                            f(gt[:, 0, 0:2 * C], PS[4][:, 0:2 * C], ACT.Tanh, scale=0.5).then_inc(s["ov_act"], 1)
                            act.wait_ge(s["ov_pe"], 3 * j + 3)
                            f(yy[0:C, 0, 0:512], PS[6][0:C, :], ACT.Copy).then_inc(s["ov_act"], 1)
                            act.wait_ge(s["ov_act"], 3 * j + 3)
                            act.wait_ge(s["ov_dve"], 3 * j + 3)
                            act.dma_start(yrow[0:C, bass.ds(NE + j, 1), :], yy[0:C, 0:1, :]).then_inc(s["ov_stored"], 16)
                            wait_apart(act, s["ov_stored"], 16 * j + 16)
            act.wait_ge(empty["d"], Dn[("mix", 1, 3, 1)])
            squares(S[1], 2, None)
            take(("nf", 1))
            root(None, 52, 2, 1.0 / D)

        @block.vector
        def _(dve):
            A, Dn = number["a"], number["d"]
            own = [0]
            V = nc.vector

            def step(ins):
                own[0] += 1
                ins.then_inc(dve_step, 1)
                dve.wait_ge(dve_step, own[0])

            def stt(out, in0, sc, in1, op0=MUL, op1=MUL):
                return V.scalar_tensor_tensor(out, in0, sc, in1, op0=op0, op1=op1)

            def take(key):
                dve.wait_ge(full["d"], Dn[key])

            def give(ins):
                ins.then_inc(empty["d"], 1)

            def ada_evac(key):
                _, la, u = key
                take(key)
                give(V.tensor_tensor(ada[la][:, 4 * u:4 * u + 4, :], grid(PS[1][:, 0:8], 4),
                                     vec_at(la, "b_ada")[:, 4 * u:4 * u + 4].unsqueeze(2).to_broadcast([128, 4, 2]), op=ADD))

            def ada_after(key):
                n = unit_no[key] + 1
                while n < len(units) and units[n][0] == "ada":
                    ada_evac(units[n])
                    n += 1

            def scales(l, which):
                dve.wait_ge(empty["d"], max(Dn[("ada", l, u)] for u in {0: (0, 1, 2, 3), 1: (8, 9), 2: (4, 5)}[which]))
                if which == 2:
                    V.tensor_scalar(mod[l][:, 16:24, :], ada[l][:, 16:24, :], 0.5, None, MUL).then_inc(S[l]["g1_ready"], 1)
                    dve.wait_ge(S[l]["g1_ready"], 1)
                    return
                c0 = (KD, 4 * KD)[which]
                g = vec_at(l, ("norm1_g", "norm2_g")[which]).unsqueeze(2).to_broadcast([128, KD, 2])
                step(stt(mod[l][:, which * KD:which * KD + KD, :], ada[l][:, c0:c0 + KD, :], 1.0, g, ADD, MUL))

            def recip(s, c0, n, key):
                dve.wait_ge(empty["a"], A[key])
                V.reciprocal(st[:, c0:c0 + n], st[:, c0:c0 + n]).then_inc(s["recip_ready"], 1)

            def norm_apply(l, s, key, segs, which, q0):
                take(key)
                for k in range(KD):
                    for v, t0, t1 in segs:
                        ins = stt(h[:, k, t0:t1], x[:, k, t0:t1], mod[l][:, which * KD + k, v:v + 1],
                                  PS[1][:, t0:t1])
                        if (k, t1) == (KD - 1, T):
                            give(ins)
                        else:
                            ins.then_inc(s["modded"], 1)

            BOTH = [(1, 0, CTX), (0, CTX, T)]
            V.memset(ones[:, :], 1.0).then_inc(consts_set, 1)
            V.memset(small[:, :], 0.0).then_inc(dve_step, 1)
            own[0] += 1
            dve.wait_ge(dve_step, own[0])
            V.memset(small[:, 0:1], EPS).then_inc(consts_set, 1)
            dve.wait_ge(loaded, 16 * 5)
            for l in range(DEPTH):
                lam = vec_at(l, "lams")
                for m in range(2):
                    step(V.tensor_tensor(am[:, 0:DH], lam[:, 2 * m * DH:2 * m * DH + DH],
                                         lam[:, 2 * m * DH + DH:2 * m * DH + 2 * DH], op=MUL))
                    ins = V.reduce_sum(small[:, 1 + 2 * l + m:2 + 2 * l + m], am[:, 0:DH], AX.X)
                    if (l, m) == (1, 1):
                        ins.then_inc(lam_sums, 1)
                    else:
                        step(ins)
            dve.wait_ge(silc_tanh, 1)
            step(stt(silc[:, 0:16], silc[:, 0:16], 1.0, silc[:, 16:32], ADD, MUL))
            V.tensor_scalar(silc[:, 0:16], silc[:, 0:16], 0.5, None, MUL).then_inc(silc_ready, 1)
            dve.wait_ge(lam_exps, 1)
            for l in range(DEPTH):
                lam_init = 0.8 - 0.6 * math.exp(-0.3 * l)
                step(V.tensor_tensor(small[:, 9 + l:10 + l], small[:, 6 + 2 * l:7 + 2 * l], small[:, 5 + 2 * l:6 + 2 * l], op=SUB))
                step(V.tensor_scalar(small[:, 9 + l:10 + l], small[:, 9 + l:10 + l], -lam_init, None, ADD))
                step(V.tensor_scalar(vec_at(l, "sub_g"), vec_at(l, "sub_g"), 1.0 - lam_init, None, MUL))
                step(V.tensor_scalar(vec_at(l, "conv_w"), vec_at(l, "conv_w"), 0.5, None, MUL))
                step(V.tensor_scalar(vec_at(l, "ln_b"), vec_at(l, "ln_b"), 0.5, None, MUL))
            step(V.tensor_copy(tok, rcon_at("token")))
            V.memset(zero, 0).then_inc(table_zero, 1)
            for u in range(4):
                ada_evac(("ada", 0, u))
            dve.wait_ge(x_loaded, 16)
            for l in range(DEPTH):
                s = S[l]
                q0 = 0 if l == 0 else CTX
                qt0, NQ = q0 // 128, T - q0
                nt = 4 - qt0
                SEGS = BOTH if l == 0 else BOTH[1:]
                seqs = slice(0 if l == 0 else 1, 2)
                scales(l, 0)
                recip(s, 0, 4, ("n1", l))
                norm_apply(l, s, ("n1b", l), BOTH, 0, 0)
                take(("lora", l, 1))
                give(V.tensor_copy(lora[:, 1, q0:T], PS[1][:, 0:NQ]))
                take(("lora", l, 3))
                give(V.tensor_copy(lora[64:96, 3, :], PS[1][0:32, :]))
                ada_after(("lora", l, 0))
                dve.wait_ge(s["pads_zero"], 1)
                for j in range(CT):
                    take(("gluA", l, j))
                    dve.wait_ge(empty["a"], A[("gluG", l, j)])
                    give(stt(up[:, j, seqs, PAD:PAD + 256], PT[:, j % 2, q0:T].rearrange("p (s u) -> p s u", u=256), 1.0,
                             PS[1][:, 0:NQ].rearrange("p (s u) -> p s u", u=256), ADD, MUL))
                    if j % 2 == 1:
                        ada_after(("glu", l, j // 2))
                last_glu = Dn[("gluA", l, CT - 1)]
                recip(s, 8, nt + 4, ("loraS", l))
                take(("loraQ", l))
                stt(lora[:, 0, q0:T], lora[:, 0, q0:T], vec_at(l, "q_g")[:, 0:1], PS[1][:, q0:T])
                give(stt(lora[:, 1, q0:T], lora[:, 1, q0:T], vec_at(l, "q_g")[:, 1:2], PS[1][:, q0:T]))
                take(("loraK", l))
                give(stt(lora[:, 2, :], lora[:, 2, :], vec_at(l, "kv_g"), PS[1][:, :]))
                kr, krt = lora[64:96, 3, CTX:T], PT[64:96, 0, 0:SEQ]
                swap = [(r + 16) % 32 for r in range(32)]
                dve.wait_ge(empty["d"], last_glu)
                V.stream_shuffle(krt, kr, swap).then_inc(dve_step, 1)
                own[0] += 1
                dve.wait_ge(dve_step, own[0])
                step(V.tensor_tensor(krt, krt, con_at("sin_a")[64:96, :], op=MUL))
                step(V.tensor_tensor(kr, kr, con_at("cos_a")[64:96, :], op=MUL))
                V.tensor_tensor(kr, kr, krt, op=ADD).then_inc(s["kr_ready"], 1)

                conv_at = [0]
                base = own[0]

                def conv(n):
                    for o in range(conv_at[0], min(conv_at[0] + n, CW * CT)):
                        tap, c = divmod(o, CT)
                        w_ = vec_at(l, "conv_w")[:, c * CW + tap:c * CW + tap + 1]
                        src = up[:, c, seqs, tap:tap + 256]
                        dst = cv[:, c, q0:T].rearrange("p (s u) -> p s u", u=256)
                        if tap == 0:
                            ins = V.tensor_scalar(dst, src, w_, vec_at(l, "conv_b")[:, c:c + 1], MUL, ADD)
                        else:
                            dve.wait_ge(dve_step, conv_done[o - CT])
                            ins = stt(dst, src, w_, dst, MUL, ADD)
                        own[0] += 1
                        conv_done[o] = own[0]
                        ins.then_inc(dve_step, 1)
                    conv_at[0] = min(conv_at[0] + n, CW * CT)

                conv_done = {}

                def swapped_sin(dst, src, nth, wait):
                    dve.wait_ge(s["rope_pool"], wait) if wait else dve.wait_ge(full["a"], A[("loraS", l)])
                    for o_, i_ in ((0, 1), (1, 0), (2, 3), (3, 2)):
                        ins = V.tensor_tensor(dst[32 * o_:32 * o_ + 32], src[32 * i_:32 * i_ + 32, :, CTX:T],
                                              con_at("sin_d")[32 * i_:32 * i_ + 32, :].unsqueeze(1).to_broadcast([32, HD, SEQ]),
                                              op=MUL)
                    ins.then_inc(s["rope_part"], 1)

                Pd = P[:, 0:2, :].rearrange("p a (b n) -> p (a b) n", b=2)
                Pq = P[64:96, :, :].rearrange("p a (b n) -> p (a b) n", b=2)
                few, many = (4, 16)
                conv(few)
                for i in range(1, HD, 2):
                    take(("dq", l, i))
                    give(V.tensor_copy(qd[:, i, q0:T], PS[1][:, 0:NQ]))
                    conv(many - 4)
                ada_after(("dq", l, 0))
                dve.wait_ge(empty["d"], Dn[("dq", l, HD - 1)])
                dve.wait_ge(empty["a"], A[("dq", l, HD - 2)])
                swapped_sin(Pd, qd, 1, 0)
                dve.wait_ge(y_zeroed, 16 * DEPTH)
                for i in range(1, HA, 2):
                    take(("uq", l, i))
                    give(V.tensor_copy(qa[0:96, i, q0:T], PS[1][0:96, 0:NQ]))
                for i in range(1, HA, 2):
                    take(("uk", l, i))
                    give(V.tensor_copy(ka[0:64, i, :], PS[1][0:64, :]))
                for t in range(1, 4, 2):
                    take(("uv", l, t))
                    give(V.tensor_copy(va[:, t, :], PS[1][:, :]))
                ada_after(("ukv", l, 0))
                dve.wait_ge(empty["a"], A[("uq", l, HA - 2)])
                dve.wait_ge(empty["d"], Dn[("uq", l, HA - 1)])
                dve.wait_ge(s["rope_pool"], 1)
                V.stream_shuffle(Pq, qa[64:96, :, CTX:T], swap).then_inc(s["rope_part"], 1)
                for i in range(1, HD, 2):
                    conv(many + 4)
                    take(("dk", l, i))
                    give(V.tensor_copy(kd[:, i, :], PS[1][:, :]))
                ada_after(("dk", l, 0))
                dve.wait_ge(empty["d"], Dn[("dk", l, HD - 1)])
                dve.wait_ge(empty["a"], A[("dk", l, HD - 2)])
                swapped_sin(Pd, kd, 3, 2)
                for t in range(1, 4, 2):
                    conv(many)
                    take(("dv", l, t))
                    give(V.tensor_copy(vd[:, t, :], PS[1][:, :]))
                ada_after(("dv", l, 0))
                conv(CW * CT)
                dve.wait_ge(dve_step, own[0])
                V.memset(small[:, 14:15], 0.0).then_inc(s["conv_v"], 1)
                take(("lnMb", l))
                for c in range(CT):
                    ins = V.tensor_tensor(cv[:, c, q0:T], cv[:, c, q0:T], PS[1][:, q0:T], op=SUB)
                give(ins)
                recip(s, 24, nt, ("lnV", l))
                take(("lnVb", l))
                for c in range(CT):
                    ins = stt(cv[:, c, q0:T], cv[:, c, q0:T], vec_at(l, "ln_g")[:, c:c + 1], PS[1][:, q0:T])
                    if c < CT - 1:
                        ins.then_inc(s["conv_scaled"], 1)
                    else:
                        give(ins)
                for c in range(CT):
                    dve.wait_ge(s["conv_tanh"], c + 1)
                    stt(cv[:, c, q0:T], P[:, c, q0:T], 1.0, cv[:, c, q0:T], ADD, MUL).then_inc(s["conv_out"], 1)
                AU, DU = attn_units(l)
                nA = len(AU)
                nlam = small[:, 9 + l:10 + l]

                def peak(g, banks, nk, scale, tiles):
                    c = 8 * (g % 8)
                    for m, b in enumerate(banks):
                        dve.wait_ge(s["scores"], tiles + m + 1)
                        ins = V.reduce_max(am[:, c + m:c + m + 1], PS[b][:, 0:nk], AX.X)
                    step(ins)
                    n = len(banks)
                    V.tensor_scalar(am[:, c + 2:c + 2 + n], am[:, c:c + n], -scale, None, MUL).then_inc(s["scores_max"], 1)

                def peak_a(u):
                    peak(u, [2 + u % 4], AU[u][2], SCALE_A, u)

                def peak_d(u):
                    peak(nA + u, [2 + 2 * (u % 2), 3 + 2 * (u % 2)], DU[u][2], SCALE_D, nA + 2 * u)

                def probs_a(u):
                    c, nk = 8 * (u % 8), AU[u][2]
                    dve.wait_ge(s["exp_ready"], u + 1)
                    step(V.reciprocal(am[:, c + 6:c + 7], am[:, c + 4:c + 5]))
                    V.tensor_scalar(P[:, u % 4, 0:nk], P[:, u % 4, 0:nk], am[:, c + 6:c + 7], None, MUL) \
                        .then_inc(s["probs_ready"], 1)

                def probs_d(u):
                    c, nk = 8 * ((nA + u) % 8), DU[u][2]
                    p0, p1 = P[:, 2 * (u % 2), 0:nk], P[:, 2 * (u % 2) + 1, 0:nk]
                    dve.wait_ge(s["exp_ready"], nA + 2 * u + 2)
                    step(V.reciprocal(am[:, c + 6:c + 8], am[:, c + 4:c + 6]))
                    step(V.tensor_scalar(p1, p1, am[:, c + 7:c + 8], nlam, MUL, MUL))
                    stt(p0, p0, am[:, c + 6:c + 7], p1, MUL, ADD).then_inc(s["probs_ready"], 1)

                def out_copy(g, out, ps):
                    dve.wait_ge(s["pv_full"], g + 1)
                    V.tensor_copy(out, ps).then_inc(s["attn_out"], 1)

                def out_a(u):
                    i, t, nk = AU[u]
                    r = 64 * (i % 2)
                    out_copy(u, oa[r:r + 64, i // 2, t * 128:t * 128 + 128], PS[7][r:r + 64, 0:128])

                def out_d(u):
                    i, t, nk = DU[u]
                    out_copy(nA + u, qd[:, i, t * 128:t * 128 + 128], PS[7][:, 0:128])

                peak_a(0)
                peak_a(1)
                for u in range(nA):
                    if u + 2 < nA:
                        peak_a(u + 2)
                    probs_a(u)
                    if u >= 1:
                        out_a(u - 1)
                peak_d(0)
                out_a(nA - 1)
                for u in range(len(DU)):
                    if u + 1 < len(DU):
                        peak_d(u + 1)
                    probs_d(u)
                    if u >= 1:
                        out_d(u - 1)
                out_d(len(DU) - 1)
                recip(s, 32, HD * nt, ("dn", l))
                for i in range(HD):
                    take(("dnb", l, i))
                    give(stt(qd[:, i, q0:T], qd[:, i, q0:T], vec_at(l, "sub_g"), PS[1][:, q0:T]))
                for c in range(KD):
                    for b in range(3):
                        n = 3 * c + b
                        take(("branch", l, c, b))
                        dve.wait_ge(empty["a"], A[("gate", l, c, b)])
                        if b == 1 and c:
                            dve.wait_ge(s["merge_part"], c)
                        if b == 2 and c:
                            dve.wait_ge(s["yt_ready"], c)
                        out = yt[:, c, q0:T] if b == 0 else P[:, b + 1, q0:T]
                        give(stt(out, P[:, n % 2, q0:T], 1.0, PS[1][:, 0:NQ], ADD, MUL))
                    ada_after(("merge", l, c))
                scales(l, 2)
                for c in range(1, KD, 2):
                    take(("out", l, c))
                    for v, t0, t1 in SEGS:
                        ins = stt(x[:, c, t0:t1], PS[1][:, t0 - q0:t1 - q0], mod[l][:, 2 * KD + c, v:v + 1],
                                  x[:, c, t0:t1], MUL, ADD)
                    give(ins)
                    if c % 4 == 3:
                        ada_after(("out", l, c // 4))
                scales(l, 1)
                recip(s, 48, nt, ("n2", l))
                norm_apply(l, s, ("n2b", l), SEGS, 1, q0)
                take(("router", l))
                give(V.tensor_tensor(lg[:, 0:nt, :], grid(PS[1][:, 0:36 * nt], nt),
                                     vec_at(l, "b_r").unsqueeze(1).to_broadcast([128, nt, NG + NE]), op=ADD))
                for t in range(nt):
                    take(("h2", l, qt0 + t, 1))
                    give(V.tensor_copy(stage[:, t, 512:1024], PS[1][:, :]))

                def over(c, n):
                    return c[:, 0:nt].unsqueeze(2).to_broadcast([128, nt, n])

                def row(r, n):
                    return r.unsqueeze(1).to_broadcast([128, nt, n])

                def first_max(values, n, desc, top, tmp, hot, best):
                    step(V.reduce_max(best[:, 0:nt], values, AX.X))
                    step(V.tensor_tensor(tmp, values, over(best, n), op=ALU.is_equal))
                    step(V.tensor_tensor(tmp, tmp, row(desc, n), op=MUL))
                    step(V.reduce_max(top[:, 0:nt], tmp, AX.X))
                    step(V.tensor_tensor(hot, tmp, over(top, n), op=ALU.is_equal))

                B = [b_[:, 0:nt, :] for b_ in big]
                glog = lg[:, 0:nt, 0:NG]
                g0, g1_, g2_ = (g_[:, 0:nt, :] for g_ in g4)
                first_max(glog, NG, rcon_at("desc4"), col[1], g1_, g2_, col[0])
                step(V.tensor_tensor(g0, glog, over(col[0], NG), op=SUB))
                step(V.tensor_scalar(g2_, g2_, -1.0, 3.0e38, ADD, MUL))
                for t in range(nt):
                    ins = V.tensor_tensor(B[0][:, t, :].rearrange("p (g e) -> p g e", g=NG),
                                          lg[:, t, NG:].rearrange("p (g e) -> p g e", g=NG),
                                          g4[2][:, t, :].unsqueeze(2).to_broadcast([128, NG, EG]), op=ADD)
                step(ins)
                first_max(B[0], NE, rcon_at("desc32"), col[1], B[1], B[2], col[2])
                step(V.scalar_tensor_tensor(B[0], B[2], -3.1e38, B[0], op0=MUL, op1=ADD))
                first_max(B[0], NE, rcon_at("desc32"), col[1], B[1], B[3], col[3])
                V.tensor_tensor(col[4][:, 0:nt], col[3][:, 0:nt], col[2][:, 0:nt], op=SUB).then_inc(s["gexp_in"], 1)
                V.tensor_tensor(B[4], B[2], B[3], op=ADD).then_inc(s["mask_ready"], 1)
                dve.wait_ge(s["gexp"], 1)
                step(V.reduce_sum(col[6][:, 0:nt], g1_, AX.X))
                step(stt(col[7][:, 0:nt], col[5][:, 0:nt], 1.0, col[6][:, 0:nt], ADD, MUL))
                step(V.reciprocal(col[7][:, 0:nt], col[7][:, 0:nt]))
                step(V.tensor_scalar(col[8][:, 0:nt], col[7][:, 0:nt], 0.5, None, MUL))
                step(V.tensor_tensor(col[9][:, 0:nt], col[8][:, 0:nt], col[5][:, 0:nt], op=MUL))
                C = NQ // 8
                half_up = 1.0 / (2 * C) - 0.5
                extra, cum, cum2, dvec = c32[0], c32[1], c32[2], c32[3]
                take(("rank", l))
                step(V.tensor_copy(B[5], grid(PS[1][:, 0:32 * nt], nt)))
                step(V.tensor_scalar(extra, PS[1][:, 128:160], 1.0 / C, half_up - 1.0 / C, MUL, ADD))
                step(V.tensor_scalar(extra, extra, ROUND, None, ADD))
                step(V.tensor_scalar(extra, extra, -ROUND, 0.0, ADD, ALU.max))
                give(V.tensor_copy(cum, extra))
                dve.wait_ge(empty["d"], Dn[("rank", l)])
                for sh in (1, 2, 4, 8, 16):
                    step(V.tensor_copy(cum2[:, 0:sh], cum[:, 0:sh]))
                    step(V.tensor_tensor(cum2[:, sh:NE], cum[:, sh:NE], cum[:, 0:NE - sh], op=ADD))
                    cum, cum2 = cum2, cum
                step(V.tensor_tensor(dvec, cum, extra, op=SUB))
                step(stt(dvec, dvec, float(NE - 1), rcon_at("expert"), ADD, SUB))
                step(V.tensor_scalar(B[6], B[5], 1.0 / C, half_up, MUL, ADD))
                step(V.tensor_scalar(B[6], B[6], ROUND, None, ADD))
                step(V.tensor_scalar(B[6], B[6], -ROUND, None, ADD))
                step(V.tensor_scalar(B[7], B[6], 1.0, None, ALU.is_ge))
                step(V.tensor_tensor(B[1], B[6], row(dvec, NE), op=ADD))
                step(V.tensor_tensor(B[1], B[1], B[7], op=MUL))
                step(V.tensor_tensor(B[1], B[1], row(rcon_at("expert"), NE), op=ADD))
                step(stt(B[1], B[5], float(NBLK), B[1], MUL, ADD))
                step(stt(B[1], B[6], float(-NBLK * C), B[1], MUL, ADD))
                for m in range(2):
                    step(V.tensor_tensor(B[7], B[1], B[2 + m], op=MUL))
                    step(V.reduce_sum(col[0][:, 0:nt], B[7], AX.X))
                    step(V.tensor_copy(sl[:, m, 0:nt], col[0][:, 0:nt]))
                step(V.tensor_tensor(cmp15, cum.unsqueeze(1).to_broadcast([128, OVER, NE]),
                                     rcon_at("nth").unsqueeze(2).to_broadcast([128, OVER, NE]), op=ALU.is_le))
                step(V.reduce_sum(ov15[:, 0:OVER], cmp15, AX.X))
                step(V.tensor_copy(ov15[:, OVER:OVER + 1], cum[:, NE - 1:NE]))
                V.tensor_copy(meta[l], ov15).then_inc(s["slots_ready"], 1)

                def hidden(j, i):
                    p = j % 2
                    dve.wait_ge(s["gtanh"], i * 4 + j + 1)
                    if not (isinstance(i, int) and 4 * i + j < 2):
                        dve.wait_ge(s["y_full"], i * 4 + j - 1)
                    stt(hid[:, p, 0:2 * C], gt[:, p, 0:2 * C], 1.0, PS[4 + p][:, 0:2 * C], ADD, MUL) \
                        .then_inc(hid_half, 1)
                    dve.wait_ge(hid_half, 32 * l + i * 4 + j + 1)
                    V.tensor_tensor(hid[:, p, 0:2 * C], hid[:, p, 0:2 * C], PS[4 + p][:, 2 * C:4 * C], op=MUL) \
                        .then_inc(s["hid_ready"], 1)

                def y_half(j, i):
                    p = j % 2
                    dve.wait_ge(s["y_full"], i * 4 + j + 1)
                    if not (isinstance(i, int) and 4 * i + j < 2):
                        dve.wait_ge(s[f"y_stored{p}"], i * 32 + 16 * (j // 2))
                    V.tensor_copy(yy[0:C, p, 512:1024], PS[7][0:C, :]).then_inc(s["y_dve"], 1)

                def group(i, first):
                    for j in range(4):
                        hidden(j, i)
                        if not (first and j == 0):
                            y_half((j - 1) % 4, i - (j == 0))

                group(0, True)
                with dve.Fori(1, NE // 4) as i:
                    group(i, False)
                y_half(3, NE // 4 - 1)
                nx = dve.value_load(meta[l][0:1, 15:16], min_val=0, max_val=OVER)
                with dve.If(nx > 0):
                    dve.wait_ge(s["y_stored0"], 16 * NE // 2)
                    with dve.Fori(0, OVER) as j:
                        with dve.If(nx > j):
                            dve.wait_ge(s["ov_act"], 3 * j + 2)
                            stt(hid[:, 0, 0:2 * C], gt[:, 0, 0:2 * C], 1.0, PS[4][:, 0:2 * C], ADD, MUL) \
                                .then_inc(s["ov_dve"], 1)
                            dve.wait_ge(s["ov_dve"], 3 * j + 1)
                            V.tensor_tensor(hid[:, 0, 0:2 * C], hid[:, 0, 0:2 * C], PS[4][:, 2 * C:4 * C], op=MUL) \
                                .then_inc(s["ov_dve"], 1)
                            dve.wait_ge(s["ov_pe"], 3 * j + 3)
                            V.tensor_copy(yy[0:C, 0, 512:1024], PS[7][0:C, :]).then_inc(s["ov_dve"], 1)
                for t in range(nt):
                    p = t % 2
                    dve.wait_ge(s[f"yg_ready{p}"], 32 * (t // 2) + 32)
                    step(V.tensor_scalar(xg[:, p, :], xg[:, p, :], col[8][:, t:t + 1], None, MUL))
                    stt(xg[:, p, :], yy[:, p, :], col[9][:, t:t + 1], xg[:, p, :], MUL, ADD).then_inc(s["yg_mixed"], 1)
                    v = 1 if qt0 + t < 2 else 0
                    for half in range(2):
                        take(("mix", l, qt0 + t, half))
                        for k in range(4):
                            xs = x[:, 4 * half + k, (qt0 + t) * 128:(qt0 + t) * 128 + 128]
                            ins = stt(xs, PS[1][:, k * 128:k * 128 + 128], ada[l][:, 5 * KD + 4 * half + k, v:v + 1],
                                      xs, MUL, ADD)
                        give(ins)
            s = S[1]
            recip(s, 52, 2, ("nf", 1))
            take(("nfb", 1))
            for k in range(KD):
                ins = stt(h[:, k, CTX:T], x[:, k, CTX:T], fing[:, k:k + 1], PS[1][:, CTX:T])
            ins.then_inc(out_ready, 1)

        @block.gpsimd
        def _(pool):
            A, Dn = number["a"], number["d"]
            own = [0]
            G = nc.gpsimd

            def step(ins):
                own[0] += 1
                ins.then_inc(pool_step, 1)
                pool.wait_ge(pool_step, own[0])

            pool.wait_ge(table_zero, 1)
            for l in range(DEPTH):
                pool.dma_start(td[l].rearrange("(r b) o -> r (b o)", b=NBLK), zero[0:CAP[l], :]).then_inc(zeroed, 16)
            for l in range(DEPTH):
                s = S[l]
                q0 = 0 if l == 0 else CTX
                qt0, NQ = q0 // 128, T - q0
                nt = 4 - qt0
                if l == 1:
                    pool.wait_ge(empty["d"], Dn[("mix", 0, 3, 1)])
                G.memset(arena[:, 16384:16384 + CT * 2 * UP], 0.0).then_inc(s["pads_zero"], 1)
                pool.wait_ge(s["pads_zero"], 1)
                if l == 0:
                    G.memset(arena[:, 0:D], 0.0).then_inc(pool_step, 1)
                    own[0] += 1
                    pool.wait_ge(pool_step, own[0])
                    pool.wait_ge(empty["d"], Dn[("lora", 0, 1)])
                    for ll in range(DEPTH):
                        pool.dma_start(yd[ll].rearrange("(r b) d -> r b d", b=NBLK)[:, NE:, :],
                                       arena[0:CAP[ll], 0:D].unsqueeze(1).to_broadcast([CAP[ll], NBLK - NE, D])) \
                            .then_inc(y_zeroed, 16)
                pool.wait_ge(s["kr_ready"], 1)
                G.tensor_copy(ka[64:96, :, :], lora[64:96, 3:4, :].to_broadcast([32, HA, T])).then_inc(s["kr_copied"], 1)

                pool.wait_ge(s["kr_copied"], 1)

                def rotate(part, rows, q, t, cos, sin, heads):
                    pool.wait_ge(s["rope_part"], part)
                    r = slice(*rows)
                    if sin is not None:
                        step(G.tensor_tensor(t, t, con_at(sin)[r, :].unsqueeze(1).to_broadcast([rows[1] - rows[0], heads, SEQ]), op=MUL))
                    step(G.tensor_tensor(q[r, :, CTX:T], q[r, :, CTX:T],
                                         con_at(cos)[r, :].unsqueeze(1).to_broadcast([rows[1] - rows[0], heads, SEQ]), op=MUL))
                    pool.wait_ge(pool_step, own[0])
                    G.tensor_tensor(q[r, :, CTX:T], q[r, :, CTX:T], t, op=ADD).then_inc(s["rope_pool"], 1)
                    pool.wait_ge(s["rope_pool"], part)

                Pd = P[:, 0:2, :].rearrange("p a (b n) -> p (a b) n", b=2)
                Pq = P[64:96, :, :].rearrange("p a (b n) -> p (a b) n", b=2)
                rotate(1, (0, 128), qd, Pd, "cos_d", None, HD)
                rotate(2, (64, 96), qa, Pq, "cos_a", "sin_a", HA)
                rotate(3, (0, 128), kd, Pd, "cos_d", None, HD)
                for c in range(KD):
                    pool.wait_ge(empty["d"], Dn[("branch", l, c, 1)])
                    G.tensor_tensor(yt[:, c, q0:T], yt[:, c, q0:T], P[:, 2, q0:T], op=ADD).then_inc(s["merge_part"], 1)
                    pool.wait_ge(s["merge_part"], c + 1)
                    pool.wait_ge(empty["d"], Dn[("branch", l, c, 2)])
                    G.tensor_tensor(yt[:, c, q0:T], yt[:, c, q0:T], P[:, 3, q0:T], op=ADD).then_inc(s["yt_ready"], 1)
                for c in range(0, KD, 2):
                    pool.wait_ge(empty["a"], A[("out", l, c)])
                    G.tensor_tensor(x[:, c, q0:T], x[:, c, q0:T], P[:, (c // 2) % 2, q0:T], op=ADD) \
                        .then_inc(s["out_part"], 1)
                C = NQ // 8
                pool.wait_ge(zeroed, 16 * DEPTH)
                pool.wait_ge(s["slots_ready"], 1)
                for t in range(nt):
                    for m in range(2):
                        pool.indirect_dma_start(out=td[l][:, :], out_offset=bass.IndirectOffsetOnAxis(ap=sl[:, m, t:t + 1], axis=0),
                                                in_=tok[:, t:t + 1], in_offset=None).then_inc(s["scattered"], 16)
                pool.wait_ge(s["scattered"], 16 * 2 * nt)
                pool.dma_start(idx[0:C, :], td[l].rearrange("(r b) o -> r (b o)", b=NBLK)[0:C, :]).then_inc(s["idx_loaded"], 16)
                pool.wait_ge(s["idx_loaded"], 16)
                pool.wait_ge(s["h2_stored"], 16 * nt)

                def gather(j, i):
                    p = j % 2
                    if not (isinstance(i, int) and 4 * i + j < 2):
                        pool.wait_ge(s["xgt_full"], i * 4 + j - 1)
                    G.tensor_copy(icol[0:C, p:p + 1], idx[0:C, bass.ds(i * 4 + j, 1)]).then_inc(s["icol_ready"], 1)
                    wait_apart(pool, s["icol_ready"], i * 4 + j + 1)
                    pool.indirect_dma_start(out=xg[0:C, p, :], out_offset=None, in_=h2d[l][:, :],
                                            in_offset=bass.IndirectOffsetOnAxis(ap=icol[0:C, p:p + 1], axis=0)) \
                        .then_inc(s[f"xg_ready{p}"], 16)

                for j in range(4):
                    gather(j, 0)
                with pool.Fori(1, NE // 4) as i:
                    for j in range(4):
                        gather(j, i)
                nx = pool.value_load(meta[l][0:1, 15:16], min_val=0, max_val=OVER)
                with pool.If(nx > 0):
                    pool.wait_ge(s["xgt_full"], NE)
                    with pool.Fori(0, OVER) as j:
                        with pool.If(nx > j):
                            G.tensor_copy(icol[0:C, 0:1], idx[0:C, bass.ds(NE + j, 1)]).then_inc(s["ov_icol"], 1)
                            wait_apart(pool, s["ov_icol"], j + 1)
                            pool.indirect_dma_start(out=xg[0:C, 0, :], out_offset=None, in_=h2d[l][:, :],
                                                    in_offset=bass.IndirectOffsetOnAxis(ap=icol[0:C, 0:1], axis=0)) \
                                .then_inc(s["ov_xg"], 16)
                            wait_apart(pool, s["ov_stored"], 16 * j + 16)
                for p in range(2):
                    pool.wait_ge(s[f"y_stored{p}"], 16 * NE // 2)
                for t in range(nt):
                    p = t % 2
                    if t >= 2:
                        pool.wait_ge(full["d"], Dn[("mix", l, qt0 + t - 2, 1)])
                    for buf, m in ((xg, 0), (yy, 1)):
                        pool.indirect_dma_start(out=buf[:, p, :], out_offset=None, in_=yd[l][:, :],
                                                in_offset=bass.IndirectOffsetOnAxis(ap=sl[:, m, t:t + 1], axis=0)) \
                            .then_inc(s[f"yg_ready{p}"], 16)

        @block.sync
        def _(sp):
            Dn = number["d"]
            sp.dma_start(silc[:, 16:32], a["cvec"]).then_inc(loaded, 16)
            sp.dma_start(vec, a["vecs"]).then_inc(loaded, 16)
            sp.dma_start(con[:, :], a["con"]).then_inc(loaded, 16)
            sp.dma_start(fing[:, :], a["final_g"]).then_inc(loaded, 16)
            sp.dma_start(rcon, a["rcon"]).then_inc(loaded, 16)

            def load(n):
                kind, l, i = units[n]
                slot, src = ring[:, n % NRING, :], a["out_w" if kind == "out" else kind][l, i]
                if n >= NRING:
                    b, e = unit_end[units[n - NRING]]
                    sp.wait_ge(full[b], e)
                sp.dma_start(slot[:, 0:src.shape[1]], src).then_inc(ring_ready[n % NRING], 16)

            def expert(l, j, i, e):
                s = S[l]
                if not (isinstance(i, int) and i == 0):
                    sp.wait_ge(s["gu_full"], i * 4 + j - 3)
                for m, n_ in enumerate(("w_gate", "w_up")):
                    sp.dma_start(gu[j][:, 2048 * m:2048 * m + 2048].unsqueeze(1),
                                 a[n_][l][bass.ds(e, 1)].rearrange("e p n -> p e n")).then_inc(s[f"gu_ready{j}"], 16)
                if not (isinstance(i, int) and i == 0):
                    sp.wait_ge(s["y_full"], i * 4 + j - 3)
                sp.dma_start(wd[:, j:j + 1, :], a["w_down"][l][bass.ds(e, 1)].rearrange("e p n -> p e n")) \
                    .then_inc(s[f"wd_ready{j}"], 16)

            n = 0
            for l in range(DEPTH):
                s = S[l]
                while n < len(units) and (l == 1 or n < first_of_layer1):
                    load(n)
                    n += 1
                    if n == NRING and l == 0:
                        sp.dma_start(x, a["x"]).then_inc(x_loaded, 16)
                        sp.dma_start(wr, a["router"][0]).then_inc(router_loaded, 16)
                b, e = unit_end[("out", l, 1)]
                sp.wait_ge(full[b], e)
                for j in range(4):
                    expert(l, j, 0, j)
                if l == 0:
                    sp.wait_ge(full["d"], Dn[("router", 0)])
                    sp.dma_start(wr, a["router"][1]).then_inc(router_loaded, 16)
                with sp.Fori(1, NE // 4) as i:
                    for j in range(4):
                        expert(l, j, i, i * 4 + j)
                sp.wait_ge(s["slots_ready"], 1)
                nx = sp.value_load(meta[l][0:1, 15:16], min_val=0, max_val=OVER)
                with sp.If(nx > 0):
                    sp.wait_ge(s["gu_full"], NE)
                    sp.wait_ge(s["y_full"], NE)
                    with sp.Fori(0, OVER) as j:
                        with sp.If(nx > j):
                            e = sp.value_load(meta[l][0:1, bass.ds(j, 1)], min_val=0, max_val=NE - 1)
                            for m, n_ in enumerate(("w_gate", "w_up")):
                                sp.dma_start(gu[3][:, 2048 * m:2048 * m + 2048].unsqueeze(1),
                                             a[n_][l][bass.ds(e, 1)].rearrange("e p n -> p e n")).then_inc(s["ov_w"], 16)
                            sp.dma_start(wd[:, 3:4, :], a["w_down"][l][bass.ds(e, 1)].rearrange("e p n -> p e n")) \
                                .then_inc(s["ov_w"], 16)
                            wait_apart(sp, s["ov_stored"], 16 * j + 16)
                sp.wait_ge(s["gu_full"], NE)
            sp.wait_ge(out_ready, 1)
            sp.dma_start(a["out"].rearrange("(k p) t -> p k t", p=128), h[:, :, CTX:T]).then_inc(out_stored, 16)
            sp.wait_ge(out_stored, 16)


def tables():
    con = np.zeros((128, NC), np.float32)
    con[:, 0:128] = np.eye(128)
    tok = np.arange(SEQ)
    row, colm = (tok // GRID_W).astype(np.float32), (tok % GRID_W).astype(np.float32)
    for dim, c, s_, rows in ((2 * DH // 2, "cos_d", "sin_d", None), (ROPE, "cos_a", "sin_a", 64)):
        n = dim // 4
        inv = (np.float32(ROPE_BASE) ** (-np.arange(n, dtype=np.float32) / np.float32(n))).astype(np.float32)
        ang = np.concatenate([row[:, None] * inv, colm[:, None] * inv], -1).astype(np.float32)
        cos, sin = np.cos(ang).T, np.sin(ang).T
        if rows is None:
            con[:, CON[c][0]:CON[c][1]] = np.concatenate([cos] * 4)
            con[:, CON[s_][0]:CON[s_][1]] = np.concatenate([sin, -sin] * 2)
        else:
            con[rows:rows + 32, CON[c][0]:CON[c][1]] = np.concatenate([cos] * 2)
            con[rows:rows + 32, CON[s_][0]:CON[s_][1]] = np.concatenate([-sin, sin])
    r = np.zeros((128, NRC), np.float32)
    r[:, 0:128] = np.triu(np.ones((128, 128)), 1)
    for n_, v in (("desc4", np.arange(NG, 0, -1)), ("desc32", np.arange(NE, 0, -1)), ("expert", np.arange(NE)),
                  ("nth", np.arange(OVER))):
        r[:, RCON[n_][0]:RCON[n_][1]] = v
    r[:, RCON["token"][0]:RCON["token"][1]] = np.arange(128)[:, None] + 128 * np.arange(4)
    return con, r


def kernel(x, c, ctx, c_ctx, w_ada, b_ada, norm1_g, w_in, q_norm_g, w_uq, kv_norm_g, w_ukv, conv_w, conv_b,
           conv_ln_g, conv_ln_b, lam_q1, lam_k1, lam_q2, lam_k2, diff_subln_g, w_o_mla, w_o_conv, w_o_diff, w_out,
           norm2_g, w_rg, b_rg, w_re, b_re, w_gate, w_up, w_down, final_g):
    import concourse.bacc as bacc
    from concourse.bass_utils import run_bass_kernel_spmd as run

    L = DEPTH
    A = np.asarray

    def rows(w, k):
        w = A(w)
        return w.reshape(L, k, 128, w.shape[-1]).transpose(0, 2, 1, 3)

    def flat(w, lead):
        w = np.ascontiguousarray(w)
        return w.reshape(w.shape[:lead] + (-1,))

    def part(v):
        v = A(v)
        return v.reshape(L, -1, 128).transpose(0, 2, 1)

    def alike(v):
        v = A(v)
        return np.broadcast_to(v[:, None, :], (L, 128, v.shape[-1]))

    win = rows(w_in, KD)
    o_glu, o_q = LW, LW + 2 * CC
    o_k, o_v, o_g = o_q + HD * 2 * DH, o_q + 2 * HD * 2 * DH, o_q + 3 * HD * 2 * DH
    glu = win[..., o_glu:o_q].reshape(L, 128, KD, 2, 2, 2, 128)
    gates = win[..., o_g:].reshape(L, 128, KD, 3, KD, 128)
    wo = np.concatenate([rows(w, 4) for w in (w_o_mla, w_o_conv, w_o_diff)], 2).reshape(L, 128, 12, KD, 128)
    con, rcon = tables()
    vecs = np.concatenate([part(norm1_g), part(norm2_g), part(b_ada), part(q_norm_g), part(kv_norm_g),
                           A(conv_w).reshape(L, CW, CT, 128).transpose(0, 3, 2, 1).reshape(L, 128, CT * CW),
                           part(conv_b), part(conv_ln_g), part(conv_ln_b), part(diff_subln_g),
                           alike(lam_q1), alike(lam_k1), alike(lam_q2), alike(lam_k2), alike(b_rg), alike(b_re)], 2)
    arrays = {
        "cvec": np.stack([A(c)[0], A(c_ctx)], 1).reshape(KD, 128, 2).transpose(1, 0, 2).reshape(128, 2 * KD),
        "vecs": vecs.transpose(1, 0, 2),
        "con": con, "rcon": rcon,
        "final_g": A(final_g).reshape(KD, 128).T,
        "x": np.concatenate([A(ctx)[0], A(x)[0]], 0).T.reshape(KD, 128, T).transpose(1, 0, 2),
        "router": np.concatenate([rows(w_rg, KD), rows(w_re, KD)], 3),
        "ada": flat(rows(w_ada, KD).reshape(L, 128, KD, NADA, 512).transpose(0, 3, 1, 2, 4), 3),
        "lora": flat(win[:, None, :, :, 0:LW], 3),
        "glu": flat(glu.transpose(0, 4, 1, 2, 5, 3, 6), 3),
        "dq": flat(win[:, None, :, :, o_q:o_k], 3),
        "dk": flat(win[:, None, :, :, o_k:o_v], 3),
        "dv": flat(win[:, None, :, :, o_v:o_g], 3),
        "ukv": np.concatenate([flat(rows(w_uq, 2), 2), A(w_ukv)], 2)[:, None],
        "merge": np.concatenate([flat(gates.transpose(0, 4, 1, 2, 3, 5), 3), flat(wo.transpose(0, 3, 1, 2, 4), 3)], 3),
        "out_w": flat(rows(w_out, KD).reshape(L, 128, KD, 2, 512).transpose(0, 3, 1, 2, 4), 3),
        "w_gate": A(w_gate).reshape(L, NE, KD, 128, FF).transpose(0, 1, 3, 2, 4).reshape(L, NE, 128, KD * FF),
        "w_up": A(w_up).reshape(L, NE, KD, 128, FF).transpose(0, 1, 3, 2, 4).reshape(L, NE, 128, KD * FF),
        "w_down": A(w_down).reshape(L, NE, 2, 128, D).transpose(0, 1, 3, 2, 4).reshape(L, NE, 128, 2 * D),
    }
    nc = bacc.Bacc("TRN2", target_bir_lowering=False, num_devices=1)
    aps, given = {}, {}
    for name, v in arrays.items():
        v = np.ascontiguousarray(v)
        given[f"{name}_in"] = v
        aps[name] = nc.dram_tensor(f"{name}_in", v.shape, mybir.dt.float32, kind="ExternalInput").ap()
    out = nc.dram_tensor("result", (D, SEQ), mybir.dt.float32, kind="ExternalOutput").ap()
    build(nc, dict(aps, out=out))
    r = run(nc, [given], core_ids=[0])
    return np.ascontiguousarray(r.results[0]["result"].T).reshape(1, SEQ, D)
```

```python
import math
from contextlib import ExitStack

import numpy as np
import concourse.bass as bass
from concourse import mybir

D = 1024
KD = D // 128
SEQ, CTX = 256, 256
T = CTX + SEQ
DEPTH = 2
GRID_W = 64
ROPE_BASE = 10000.0
EPS = 1e-6
HA, NOPE, ROPE, VA = 8, 64, 32, 64
QL, KVL = 256, 128
CC, CW = 512, 31
HD, DH = 4, 64
NG, EG, FF = 4, 8, 256
NE = NG * EG
CT = CC // 128
PAD = CW // 2
UP = 256 + 2 * PAD
LW = QL + KVL + ROPE
SLOT = 4608
NRING = 3
NADA = 12
OVER = 15
NBLK = 48
SCALE_A = 1.0 / math.sqrt(NOPE + ROPE)
SCALE_D = 1.0 / math.sqrt(DH)
ROUND = 12582912.0

VEC = {}
_at = 0
for _n, _w in (("norm1_g", KD), ("norm2_g", KD), ("b_ada", 48), ("q_g", 2), ("kv_g", 1), ("conv_w", CT * CW),
               ("conv_b", CT), ("ln_g", CT), ("ln_b", CT), ("sub_g", 1), ("lams", 4 * DH), ("b_r", NG + NE)):
    VEC[_n] = (_at, _at + _w)
    _at += _w
NV = _at

CON = {}
_at = 0
for _n, _w in (("ident", 128), ("pick", 2), ("cos_d", SEQ), ("sin_d", SEQ), ("cos_a", SEQ), ("sin_a", SEQ)):
    CON[_n] = (_at, _at + _w)
    _at += _w
NC = _at
RCON = {}
_at = 0
for _n, _w in (("tri", 128), ("desc4", NG), ("desc32", NE), ("expert", NE), ("nth", OVER), ("token", 4)):
    RCON[_n] = (_at, _at + _w)
    _at += _w
NRC = _at


def build(nc, a):
    f32, i32 = mybir.dt.float32, mybir.dt.int32
    ALU, ACT, AX = mybir.AluOpType, mybir.ActivationFunctionType, mybir.AxisListType
    MUL, ADD, SUB = ALU.mult, ALU.add, ALU.subtract
    ctx = ExitStack()

    def sb(name, shape, dt=f32):
        return ctx.enter_context(nc.sbuf_tensor(name, shape, dt))

    def sem(name):
        return ctx.enter_context(nc.semaphore(name))

    def grid(ap, n):
        return ap.rearrange("p (n m) -> p n m", n=n)

    with ctx:
        x = grid(sb("x", [128, KD * T])[:, :], KD)
        h = grid(sb("h", [128, KD * T])[:, :], KD)
        arena = sb("arena", [128, 20720])
        ring = grid(sb("ring", [128, NRING * SLOT])[:, :], NRING)
        qa = grid(arena[:, 0:4096], HA)
        oa = grid(arena[:, 0:4096], HA)[:, 0:8:2, :]
        va = grid(arena[:, 4096:6144], 4)
        qd = grid(arena[:, 6144:8192], HD)
        kd = grid(arena[:, 8192:10240], HD)
        vd = grid(arena[:, 10240:12288], 4)
        ka = grid(arena[:, 12288:16384], HA)
        yt = grid(arena[:, 12288:16384], KD)
        up = arena[:, 16384:16384 + CT * 2 * UP].rearrange("p (c s u) -> p c s u", c=CT, s=2)
        cv = grid(arena[:, 18672:20720], CT)
        lora = grid(sb("lora", [128, 4 * T])[:, :], 4)
        P = grid(sb("P", [128, 4 * 512])[:, :], 4)
        PT = grid(sb("PT", [128, 2 * 512])[:, :], 2)
        con = sb("con", [128, NC])
        vec = grid(sb("vec", [128, 2 * NV])[:, :], 2)
        ones = sb("ones", [128, 128])
        fing = sb("fing", [128, KD])
        silc = sb("silc", [128, 2 * KD * 2])
        silz = sb("silz", [128, KD * 32])[:, :]
        ada = [grid(sb(f"ada{l}", [128, 96])[:, :], 48) for l in range(2)]
        mod = [grid(sb(f"mod{l}", [128, 3 * KD * 2])[:, :], 3 * KD) for l in range(2)]
        st = sb("st", [128, 64])
        am = sb("am", [128, 96])
        small = sb("small", [128, 16])
        wr = grid(sb("wr", [128, KD * (NG + NE)])[:, :], KD)
        wd = grid(arena[:, 0:8192], 4)
        gu = [ring[:, 0, 0:4096], ring[:, 1, 0:4096], ring[:, 2, 0:4096], arena[:, 8192:12288]]
        m0 = 12288
        xg = grid(arena[:, m0:m0 + 2048], 2)
        yy = grid(arena[:, m0 + 2048:m0 + 4096], 2)
        stage = grid(arena[:, m0:m0 + 4096], 4)
        xgt = grid(arena[:, m0 + 4096:m0 + 5120], 2)
        gt = grid(arena[:, m0 + 5120:m0 + 5632], 2)
        hid = grid(arena[:, m0 + 5632:m0 + 6144], 2)
        hidt = grid(arena[:, m0 + 6144:m0 + 6400], 2)
        rt = sb("routing", [128, 1824])[:, :]
        rat = [0]

        def rtile(n, dt=f32):
            rat[0] += n
            assert rat[0] <= 1824, rat[0]
            t = rt[:, rat[0] - n:rat[0]]
            return t if dt == f32 else t.bitcast(dt)

        rcon = rtile(NRC)
        lg = grid(rtile(4 * 36), 4)
        g4 = [grid(rtile(16), 4) for _ in range(3)]
        bigs = rtile(8 * 128)
        big = [grid(bigs[:, 128 * n_:128 * n_ + 128], 4) for n_ in range(8)]
        col = [rtile(4) for _ in range(10)]
        c32 = [rtile(32) for _ in range(6)]
        cmp15 = grid(bigs[:, 0:OVER * NE], OVER)
        ov15 = rtile(16)
        icol = rtile(4, i32)
        sl = grid(rtile(8, i32), 2)
        tok = rtile(4, i32)
        meta = [rtile(16, i32) for _ in range(2)]
        idx = rtile(NBLK, i32)
        zero = rtile(NBLK, i32)

        PS = [ctx.enter_context(nc.psum_tensor(f"bank{i}", [128, 512], f32)) for i in range(8)]
        BANK = {"a": PS[0], "d": PS[1]}

        CAP = [T // 8, SEQ // 8]
        h2d = [nc.dram_tensor(f"h2_{l}", [8 * CAP[l], D], f32).ap() for l in range(2)]
        yd = [nc.dram_tensor(f"y_{l}", [CAP[l] * NBLK, D], f32).ap() for l in range(2)]
        td = [nc.dram_tensor(f"tok_{l}", [CAP[l] * NBLK, 1], i32).ap() for l in range(2)]

        full = {"a": sem("act_tile_full"), "d": sem("dve_tile_full")}
        empty = {"a": sem("act_tile_empty"), "d": sem("dve_tile_empty")}
        number = {"a": {}, "d": {}}
        ring_ready = [sem(f"ring_ready{s}") for s in range(NRING)]
        unit_end = {}
        loaded = sem("inputs_loaded")
        x_loaded, router_loaded, table_zero = sem("x_loaded"), sem("router_loaded"), sem("table_zero")
        hid_half, zeroed = sem("hid_half"), sem("zeroed")
        y_zeroed = sem("y_zeroed")
        passed = sem("waits_passed")
        lam_sums, lam_exps = sem("lam_sums"), sem("lam_exps")
        consts_set = sem("consts_set")
        silc_tanh, silc_ready = sem("silc_tanh"), sem("silc_ready")
        dve_step, pool_step = sem("dve_step"), sem("pool_step")
        out_ready, out_stored = sem("out_ready"), sem("out_stored")
        NAMES = ["sq_ready", "stat_ready", "recip_ready", "modded", "shifted",
                 "conv_v", "conv_sq", "conv_scaled", "conv_act", "conv_out",
                 "rope_part", "rope_pool", "kr_ready", "pool_set", "scores", "scores_max", "exp_ready",
                 "probs_ready", "pt_full", "pt_ready", "pv_full", "attn_out", "merge_part", "yt_ready", "g1_ready", "out_part",
                 "h2_stored", "gexp_in", "gexp", "mask_ready", "slots_ready", "tokens_moved", "icol_ready",
                 "xg_ready0", "xg_ready1", "xgt_full", "xgt_ready", "gu_ready0", "gu_ready1", "gu_ready2", "gu_ready3",
                 "wd_ready0", "wd_ready1", "wd_ready2", "wd_ready3", "gu_full", "gtanh", "hid_ready", "ht_full", "hidt_ready", "ssq",
                 "y_full", "y_act", "y_stored0", "y_stored1", "yg_ready0", "yg_ready1", "yg_mixed",
                 "ov_w", "ov_icol", "ov_xg", "ov_pe", "ov_act", "ov_dve", "ov_stored"]
        S = [{n: sem(f"{n}_{l}") for n in NAMES} for l in range(DEPTH)]

        def sqt(k):
            return P[:, 3, :] if k == 0 else lora[:, k % 4, :]

        def dprob(u):
            return (P[:, 0:2, :], P[:, 2:4, :], lora[:, 0:2, :])[u % 3]

        def attn_units(l):
            tiles = range(0 if l == 0 else 2, 4)
            seen = [CTX if t < CTX // 128 else T for t in range(4)]
            return ([(i, t, seen[t]) for i in range(HA) for t in tiles],
                    [(i, t, seen[t]) for i in range(HD) for t in tiles])

        def wait_apart(eng, sm, value):
            eng.wait_ge(sm, value)
            eng.sem_inc(passed, 1)

        def con_at(n):
            return con[:, CON[n][0]:CON[n][1]]

        def vec_at(l, n):
            return vec[:, l, VEC[n][0]:VEC[n][1]]

        def rcon_at(n):
            return rcon[:, RCON[n][0]:RCON[n][1]]

        ident = con_at("ident")

        units = [("ada", 0, u) for u in range(4)]
        more = [("ada", 0, u) for u in range(4, NADA)] + [("ada", 1, u) for u in range(NADA)]
        for l in range(DEPTH):
            for kind, n in (("lora", 1), ("glu", 2), ("dq", 1), ("ukv", 1), ("dk", 1), ("dv", 1), ("merge", KD), ("out", 2)):
                for i in range(n):
                    units.append((kind, l, i))
                    units += more[:1]
                    del more[:1]
        assert not more
        unit_no = {u: i for i, u in enumerate(units)}
        first_of_layer1 = unit_no[("lora", 1, 0)]

        def ada_behind(key):
            n = 0 if key is None else unit_no[key] + 1
            out_ = []
            while n < len(units) and units[n][0] == "ada":
                out_.append(n)
                n += 1
            return out_

        def ada_tmp(n):
            before = [k_[0] for k_ in units[:n] if k_[0] != "ada"]
            return ka[:, n % 4, :] if not before or before[-1] in ("lora", "glu") else PT[:, 1, :]

        block = ctx.enter_context(nc.Block())

        @block.tensor
        def _(pe):
            made = {}

            def begin(b, name):
                n = len(number[b]) + 1
                made["a"], made["d"] = int(b == "a"), int(b == "d")
                assert (name not in number[b])
                number[b][name] = n
                if n > 1:
                    pe.wait_ge(empty[b], n - 1)
                return BANK[b]

            def end(b, ins):
                ins.then_inc(full[b], 1)

            def unit(key):
                n = unit_no[key]
                pe.wait_ge(ring_ready[n % NRING], 16 * (n // NRING + 1))
                return ring[:, n % NRING, :]

            def mm(out, w, rhs, start, stop):
                return nc.tensor.matmul(out, w, rhs, start=start, stop=stop)

            def ada_units(after):
                for n in ada_behind(after):
                    ada_unit(units[n])

            def ada_unit(key):
                _, la, u = key
                w = grid(unit(key)[:, 0:4096], KD)
                ps = begin("d", ("ada", la, u))
                for k in range(KD):
                    g = 32 * (k % 4)
                    last = mm(ps[g:g + 32, :], silz[:, 32 * k:32 * k + 32], w[:, k, :], k < 4, k >= 4)
                end("d", last)
                used(key)

            def ada_finish(key):
                for n in ada_behind(key):
                    _, la, u = units[n]
                    ps = begin("d", ("adaT", la, u))
                    pe.wait_ge(empty["d"], number["d"][("ada", la, u)])
                    for m in range(4):
                        last = mm(ps[:, 2 * m:2 * m + 2], ada_tmp(n)[:, 128 * m:128 * m + 128],
                                  con_at("pick")[:, 0:2], True, True)
                    end("d", last)

            def used(key):
                b = max("ad", key=lambda n_: made[n_])
                unit_end[key] = (b, len(number[b]))

            def column_tile(b, name, w, q0, cols=128, kk=KD, src=None):
                ps = begin(b, name)
                for k in range(kk):
                    last = mm(ps[0:cols, 0:T - q0], w(k), src[:, k, q0:T], k == 0, k == kk - 1)
                end(b, last)

            def row_stats(name, parts):
                ps = begin("a", name)
                for c, (src, t) in enumerate(parts):
                    for j, s_ in enumerate(src):
                        last = mm(ps[:, c:c + 1], s_[:, t * 128:t * 128 + 128], ones[:, 0:1],
                                  j == 0, j == len(src) - 1)
                end("a", last)

            def spread(name, cols, q0=0):
                ps = begin("d", name)
                for t, c in cols:
                    last = mm(ps[:, t * 128:t * 128 + 128], st[:, c:c + 1].to_broadcast([128, 128]), ident, True, True)
                end("d", last)

            def norm_stats(l, which, t0, seen):
                pe.wait_ge(S[l]["ssq"], seen)
                row_stats((which, l), [([P[:, 3]], t) for t in range(t0, 4)])

            pe.wait_ge(loaded, 16 * 5)
            pe.wait_ge(consts_set, 2)
            pe.wait_ge(silc_ready, 1)
            for n in ada_behind(None):
                ada_unit(units[n])
            ada_finish(None)

            for l in range(DEPTH):
                s = S[l]
                q0 = 0 if l == 0 else CTX
                qt0 = q0 // 128
                norm_stats(l, "n1", 0, KD - 1)
                pe.wait_ge(s["recip_ready"], 1)
                spread(("n1b", l), [(t, t) for t in range(4)])
                pe.wait_ge(s["shifted"], 2 * KD)
                w = grid(unit(("lora", l, 0))[:, 0:KD * LW], KD)
                for i, (b, c0, cols, qq) in enumerate((("a", 0, 128, q0), ("d", 128, 128, q0),
                                                      ("a", 256, 128, 0), ("d", 384, 32, 0))):
                    column_tile(b, ("lora", l, i), lambda k: w[:, k, c0:c0 + cols], qq, cols, KD, h)
                used(("lora", l, 0))
                ada_units(("lora", l, 0))
                for j in range(2):
                    w = unit(("glu", l, j))[:, 0:4096].rearrange("p (k n m) -> p k n m", k=KD, n=4)
                    for i in range(2):
                        column_tile("a", ("gluG", l, 2 * j + i), lambda k: w[:, k, 2 * i + 1, :], q0, 128, KD, h)
                        if i == 0:
                            ada_finish(("glu", l, 0) if j else ("lora", l, 0))
                        column_tile("d", ("gluA", l, 2 * j + i), lambda k: w[:, k, 2 * i, :], q0, 128, KD, h)
                    used(("glu", l, j))
                    ada_units(("glu", l, j))
                    if j == 0:
                        pe.wait_ge(s["stat_ready"], 1)
                        row_stats(("loraS", l), [([P[:, 0], P[:, 1]], t) for t in range(qt0, 4)]
                                  + [([P[:, 2]], t) for t in range(4)])
                pe.wait_ge(s["recip_ready"], 2)
                spread(("loraQ", l), [(t, 8 + t - qt0) for t in range(qt0, 4)])
                spread(("loraK", l), [(t, 8 + 4 - qt0 + t) for t in range(4)])
                w = grid(unit(("dq", l, 0))[:, 0:4096], KD)
                for i in range(HD):
                    column_tile("ad"[i % 2], ("dq", l, i), lambda k: w[:, k, 128 * i:128 * i + 128], q0, 128, KD, h)
                    if i == 0:
                        ada_finish(("glu", l, 1))
                used(("dq", l, 0))
                ada_units(("dq", l, 0))
                pe.wait_ge(empty["d"], number["d"][("loraK", l)])
                w = unit(("ukv", l, 0))
                wq, wkv = grid(w[:, 0:1536], 2), w[:, 1536:2560]
                for i in range(HA):
                    column_tile("ad"[i % 2], ("uq", l, i), lambda k: wq[:, k, 96 * i:96 * i + 96], q0, 96, 2, lora)
                    if i == 0:
                        ada_finish(("dq", l, 0))
                for i in range(HA):
                    column_tile("ad"[i % 2], ("uk", l, i), lambda k: wkv[:, 128 * i:128 * i + 64], 0, 64, 1, lora[:, 2:3])
                for t in range(4):
                    b = "ad"[t % 2]
                    ps = begin(b, ("uv", l, t))
                    end(b, mm(ps[:, :], lora[:, 2, t * 128:t * 128 + 128],
                              wkv.rearrange("p (h n) -> p h n", h=HA)[:, :, NOPE:], True, True))
                used(("ukv", l, 0))
                ada_units(("ukv", l, 0))
                w = grid(unit(("dk", l, 0))[:, 0:4096], KD)
                for i in range(HD):
                    column_tile("ad"[i % 2], ("dk", l, i), lambda k: w[:, k, 128 * i:128 * i + 128], 0, 128, KD, h)
                    if i == 0:
                        ada_finish(("ukv", l, 0))
                used(("dk", l, 0))
                ada_units(("dk", l, 0))
                w = grid(unit(("dv", l, 0))[:, 0:4096], KD)
                for t in range(4):
                    b = "ad"[t % 2]
                    ps = begin(b, ("dv", l, t))
                    for k in range(KD):
                        last = mm(ps[:, :], h[:, k, t * 128:t * 128 + 128], w[:, k, :], k == 0, k == KD - 1)
                    end(b, last)
                    if t == 0:
                        ada_finish(("dk", l, 0))
                used(("dv", l, 0))
                ada_units(("dv", l, 0))
                ada_finish(("dv", l, 0))
                def conv_norm(u):
                    if u == 2:
                        pe.wait_ge(s["conv_v"], 1)
                        row_stats(("lnM", l), [([cv[:, c] for c in range(CT)], t) for t in range(qt0, 4)])
                    elif u == 5:
                        pe.wait_ge(empty["a"], number["a"][("lnM", l)])
                        spread(("lnMb", l), [(t, 16 + t - qt0) for t in range(qt0, 4)])
                    elif u == 9:
                        pe.wait_ge(s["conv_sq"], CT)
                        row_stats(("lnV", l), [([lora[:, c] for c in range(CT)], t) for t in range(qt0, 4)])
                    elif u == 12:
                        pe.wait_ge(s["recip_ready"], 3)
                        spread(("lnVb", l), [(t, 24 + t - qt0) for t in range(qt0, 4)])

                AU, DU = attn_units(l)
                n_all = len(AU) + len(DU)
                for b in "ad":
                    pe.wait_ge(empty[b], len(number[b]))
                pe.wait_ge(s["rope_pool"], 3)
                pe.wait_ge(s["pool_set"], 2)

                def scores_a(u):
                    i, t, nk = AU[u]
                    if u >= 4:
                        pe.wait_ge(s["exp_ready"], u - 3)
                    mm(PS[2 + u % 4][:, 0:nk], qa[0:96, i, t * 128:t * 128 + 128], ka[0:96, i, 0:nk], True, True) \
                        .then_inc(s["scores"], 1)

                def scores_d(u):
                    i, t, nk = DU[u]
                    g = len(AU) + 2 * u
                    pe.wait_ge(s["exp_ready"], len(AU) if u < 3 else g - 4)
                    for m in range(2):
                        mm(PS[2 * (u % 3) + m][:, 0:nk], qd[64 * m:64 * m + 64, i, t * 128:t * 128 + 128],
                           kd[64 * m:64 * m + 64, i, 0:nk], True, True).then_inc(s["scores"], 1)

                def turn(g, src, nk):
                    pe.wait_ge(s["probs_ready"], g + 1)
                    if g >= 1:
                        pe.wait_ge(s["pt_ready"], g)
                    for kt in range(nk // 128):
                        last = nc.tensor.transpose(PS[6][:, kt * 128:kt * 128 + 128],
                                                   src[:, kt * 128:kt * 128 + 128], ident)
                    last.then_inc(s["pt_full"], 1)

                def values(g, lhs, out, nk):
                    pe.wait_ge(s["pt_ready"], g + 1)
                    if g >= 1:
                        pe.wait_ge(s["attn_out"], g)
                    for kt in range(nk // 128):
                        last = mm(out, lhs(kt), PT[:, g % 2, kt * 128:kt * 128 + 128], kt == 0, kt == nk // 128 - 1)
                    last.then_inc(s["pv_full"], 1)

                def values_a(u):
                    i, t, nk = AU[u]
                    r = 64 * (i % 2)
                    values(u, lambda kt: va[:, kt, 64 * i:64 * i + 64], PS[7][r:r + 64, 0:128], nk)

                def values_d(u):
                    i, t, nk = DU[u]
                    values(len(AU) + u, lambda kt: vd[:, kt, 128 * i:128 * i + 128], PS[7][:, 0:128], nk)

                scores_a(0)
                scores_a(1)
                for u in range(len(AU)):
                    turn(u, P[:, u % 4], AU[u][2])
                    if u + 2 < len(AU):
                        scores_a(u + 2)
                    elif u + 2 == len(AU):
                        for b in "ad":
                            pe.wait_ge(empty[b], len(number[b]))
                    if u >= 1:
                        values_a(u - 1)
                    conv_norm(u)
                pe.wait_ge(s["conv_out"], CT)
                scores_d(0)
                scores_d(1)
                values_a(len(AU) - 1)
                for u in range(len(DU)):
                    turn(len(AU) + u, dprob(u)[:, 0], DU[u][2])
                    if u + 2 < len(DU):
                        scores_d(u + 2)
                    if u >= 1:
                        values_d(u - 1)
                values_d(len(DU) - 1)
                pe.wait_ge(s["stat_ready"], 1 + HD)
                row_stats(("dn", l), [([P[:, i]], t) for i in range(HD) for t in range(qt0, 4)])
                pe.wait_ge(s["recip_ready"], 4)
                for i in range(HD):
                    spread(("dnb", l, i), [(t, 32 + i * (4 - qt0) + t - qt0) for t in range(qt0, 4)])
                pe.wait_ge(empty["d"], number["d"][("dnb", l, HD - 1)])
                for c in range(KD):
                    w = unit(("merge", l, c))
                    wg = w[:, 0:3072].rearrange("p (k n m) -> p k n m", k=KD, n=3)
                    wo = grid(w[:, 3072:4608], 12)
                    for b in range(3):
                        column_tile("a", ("gate", l, c, b), lambda k: wg[:, k, b, :], q0, 128, KD, h)
                        if b == 0 and c:
                            ada_finish(("merge", l, c - 1))
                        column_tile("d", ("branch", l, c, b), lambda k: wo[:, 4 * b + k, :], q0, 128, 4, (oa, cv, qd)[b])
                    used(("merge", l, c))
                    ada_units(("merge", l, c))
                pe.wait_ge(s["yt_ready"], KD)
                for c in range(KD):
                    if c % 4 == 0:
                        w = unit(("out", l, c // 4))[:, 0:4096].rearrange("p (k n m) -> p k n m", k=KD, n=4)
                    column_tile("ad"[c % 2], ("out", l, c), lambda k: w[:, k, c % 4, :], q0, 128, KD, yt)
                    if c % 4 == 0:
                        ada_finish(("merge", l, KD - 1) if c == 0 else ("out", l, 0))
                    if c % 4 == 3:
                        used(("out", l, c // 4))
                        ada_units(("out", l, c // 4))
                ada_finish(("out", l, 1))
                norm_stats(l, "n2", qt0, 2 * (KD - 1))
                pe.wait_ge(s["recip_ready"], 5)
                spread(("n2b", l), [(t, 48 + t - qt0) for t in range(qt0, 4)])
                pe.wait_ge(s["shifted"], 2 * KD + (2 if l == 0 else 1) * KD)
                pe.wait_ge(router_loaded, 16 * (l + 1))
                ps = begin("d", ("router", l))
                for t in range(qt0, 4):
                    for k in range(KD):
                        last = mm(ps[:, (t - qt0) * 36:(t - qt0) * 36 + 36], h[:, k, t * 128:t * 128 + 128],
                                  wr[:, k, :], k == 0, k == KD - 1)
                end("d", last)
                for t in range(qt0, 4):
                    for half in range(2):
                        b = "ad"[half]
                        ps = begin(b, ("h2", l, t, half))
                        for k in range(4):
                            last = nc.tensor.transpose(ps[:, k * 128:k * 128 + 128],
                                                       h[:, 4 * half + k, t * 128:t * 128 + 128], ident)
                        end(b, last)
                TT = 4 - qt0
                pe.wait_ge(s["mask_ready"], 1)
                ps = begin("d", ("rank", l))
                for t in range(TT):
                    for j in range(t + 1):
                        mm(ps[:, t * 32:t * 32 + 32], ones[:, :] if j < t else rcon_at("tri"), big[4][:, j, :], j == 0, j == t)
                for j in range(TT):
                    last = mm(ps[:, 128:160], ones[:, :], big[4][:, j, :], j == 0, j == TT - 1)
                end("d", last)

                C = (T - q0) // 8

                def gather_turn(par, full_sem):
                    for k in range(KD):
                        last = nc.tensor.transpose(PS[2 + par][:, k * C:k * C + C], xg[0:C, par, k * 128:k * 128 + 128],
                                                   ident[0:C, 0:C])
                    last.then_inc(full_sem, 1)

                def up_products(par, slot, full_sem):
                    w = slot.rearrange("p (g k m) -> p g k m", g=2, k=KD)
                    for k in range(KD):
                        for g in range(2):
                            last = mm(PS[4 + par][64 * g:64 * g + C, 0:FF], xgt[:, par, k * C:k * C + C], w[:, g, k, :],
                                      k == 0, k == KD - 1)
                    last.then_inc(full_sem, 1)

                def hidden_turn(par, full_sem):
                    for k in range(2):
                        last = nc.tensor.transpose(PS[0][:, k * C:k * C + C], hid[0:C, par, k * 128:k * 128 + 128],
                                                   ident[0:C, 0:C])
                    last.then_inc(full_sem, 1)

                def down_products(par, slot, full_sem):
                    w = grid(slot, 2)
                    for k in range(2):
                        for n in range(2):
                            last = mm(PS[6 + par][64 * n:64 * n + C, :], hidt[:, par, k * C:k * C + C],
                                      w[:, k, n * 512:n * 512 + 512], k == 0, k == 1)
                    last.then_inc(full_sem, 1)

                def do_turn(j, i):
                    wait_apart(pe, s[f"xg_ready{j % 2}"], i * 32 + 16 * (j // 2 + 1))
                    if not (isinstance(i, int) and 4 * i + j < 2):
                        wait_apart(pe, s["xgt_ready"], i * 4 + j - 1)
                    gather_turn(j % 2, s["xgt_full"])

                def do_up(j, i):
                    pe.wait_ge(s[f"gu_ready{j}"], i * 32 + 32)
                    pe.wait_ge(s["xgt_ready"], i * 4 + j + 1)
                    if not (isinstance(i, int) and 4 * i + j < 2):
                        pe.wait_ge(s["hid_ready"], i * 4 + j - 1)
                    up_products(j % 2, gu[j], s["gu_full"])

                def do_hidden(j, i):
                    wait_apart(pe, s["hid_ready"], i * 4 + j + 1)
                    if not (isinstance(i, int) and 4 * i + j < 1):
                        wait_apart(pe, s["hidt_ready"], i * 4 + j)
                    hidden_turn(j % 2, s["ht_full"])

                def do_down(j, i):
                    pe.wait_ge(s[f"wd_ready{j}"], i * 16 + 16)
                    pe.wait_ge(s["hidt_ready"], i * 4 + j + 1)
                    if not (isinstance(i, int) and 4 * i + j < 2):
                        pe.wait_ge(s["y_act"], i * 4 + j - 1)
                    down_products(j % 2, wd[:, j, :], s["y_full"])

                def group(i, first, last):
                    for j in range(4):
                        do_up(j, i)
                        if not (last and j == 3):
                            jn, inn = (j + 1, i) if j < 3 else (0, i + 1)
                            do_turn(jn, inn)
                        if not (first and j == 0):
                            jp, ip = (j - 1, i) if j > 0 else (3, i - 1)
                            do_down(jp, ip)
                        do_hidden(j, i)

                do_turn(0, 0)
                group(0, True, False)
                with pe.Fori(1, NE // 4 - 1) as i:
                    group(i, False, False)
                group(NE // 4 - 1, False, True)
                do_down(3, NE // 4 - 1)
                nx = pe.value_load(meta[l][0:1, 15:16], min_val=0, max_val=OVER)
                with pe.If(nx > 0):
                    pe.wait_ge(s["y_act"], NE)
                    with pe.Fori(0, OVER) as j:
                        with pe.If(nx > j):
                            wait_apart(pe, s["ov_xg"], 16 * j + 16)
                            gather_turn(0, s["ov_pe"])
                            pe.wait_ge(s["ov_w"], 48 * j + 48)
                            pe.wait_ge(s["ov_act"], 3 * j + 1)
                            up_products(0, gu[0], s["ov_pe"])
                            wait_apart(pe, s["ov_dve"], 3 * j + 2)
                            hidden_turn(0, s["ov_pe"])
                            pe.wait_ge(s["ov_dve"], 3 * j + 3)
                            down_products(0, wd[:, 0, :], s["ov_pe"])
                for t in range(qt0, 4):
                    pe.wait_ge(s["yg_mixed"], t - qt0 + 1)
                    for half in range(2):
                        ps = begin("d", ("mix", l, t, half))
                        for k in range(4):
                            last = nc.tensor.transpose(ps[:, k * 128:k * 128 + 128],
                                                       xg[:, (t - qt0) % 2, (4 * half + k) * 128:(4 * half + k) * 128 + 128],
                                                       ident)
                        end("d", last)
            s = S[1]
            norm_stats(1, "nf", 2, 3 * (KD - 1))
            pe.wait_ge(s["recip_ready"], 6)
            spread(("nfb", 1), [(t, 52 + t - 2) for t in range(2, 4)])

        @block.scalar
        def _(act):
            A, Dn = number["a"], number["d"]
            own = [0]

            def f(out, in_, fn, **kw):
                return nc.scalar.activation(out, in_, fn, **kw)

            eps = small[:, 0:1]

            def take(key):
                act.wait_ge(full["a"], A[key])

            def give(ins):
                ins.then_inc(empty["a"], 1)

            def square(s, k, t0, seen):
                if k >= 5:
                    act.wait_ge(s["ssq"], seen + k - 4)
                f(sqt(k)[:, t0 * 128:T], x[:, k, t0 * 128:T], ACT.Square).then_inc(s["sq_ready"], 1)

            def root(key, c0, n, scale, psc=0, done=True):
                ins = f(st[:, c0:c0 + n], PS[0][:, psc:psc + n], ACT.Sqrt, scale=scale, bias=eps)
                if done:
                    give(ins)

            def shifts(s, l, name, segs, col0, base):
                n = 0
                for k in range(KD):
                    for v, t0, t1 in segs:
                        n += 1
                        if n < KD * len(segs):
                            act.wait_ge(s["modded"], base + n)
                        else:
                            act.wait_ge(empty["d"], Dn[name])
                        f(h[:, k, t0:t1], h[:, k, t0:t1], ACT.Identity, bias=ada[l][:, col0 + k, v:v + 1]) \
                            .then_inc(s["shifted"], 1)

            BOTH = [(1, 0, CTX), (0, CTX, T)]
            act.wait_ge(loaded, 16 * 5)
            f(silc[:, 0:16], silc[:, 16:32], ACT.Tanh, scale=0.5).then_inc(silc_tanh, 1)
            act.wait_ge(lam_sums, 1)
            f(small[:, 5:9], small[:, 1:5], ACT.Exp).then_inc(lam_exps, 1)
            act.wait_ge(consts_set, 2)
            act.wait_ge(x_loaded, 16)
            for l in range(DEPTH):
                s = S[l]
                q0 = 0 if l == 0 else CTX
                qt0, NQ = q0 // 128, T - q0
                nt = 4 - qt0
                SEGS = BOTH if l == 0 else BOTH[1:]
                if l == 1:
                    act.wait_ge(empty["d"], Dn[("mix", 0, 3, 1)])
                for k in range(KD):
                    square(s, k, 0, 0)
                take(("n1", l))
                root(("n1", l), 0, 4, 1.0 / D)
                shifts(s, l, ("n1b", l), BOTH, 0, 0)
                for i, p in ((0, 0), (2, 2)):
                    take(("lora", l, i))
                    t0 = q0 if i == 0 else 0
                    f(lora[:, i, t0:T], PS[0][:, 0:T - t0], ACT.Copy)
                    give(f(P[:, p, t0:T], PS[0][:, 0:T - t0], ACT.Square))
                    if i == 0:
                        act.wait_ge(empty["d"], Dn[("lora", l, 1)])
                        f(P[:, 1, q0:T], lora[:, 1, q0:T], ACT.Square)
                f(small[:, 15:16], small[:, 15:16], ACT.Copy).then_inc(s["stat_ready"], 1)
                for j in range(CT):
                    take(("gluG", l, j))
                    if j >= 2:
                        act.wait_ge(empty["d"], Dn[("gluA", l, j - 2)])
                    give(f(PT[:, j % 2, q0:T], PS[0][:, 0:NQ], ACT.Tanh, scale=0.5))
                    if j == 1:
                        take(("loraS", l))
                        root(None, 8, nt, 1.0 / QL, 0, False)
                        root(None, 8 + nt, 4, 1.0 / KVL, nt)
                for i in range(0, HD, 2):
                    take(("dq", l, i))
                    give(f(qd[:, i, q0:T], PS[0][:, 0:NQ], ACT.Copy))
                act.wait_ge(y_zeroed, 16 * DEPTH)
                for i in range(0, HA, 2):
                    take(("uq", l, i))
                    give(f(qa[0:96, i, q0:T], PS[0][0:96, 0:NQ], ACT.Copy))
                for i in range(0, HA, 2):
                    take(("uk", l, i))
                    give(f(ka[0:64, i, :], PS[0][0:64, :], ACT.Copy))
                for t in range(0, 4, 2):
                    take(("uv", l, t))
                    give(f(va[:, t, :], PS[0][:, :], ACT.Copy))
                for i in range(0, HD, 2):
                    take(("dk", l, i))
                    give(f(kd[:, i, :], PS[0][:, :], ACT.Copy))
                for t in range(0, 4, 2):
                    take(("dv", l, t))
                    give(f(vd[:, t, :], PS[0][:, :], ACT.Copy))
                def conv_norm(u):
                    if u == 3:
                        take(("lnM", l))
                        give(f(st[:, 16:16 + nt], PS[0][:, 0:nt], ACT.Copy, scale=1.0 / CC))
                    elif u == 6:
                        act.wait_ge(empty["d"], Dn[("lnMb", l)])
                        for c in range(CT):
                            f(lora[:, c, q0:T], cv[:, c, q0:T], ACT.Square).then_inc(s["conv_sq"], 1)
                    elif u == 10:
                        take(("lnV", l))
                        root(None, 24, nt, 1.0 / CC)
                    elif u == 14:
                        for c in range(CT):
                            if c < CT - 1:
                                act.wait_ge(s["conv_scaled"], c + 1)
                            else:
                                act.wait_ge(empty["d"], Dn[("lnVb", l)])
                            f(cv[:, c, q0:T], cv[:, c, q0:T], ACT.Identity, scale=0.5,
                              bias=vec_at(l, "ln_b")[:, c:c + 1]).then_inc(s["conv_act"], 1)
                            act.wait_ge(s["conv_act"], 2 * c + 1)
                            f(lora[:, c, q0:T], cv[:, c, q0:T], ACT.Tanh).then_inc(s["conv_act"], 1)

                AU, DU = attn_units(l)
                nA = len(AU)

                def exp_a(u):
                    i, t, nk = AU[u]
                    c = 8 * (u % 8)
                    act.wait_ge(s["scores_max"], u + 1)
                    if u >= 4:
                        act.wait_ge(s["pt_full"], u - 3)
                    f(P[:, u % 4, 0:nk], PS[2 + u % 4][:, 0:nk], ACT.Exp, scale=SCALE_A, bias=am[:, c + 2:c + 3],
                      accum_out=am[:, c + 4:c + 5]).then_inc(s["exp_ready"], 1)

                def exp_d(u):
                    i, t, nk = DU[u]
                    c = 8 * ((nA + u) % 8)
                    act.wait_ge(s["scores_max"], nA + u + 1)
                    act.wait_ge(s["pt_full"], nA + max(u - 2, 0))
                    if u == 2:
                        act.wait_ge(s["conv_out"], CT)
                    for m in range(2):
                        f(dprob(u)[:, m, 0:nk], PS[2 * (u % 3) + m][:, 0:nk], ACT.Exp, scale=SCALE_D,
                          bias=am[:, c + 2 + m:c + 3 + m], accum_out=am[:, c + 4 + m:c + 5 + m]) \
                            .then_inc(s["exp_ready"], 1)

                def pt_copy(g, nk):
                    act.wait_ge(s["pt_full"], g + 1)
                    if g >= 2:
                        act.wait_ge(s["pv_full"], g - 1)
                    f(PT[:, g % 2, 0:nk], PS[6][:, 0:nk], ACT.Copy).then_inc(s["pt_ready"], 1)

                exp_a(0)
                exp_a(1)
                for u in range(nA):
                    pt_copy(u, AU[u][2])
                    if u + 2 < nA:
                        exp_a(u + 2)
                    conv_norm(u)
                exp_d(0)
                exp_d(1)
                for u in range(len(DU)):
                    pt_copy(nA + u, DU[u][2])
                    if u + 2 < len(DU):
                        exp_d(u + 2)
                act.wait_ge(s["attn_out"], nA + len(DU))
                for i in range(HD):
                    f(P[:, i, q0:T], qd[:, i, q0:T], ACT.Square).then_inc(s["stat_ready"], 1)
                take(("dn", l))
                root(None, 32, HD * nt, 1.0 / (2 * DH))
                for n in range(3 * KD):
                    c, b = divmod(n, 3)
                    take(("gate", l, c, b))
                    if n >= 2:
                        act.wait_ge(empty["d"], Dn[("branch", l, (n - 2) // 3, (n - 2) % 3)])
                    give(f(P[:, n % 2, q0:T], PS[0][:, 0:NQ], ACT.Tanh, scale=0.5))
                act.wait_ge(s["g1_ready"], 1)

                def square_pair(c):
                    act.wait_ge(s["out_part"], c // 2 + 1)
                    square(s, c, qt0, KD - 1)
                    act.wait_ge(empty["d"], Dn[("out", l, c + 1)])
                    square(s, c + 1, qt0, KD - 1)

                for c in range(0, KD, 2):
                    take(("out", l, c))
                    j = (c // 2) % 2
                    if c >= 4:
                        act.wait_ge(s["out_part"], c // 2 - 1)
                    for v, t0, t1 in SEGS:
                        ins = f(P[:, j, t0:t1], PS[0][:, t0 - q0:t1 - q0], ACT.Copy,
                                scale=mod[l][:, 2 * KD + c, v:v + 1])
                    give(ins)
                    if c:
                        square_pair(c - 2)
                square_pair(KD - 2)
                take(("n2", l))
                root(None, 48, nt, 1.0 / D)
                shifts(s, l, ("n2b", l), SEGS, 3 * KD, 2 * KD - 1)
                for t in range(nt):
                    take(("h2", l, qt0 + t, 0))
                    give(f(stage[:, t, 0:512], PS[0][:, :], ACT.Copy))
                    act.wait_ge(empty["a"], A[("h2", l, qt0 + t, 0)])
                    act.wait_ge(empty["d"], Dn[("h2", l, qt0 + t, 1)])
                    act.dma_start(h2d[l][t * 128:t * 128 + 128, :], stage[:, t, :]).then_inc(s["h2_stored"], 16)
                act.wait_ge(s["gexp_in"], 1)
                f(g4[1][:, 0:nt, :], g4[0][:, 0:nt, :], ACT.Exp)
                f(col[5][:, 0:nt], col[4][:, 0:nt], ACT.Exp).then_inc(s["gexp"], 1)
                C = NQ // 8
                yrow = yd[l].rearrange("(r b) d -> r b d", b=NBLK)

                def xgt_copy(j, i):
                    act.wait_ge(s["xgt_full"], i * 4 + j + 1)
                    if not (isinstance(i, int) and 4 * i + j < 2):
                        act.wait_ge(s["gu_full"], i * 4 + j - 1)
                    f(xgt[:, j % 2, 0:KD * C], PS[2 + j % 2][:, 0:KD * C], ACT.Copy).then_inc(s["xgt_ready"], 1)

                def gate_tanh(j, i):
                    act.wait_ge(s["gu_full"], i * 4 + j + 1)
                    if not (isinstance(i, int) and 4 * i + j < 2):
                        act.wait_ge(s["hid_ready"], i * 4 + j - 1)
                    f(gt[0:C, j % 2, :], PS[4 + j % 2][0:C, 0:FF], ACT.Tanh, scale=0.5).then_inc(s["gtanh"], 1)

                def y_out(j, i):
                    p = j % 2
                    act.wait_ge(s["y_full"], i * 4 + j + 1)
                    if not (isinstance(i, int) and 4 * i + j < 2):
                        act.wait_ge(s[f"y_stored{p}"], i * 64 + 32 * (j // 2))
                    f(yy[0:64 + C, p, 0:512], PS[6 + p][0:64 + C, :], ACT.Copy).then_inc(s["y_act"], 1)
                    act.wait_ge(s["y_act"], i * 4 + j + 1)
                    for n in range(2):
                        act.dma_start(yrow[0:C, bass.ds(i * 4 + j, 1), n * 512:n * 512 + 512],
                                      yy[64 * n:64 * n + C, p:p + 1, 0:512]).then_inc(s[f"y_stored{p}"], 16)

                def group(i, first, last):
                    for j in range(4):
                        gate_tanh(j, i)
                        if not (last and j == 3):
                            xgt_copy((j + 1) % 4, i + (j + 1) // 4)
                        if not (first and j == 0):
                            y_out((j - 1) % 4, i - (j == 0))

                xgt_copy(0, 0)
                group(0, True, False)
                with act.Fori(1, NE // 4 - 1) as i:
                    group(i, False, False)
                group(NE // 4 - 1, False, True)
                y_out(3, NE // 4 - 1)
                nx = act.value_load(meta[l][0:1, 15:16], min_val=0, max_val=OVER)
                with act.If(nx > 0):
                    act.wait_ge(s["y_stored0"], 32 * NE // 2)
                    with act.Fori(0, OVER) as j:
                        with act.If(nx > j):
                            act.wait_ge(s["ov_pe"], 4 * j + 1)
                            f(xgt[:, 0, 0:KD * C], PS[2][:, 0:KD * C], ACT.Copy).then_inc(s["ov_act"], 1)
                            act.wait_ge(s["ov_pe"], 4 * j + 2)
                            f(gt[0:C, 0, :], PS[4][0:C, 0:FF], ACT.Tanh, scale=0.5).then_inc(s["ov_act"], 1)
                            act.wait_ge(s["ov_pe"], 4 * j + 4)
                            f(yy[0:64 + C, 0, 0:512], PS[6][0:64 + C, :], ACT.Copy).then_inc(s["ov_act"], 1)
                            act.wait_ge(s["ov_act"], 3 * j + 3)
                            for n in range(2):
                                act.dma_start(yrow[0:C, bass.ds(NE + j, 1), n * 512:n * 512 + 512],
                                              yy[64 * n:64 * n + C, 0:1, 0:512]).then_inc(s["ov_stored"], 16)
                            wait_apart(act, s["ov_stored"], 32 * j + 32)
            act.wait_ge(empty["d"], Dn[("mix", 1, 3, 1)])
            for k in range(KD):
                square(S[1], k, 2, 2 * (KD - 1))
            take(("nf", 1))
            root(None, 52, 2, 1.0 / D)

        @block.vector
        def _(dve):
            A, Dn = number["a"], number["d"]
            own = [0]
            V = nc.vector

            def step(ins):
                own[0] += 1
                ins.then_inc(dve_step, 1)
                dve.wait_ge(dve_step, own[0])

            def stt(out, in0, sc, in1, op0=MUL, op1=MUL):
                return V.scalar_tensor_tensor(out, in0, sc, in1, op0=op0, op1=op1)

            def take(key):
                dve.wait_ge(full["d"], Dn[key])

            def give(ins):
                ins.then_inc(empty["d"], 1)

            def ada_raw(key):
                for n in ada_behind(key):
                    take(units[n])
                    give(V.tensor_copy(ada_tmp(n), PS[1][:, :]))

            def ada_finish(key):
                for n in ada_behind(key):
                    ada_evac(units[n])

            def ada_evac(key):
                _, la, u = key
                take(("adaT", la, u))
                give(V.tensor_tensor(ada[la][:, 4 * u:4 * u + 4, :], grid(PS[1][:, 0:8], 4),
                                     vec_at(la, "b_ada")[:, 4 * u:4 * u + 4].unsqueeze(2).to_broadcast([128, 4, 2]), op=ADD))

            def scales(l, which):
                dve.wait_ge(empty["d"], max(Dn[("adaT", l, u)] for u in {0: (0, 1, 2, 3), 1: (8, 9), 2: (4, 5)}[which]))
                if which == 2:
                    V.tensor_scalar(mod[l][:, 16:24, :], ada[l][:, 16:24, :], 0.5, None, MUL).then_inc(S[l]["g1_ready"], 1)
                    dve.wait_ge(S[l]["g1_ready"], 1)
                    return
                c0 = (KD, 4 * KD)[which]
                g = vec_at(l, ("norm1_g", "norm2_g")[which]).unsqueeze(2).to_broadcast([128, KD, 2])
                step(stt(mod[l][:, which * KD:which * KD + KD, :], ada[l][:, c0:c0 + KD, :], 1.0, g, ADD, MUL))

            def recip(s, c0, n, key):
                dve.wait_ge(empty["a"], A[key])
                V.reciprocal(st[:, c0:c0 + n], st[:, c0:c0 + n]).then_inc(s["recip_ready"], 1)

            def norm_apply(l, s, key, segs, which, q0):
                take(key)
                for k in range(KD):
                    for v, t0, t1 in segs:
                        ins = stt(h[:, k, t0:t1], x[:, k, t0:t1], mod[l][:, which * KD + k, v:v + 1],
                                  PS[1][:, t0:t1])
                        if (k, t1) == (KD - 1, T):
                            give(ins)
                        else:
                            ins.then_inc(s["modded"], 1)

            BOTH = [(1, 0, CTX), (0, CTX, T)]
            V.memset(ones[:, :], 1.0).then_inc(consts_set, 1)
            step(V.memset(silz, 0.0))
            step(V.memset(small[:, :], 0.0))
            V.memset(small[:, 0:1], EPS).then_inc(consts_set, 1)
            dve.wait_ge(loaded, 16 * 5)
            for l in range(DEPTH):
                lam = vec_at(l, "lams")
                for m in range(2):
                    step(V.tensor_tensor(am[:, 0:DH], lam[:, 2 * m * DH:2 * m * DH + DH],
                                         lam[:, 2 * m * DH + DH:2 * m * DH + 2 * DH], op=MUL))
                    ins = V.reduce_sum(small[:, 1 + 2 * l + m:2 + 2 * l + m], am[:, 0:DH], AX.X)
                    if (l, m) == (1, 1):
                        ins.then_inc(lam_sums, 1)
                    else:
                        step(ins)
            dve.wait_ge(silc_tanh, 1)
            step(stt(silc[:, 0:16], silc[:, 0:16], 1.0, silc[:, 16:32], ADD, MUL))
            V.tensor_scalar(silz.rearrange("p (k n) -> p k n", k=KD)[:, :, 0:2], silc[:, 0:16].rearrange("p (k n) -> p k n", k=KD),
                            0.5, None, MUL).then_inc(silc_ready, 1)
            dve.wait_ge(lam_exps, 1)
            for l in range(DEPTH):
                lam_init = 0.8 - 0.6 * math.exp(-0.3 * l)
                step(V.tensor_tensor(small[:, 9 + l:10 + l], small[:, 6 + 2 * l:7 + 2 * l], small[:, 5 + 2 * l:6 + 2 * l], op=SUB))
                step(V.tensor_scalar(small[:, 9 + l:10 + l], small[:, 9 + l:10 + l], -lam_init, None, ADD))
                step(V.tensor_scalar(vec_at(l, "sub_g"), vec_at(l, "sub_g"), 1.0 - lam_init, None, MUL))
                step(V.tensor_scalar(vec_at(l, "conv_w"), vec_at(l, "conv_w"), 0.5, None, MUL))
                step(V.tensor_scalar(vec_at(l, "ln_b"), vec_at(l, "ln_b"), 0.5, None, MUL))
            step(V.tensor_copy(tok, rcon_at("token")))
            V.memset(zero, 0).then_inc(table_zero, 1)
            ada_raw(None)
            ada_finish(None)
            dve.wait_ge(x_loaded, 16)
            for l in range(DEPTH):
                s = S[l]
                q0 = 0 if l == 0 else CTX
                qt0, NQ = q0 // 128, T - q0
                nt = 4 - qt0
                SEGS = BOTH if l == 0 else BOTH[1:]
                seqs = slice(0 if l == 0 else 1, 2)
                scales(l, 0)
                recip(s, 0, 4, ("n1", l))
                norm_apply(l, s, ("n1b", l), BOTH, 0, 0)
                take(("lora", l, 1))
                give(V.tensor_copy(lora[:, 1, q0:T], PS[1][:, 0:NQ]))
                take(("lora", l, 3))
                give(V.tensor_copy(lora[64:96, 3, :], PS[1][0:32, :]))
                ada_raw(("lora", l, 0))
                dve.wait_ge(s["pool_set"], 1)
                for j in range(CT):
                    if j % 2 == 0:
                        ada_finish(("glu", l, 0) if j else ("lora", l, 0))
                    take(("gluA", l, j))
                    dve.wait_ge(empty["a"], A[("gluG", l, j)])
                    give(stt(up[:, j, seqs, PAD:PAD + 256], PT[:, j % 2, q0:T].rearrange("p (s u) -> p s u", u=256), 1.0,
                             PS[1][:, 0:NQ].rearrange("p (s u) -> p s u", u=256), ADD, MUL))
                    if j % 2 == 1:
                        ada_raw(("glu", l, j // 2))
                last_glu = Dn[("gluA", l, CT - 1)]
                recip(s, 8, nt + 4, ("loraS", l))
                take(("loraQ", l))
                stt(lora[:, 0, q0:T], lora[:, 0, q0:T], vec_at(l, "q_g")[:, 0:1], PS[1][:, q0:T])
                give(stt(lora[:, 1, q0:T], lora[:, 1, q0:T], vec_at(l, "q_g")[:, 1:2], PS[1][:, q0:T]))
                take(("loraK", l))
                give(stt(lora[:, 2, :], lora[:, 2, :], vec_at(l, "kv_g"), PS[1][:, :]))
                kr, krt = lora[64:96, 3, CTX:T], PT[64:96, 0, 0:SEQ]
                swap = [(r + 16) % 32 for r in range(32)]
                dve.wait_ge(empty["d"], last_glu)
                V.stream_shuffle(krt, kr, swap).then_inc(dve_step, 1)
                own[0] += 1
                dve.wait_ge(dve_step, own[0])
                step(V.tensor_tensor(krt, krt, con_at("sin_a")[64:96, :], op=MUL))
                step(V.tensor_tensor(kr, kr, con_at("cos_a")[64:96, :], op=MUL))
                V.tensor_tensor(kr, kr, krt, op=ADD).then_inc(s["kr_ready"], 1)

                conv_at = [0]
                base = own[0]

                def conv(n):
                    for o in range(conv_at[0], min(conv_at[0] + n, CW * CT)):
                        tap, c = divmod(o, CT)
                        w_ = vec_at(l, "conv_w")[:, c * CW + tap:c * CW + tap + 1]
                        src = up[:, c, seqs, tap:tap + 256]
                        dst = cv[:, c, q0:T].rearrange("p (s u) -> p s u", u=256)
                        if tap == 0:
                            ins = V.tensor_scalar(dst, src, w_, vec_at(l, "conv_b")[:, c:c + 1], MUL, ADD)
                        else:
                            dve.wait_ge(dve_step, conv_done[o - CT])
                            ins = stt(dst, src, w_, dst, MUL, ADD)
                        own[0] += 1
                        conv_done[o] = own[0]
                        ins.then_inc(dve_step, 1)
                    conv_at[0] = min(conv_at[0] + n, CW * CT)

                conv_done = {}

                def swapped_sin(dst, src, nth, wait):
                    dve.wait_ge(s["rope_pool"], wait) if wait else dve.wait_ge(full["a"], A[("loraS", l)])
                    for o_, i_ in ((0, 1), (1, 0), (2, 3), (3, 2)):
                        ins = V.tensor_tensor(dst[32 * o_:32 * o_ + 32], src[32 * i_:32 * i_ + 32, :, CTX:T],
                                              con_at("sin_d")[32 * i_:32 * i_ + 32, :].unsqueeze(1).to_broadcast([32, HD, SEQ]),
                                              op=MUL)
                    ins.then_inc(s["rope_part"], 1)

                Pd = P[:, 0:2, :].rearrange("p a (b n) -> p (a b) n", b=2)
                Pq = P[64:96, :, :].rearrange("p a (b n) -> p (a b) n", b=2)
                few, many = (4, 16)
                conv(few)
                for i in range(1, HD, 2):
                    if i == 1:
                        ada_finish(("glu", l, 1))
                    take(("dq", l, i))
                    give(V.tensor_copy(qd[:, i, q0:T], PS[1][:, 0:NQ]))
                    conv(many - 4)
                ada_raw(("dq", l, 0))
                dve.wait_ge(empty["d"], Dn[("dq", l, HD - 1)])
                dve.wait_ge(empty["a"], A[("dq", l, HD - 2)])
                swapped_sin(Pd, qd, 1, 0)
                dve.wait_ge(y_zeroed, 16 * DEPTH)
                ada_finish(("dq", l, 0))
                for i in range(1, HA, 2):
                    take(("uq", l, i))
                    give(V.tensor_copy(qa[0:96, i, q0:T], PS[1][0:96, 0:NQ]))
                for i in range(1, HA, 2):
                    take(("uk", l, i))
                    give(V.tensor_copy(ka[0:64, i, :], PS[1][0:64, :]))
                for t in range(1, 4, 2):
                    take(("uv", l, t))
                    give(V.tensor_copy(va[:, t, :], PS[1][:, :]))
                ada_raw(("ukv", l, 0))
                dve.wait_ge(empty["a"], A[("uq", l, HA - 2)])
                dve.wait_ge(empty["d"], Dn[("uq", l, HA - 1)])
                dve.wait_ge(s["rope_pool"], 1)
                V.stream_shuffle(Pq, qa[64:96, :, CTX:T], swap).then_inc(s["rope_part"], 1)
                for i in range(1, HD, 2):
                    conv(many + 4)
                    if i == 1:
                        ada_finish(("ukv", l, 0))
                    take(("dk", l, i))
                    give(V.tensor_copy(kd[:, i, :], PS[1][:, :]))
                ada_raw(("dk", l, 0))
                dve.wait_ge(empty["d"], Dn[("dk", l, HD - 1)])
                dve.wait_ge(empty["a"], A[("dk", l, HD - 2)])
                swapped_sin(Pd, kd, 3, 2)
                for t in range(1, 4, 2):
                    conv(many)
                    if t == 1:
                        ada_finish(("dk", l, 0))
                    take(("dv", l, t))
                    give(V.tensor_copy(vd[:, t, :], PS[1][:, :]))
                ada_raw(("dv", l, 0))
                ada_finish(("dv", l, 0))
                conv(CW * CT)
                dve.wait_ge(dve_step, own[0])
                V.memset(small[:, 14:15], 0.0).then_inc(s["conv_v"], 1)
                def conv_norm(u):
                    if u == 5:
                        take(("lnMb", l))
                        for c in range(CT):
                            ins = V.tensor_tensor(cv[:, c, q0:T], cv[:, c, q0:T], PS[1][:, q0:T], op=SUB)
                        give(ins)
                    elif u == 11:
                        recip(s, 24, nt, ("lnV", l))
                    elif u == 13:
                        take(("lnVb", l))
                        for c in range(CT):
                            ins = stt(cv[:, c, q0:T], cv[:, c, q0:T], vec_at(l, "ln_g")[:, c:c + 1], PS[1][:, q0:T])
                            if c < CT - 1:
                                ins.then_inc(s["conv_scaled"], 1)
                            else:
                                give(ins)
                    elif u == 15:
                        for c in range(CT):
                            dve.wait_ge(s["conv_act"], 2 * c + 2)
                            stt(cv[:, c, q0:T], lora[:, c, q0:T], 1.0, cv[:, c, q0:T], ADD, MUL).then_inc(s["conv_out"], 1)

                AU, DU = attn_units(l)
                nA = len(AU)
                nlam = small[:, 9 + l:10 + l]

                def peak(g, banks, nk, scale, tiles):
                    c = 8 * (g % 8)
                    for m, b in enumerate(banks):
                        dve.wait_ge(s["scores"], tiles + m + 1)
                        ins = V.reduce_max(am[:, c + m:c + m + 1], PS[b][:, 0:nk], AX.X)
                    step(ins)
                    n = len(banks)
                    V.tensor_scalar(am[:, c + 2:c + 2 + n], am[:, c:c + n], -scale, None, MUL).then_inc(s["scores_max"], 1)

                def peak_a(u):
                    peak(u, [2 + u % 4], AU[u][2], SCALE_A, u)

                def peak_d(u):
                    peak(nA + u, [2 * (u % 3), 2 * (u % 3) + 1], DU[u][2], SCALE_D, nA + 2 * u)

                def probs_a(u):
                    c, nk = 8 * (u % 8), AU[u][2]
                    dve.wait_ge(s["exp_ready"], u + 1)
                    step(V.reciprocal(am[:, c + 6:c + 7], am[:, c + 4:c + 5]))
                    V.tensor_scalar(P[:, u % 4, 0:nk], P[:, u % 4, 0:nk], am[:, c + 6:c + 7], None, MUL) \
                        .then_inc(s["probs_ready"], 1)

                def probs_d(u):
                    c, nk = 8 * ((nA + u) % 8), DU[u][2]
                    p0, p1 = dprob(u)[:, 0, 0:nk], dprob(u)[:, 1, 0:nk]
                    dve.wait_ge(s["exp_ready"], nA + 2 * u + 2)
                    step(V.reciprocal(am[:, c + 6:c + 8], am[:, c + 4:c + 6]))
                    step(V.tensor_scalar(p1, p1, am[:, c + 7:c + 8], nlam, MUL, MUL))
                    stt(p0, p0, am[:, c + 6:c + 7], p1, MUL, ADD).then_inc(s["probs_ready"], 1)

                def out_copy(g, out, ps):
                    dve.wait_ge(s["pv_full"], g + 1)
                    V.tensor_copy(out, ps).then_inc(s["attn_out"], 1)

                def out_a(u):
                    i, t, nk = AU[u]
                    r = 64 * (i % 2)
                    out_copy(u, oa[r:r + 64, i // 2, t * 128:t * 128 + 128], PS[7][r:r + 64, 0:128])

                def out_d(u):
                    i, t, nk = DU[u]
                    out_copy(nA + u, qd[:, i, t * 128:t * 128 + 128], PS[7][:, 0:128])

                peak_a(0)
                peak_a(1)
                for u in range(nA):
                    probs_a(u)
                    if u + 2 < nA:
                        peak_a(u + 2)
                    if u >= 1:
                        out_a(u - 1)
                    conv_norm(u)
                peak_d(0)
                peak_d(1)
                out_a(nA - 1)
                for u in range(len(DU)):
                    probs_d(u)
                    if u + 2 < len(DU):
                        peak_d(u + 2)
                    if u >= 1:
                        out_d(u - 1)
                out_d(len(DU) - 1)
                recip(s, 32, HD * nt, ("dn", l))
                for i in range(HD):
                    take(("dnb", l, i))
                    give(stt(qd[:, i, q0:T], qd[:, i, q0:T], vec_at(l, "sub_g"), PS[1][:, q0:T]))
                for c in range(KD):
                    for b in range(3):
                        n = 3 * c + b
                        if b == 0 and c:
                            ada_finish(("merge", l, c - 1))
                        take(("branch", l, c, b))
                        dve.wait_ge(empty["a"], A[("gate", l, c, b)])
                        if b == 1 and c:
                            dve.wait_ge(s["merge_part"], c)
                        if b == 2 and c:
                            dve.wait_ge(s["yt_ready"], c)
                        out = yt[:, c, q0:T] if b == 0 else P[:, b + 1, q0:T]
                        give(stt(out, P[:, n % 2, q0:T], 1.0, PS[1][:, 0:NQ], ADD, MUL))
                    ada_raw(("merge", l, c))
                ada_finish(("merge", l, KD - 1))
                scales(l, 2)
                for c in range(1, KD, 2):
                    take(("out", l, c))
                    for v, t0, t1 in SEGS:
                        ins = stt(x[:, c, t0:t1], PS[1][:, t0 - q0:t1 - q0], mod[l][:, 2 * KD + c, v:v + 1],
                                  x[:, c, t0:t1], MUL, ADD)
                    give(ins)
                    if c % 4 == 3:
                        ada_raw(("out", l, c // 4))
                        ada_finish(("out", l, c // 4))
                scales(l, 1)
                recip(s, 48, nt, ("n2", l))
                norm_apply(l, s, ("n2b", l), SEGS, 1, q0)
                take(("router", l))
                give(V.tensor_tensor(lg[:, 0:nt, :], grid(PS[1][:, 0:36 * nt], nt),
                                     vec_at(l, "b_r").unsqueeze(1).to_broadcast([128, nt, NG + NE]), op=ADD))
                for t in range(nt):
                    take(("h2", l, qt0 + t, 1))
                    give(V.tensor_copy(stage[:, t, 512:1024], PS[1][:, :]))

                def over(c, n):
                    return c[:, 0:nt].unsqueeze(2).to_broadcast([128, nt, n])

                def row(r, n):
                    return r.unsqueeze(1).to_broadcast([128, nt, n])

                def first_max(values, n, desc, top, tmp, hot, best):
                    step(V.reduce_max(best[:, 0:nt], values, AX.X))
                    step(V.tensor_tensor(tmp, values, over(best, n), op=ALU.is_equal))
                    step(V.tensor_tensor(tmp, tmp, row(desc, n), op=MUL))
                    step(V.reduce_max(top[:, 0:nt], tmp, AX.X))
                    step(V.tensor_tensor(hot, tmp, over(top, n), op=ALU.is_equal))

                B = [b_[:, 0:nt, :] for b_ in big]
                glog = lg[:, 0:nt, 0:NG]
                g0, g1_, g2_ = (g_[:, 0:nt, :] for g_ in g4)
                first_max(glog, NG, rcon_at("desc4"), col[1], g1_, g2_, col[0])
                step(V.tensor_tensor(g0, glog, over(col[0], NG), op=SUB))
                step(V.tensor_scalar(g2_, g2_, -1.0, 3.0e38, ADD, MUL))
                for t in range(nt):
                    ins = V.tensor_tensor(B[0][:, t, :].rearrange("p (g e) -> p g e", g=NG),
                                          lg[:, t, NG:].rearrange("p (g e) -> p g e", g=NG),
                                          g4[2][:, t, :].unsqueeze(2).to_broadcast([128, NG, EG]), op=ADD)
                step(ins)
                first_max(B[0], NE, rcon_at("desc32"), col[1], B[1], B[2], col[2])
                step(V.scalar_tensor_tensor(B[0], B[2], -3.1e38, B[0], op0=MUL, op1=ADD))
                first_max(B[0], NE, rcon_at("desc32"), col[1], B[1], B[3], col[3])
                V.tensor_tensor(col[4][:, 0:nt], col[3][:, 0:nt], col[2][:, 0:nt], op=SUB).then_inc(s["gexp_in"], 1)
                V.tensor_tensor(B[4], B[2], B[3], op=ADD).then_inc(s["mask_ready"], 1)
                dve.wait_ge(s["gexp"], 1)
                step(V.reduce_sum(col[6][:, 0:nt], g1_, AX.X))
                step(stt(col[7][:, 0:nt], col[5][:, 0:nt], 1.0, col[6][:, 0:nt], ADD, MUL))
                step(V.reciprocal(col[7][:, 0:nt], col[7][:, 0:nt]))
                step(V.tensor_scalar(col[8][:, 0:nt], col[7][:, 0:nt], 0.5, None, MUL))
                step(V.tensor_tensor(col[9][:, 0:nt], col[8][:, 0:nt], col[5][:, 0:nt], op=MUL))
                C = NQ // 8
                half_up = 1.0 / (2 * C) - 0.5
                extra, cum, cum2, dvec = c32[0], c32[1], c32[2], c32[3]
                take(("rank", l))
                step(V.tensor_copy(B[5], grid(PS[1][:, 0:32 * nt], nt)))
                step(V.tensor_scalar(extra, PS[1][:, 128:160], 1.0 / C, half_up - 1.0 / C, MUL, ADD))
                step(V.tensor_scalar(extra, extra, ROUND, None, ADD))
                step(V.tensor_scalar(extra, extra, -ROUND, 0.0, ADD, ALU.max))
                give(V.tensor_copy(cum, extra))
                dve.wait_ge(empty["d"], Dn[("rank", l)])
                for sh in (1, 2, 4, 8, 16):
                    step(V.tensor_copy(cum2[:, 0:sh], cum[:, 0:sh]))
                    step(V.tensor_tensor(cum2[:, sh:NE], cum[:, sh:NE], cum[:, 0:NE - sh], op=ADD))
                    cum, cum2 = cum2, cum
                step(V.tensor_tensor(dvec, cum, extra, op=SUB))
                step(stt(dvec, dvec, float(NE - 1), rcon_at("expert"), ADD, SUB))
                step(V.tensor_scalar(B[6], B[5], 1.0 / C, half_up, MUL, ADD))
                step(V.tensor_scalar(B[6], B[6], ROUND, None, ADD))
                step(V.tensor_scalar(B[6], B[6], -ROUND, None, ADD))
                step(V.tensor_scalar(B[7], B[6], 1.0, None, ALU.is_ge))
                step(V.tensor_tensor(B[1], B[6], row(dvec, NE), op=ADD))
                step(V.tensor_tensor(B[1], B[1], B[7], op=MUL))
                step(V.tensor_tensor(B[1], B[1], row(rcon_at("expert"), NE), op=ADD))
                step(stt(B[1], B[5], float(NBLK), B[1], MUL, ADD))
                step(stt(B[1], B[6], float(-NBLK * C), B[1], MUL, ADD))
                for m in range(2):
                    step(V.tensor_tensor(B[7], B[1], B[2 + m], op=MUL))
                    step(V.reduce_sum(col[0][:, 0:nt], B[7], AX.X))
                    step(V.tensor_copy(sl[:, m, 0:nt], col[0][:, 0:nt]))
                step(V.tensor_tensor(cmp15, cum.unsqueeze(1).to_broadcast([128, OVER, NE]),
                                     rcon_at("nth").unsqueeze(2).to_broadcast([128, OVER, NE]), op=ALU.is_le))
                step(V.reduce_sum(ov15[:, 0:OVER], cmp15, AX.X))
                step(V.tensor_copy(ov15[:, OVER:OVER + 1], cum[:, NE - 1:NE]))
                V.tensor_copy(meta[l], ov15).then_inc(s["slots_ready"], 1)

                def hidden(j, i):
                    p = j % 2
                    dve.wait_ge(s["gtanh"], i * 4 + j + 1)
                    if not (isinstance(i, int) and 4 * i + j < 2):
                        dve.wait_ge(s["ht_full"], i * 4 + j - 1)
                    stt(hid[0:C, p, :], gt[0:C, p, :], 1.0, PS[4 + p][0:C, 0:FF], ADD, MUL).then_inc(hid_half, 1)
                    dve.wait_ge(hid_half, 32 * l + i * 4 + j + 1)
                    V.tensor_tensor(hid[0:C, p, :], hid[0:C, p, :], PS[4 + p][64:64 + C, 0:FF], op=MUL) \
                        .then_inc(s["hid_ready"], 1)

                def hidden_copy(j, i):
                    p = j % 2
                    dve.wait_ge(s["ht_full"], i * 4 + j + 1)
                    if not (isinstance(i, int) and 4 * i + j < 2):
                        dve.wait_ge(s["y_full"], i * 4 + j - 1)
                    V.tensor_copy(hidt[:, p, 0:2 * C], PS[0][:, 0:2 * C]).then_inc(s["hidt_ready"], 1)

                def group(i):
                    for j in range(4):
                        hidden(j, i)
                        hidden_copy(j, i)

                group(0)
                with dve.Fori(1, NE // 4) as i:
                    group(i)
                nx = dve.value_load(meta[l][0:1, 15:16], min_val=0, max_val=OVER)
                with dve.If(nx > 0):
                    with dve.Fori(0, OVER) as j:
                        with dve.If(nx > j):
                            dve.wait_ge(s["ov_act"], 3 * j + 2)
                            stt(hid[0:C, 0, :], gt[0:C, 0, :], 1.0, PS[4][0:C, 0:FF], ADD, MUL).then_inc(s["ov_dve"], 1)
                            dve.wait_ge(s["ov_dve"], 3 * j + 1)
                            V.tensor_tensor(hid[0:C, 0, :], hid[0:C, 0, :], PS[4][64:64 + C, 0:FF], op=MUL) \
                                .then_inc(s["ov_dve"], 1)
                            dve.wait_ge(s["ov_pe"], 4 * j + 3)
                            V.tensor_copy(hidt[:, 0, 0:2 * C], PS[0][:, 0:2 * C]).then_inc(s["ov_dve"], 1)
                for t in range(nt):
                    p = t % 2
                    dve.wait_ge(s[f"yg_ready{p}"], 32 * (t // 2) + 32)
                    step(V.tensor_scalar(xg[:, p, :], xg[:, p, :], col[8][:, t:t + 1], None, MUL))
                    stt(xg[:, p, :], yy[:, p, :], col[9][:, t:t + 1], xg[:, p, :], MUL, ADD).then_inc(s["yg_mixed"], 1)
                    v = 1 if qt0 + t < 2 else 0
                    for half in range(2):
                        take(("mix", l, qt0 + t, half))
                        for k in range(4):
                            xs = x[:, 4 * half + k, (qt0 + t) * 128:(qt0 + t) * 128 + 128]
                            ins = stt(xs, PS[1][:, k * 128:k * 128 + 128], ada[l][:, 5 * KD + 4 * half + k, v:v + 1],
                                      xs, MUL, ADD)
                        give(ins)
            s = S[1]
            recip(s, 52, 2, ("nf", 1))
            take(("nfb", 1))
            for k in range(KD):
                ins = stt(h[:, k, CTX:T], x[:, k, CTX:T], fing[:, k:k + 1], PS[1][:, CTX:T])
            ins.then_inc(out_ready, 1)

        @block.gpsimd
        def _(pool):
            A, Dn = number["a"], number["d"]
            own = [0]
            G = nc.gpsimd

            def step(ins):
                own[0] += 1
                ins.then_inc(pool_step, 1)
                pool.wait_ge(pool_step, own[0])

            def add_squares(s, ks, t0, n):
                for k in ks:
                    if k == 0:
                        continue
                    pool.wait_ge(s["sq_ready"], n * KD + k + 1)
                    if k > 1:
                        pool.wait_ge(s["ssq"], n * (KD - 1) + k - 1)
                    G.tensor_tensor(P[:, 3, t0 * 128:T], P[:, 3, t0 * 128:T], sqt(k)[:, t0 * 128:T], op=ADD) \
                        .then_inc(s["ssq"], 1)

            pool.wait_ge(table_zero, 1)
            for l in range(DEPTH):
                pool.dma_start(td[l].rearrange("(r b) o -> r (b o)", b=NBLK), zero[0:CAP[l], :]).then_inc(zeroed, 16)
            for l in range(DEPTH):
                s = S[l]
                q0 = 0 if l == 0 else CTX
                qt0, NQ = q0 // 128, T - q0
                nt = 4 - qt0
                if l == 1:
                    pool.wait_ge(empty["d"], Dn[("mix", 0, 3, 1)])
                G.memset(arena[:, 16384:16384 + CT * 2 * UP], 0.0).then_inc(s["pool_set"], 1)
                add_squares(s, range(KD), 0, 0)
                pool.wait_ge(s["pool_set"], 1)
                if l == 0:
                    G.memset(arena[:, 0:D], 0.0).then_inc(pool_step, 1)
                    own[0] += 1
                    pool.wait_ge(pool_step, own[0])
                    pool.wait_ge(empty["d"], Dn[("lora", 0, 1)])
                    for ll in range(DEPTH):
                        pool.dma_start(yd[ll].rearrange("(r b) d -> r b d", b=NBLK)[:, NE:, :],
                                       arena[0:CAP[ll], 0:D].unsqueeze(1).to_broadcast([CAP[ll], NBLK - NE, D])) \
                            .then_inc(y_zeroed, 16)
                pool.wait_ge(s["kr_ready"], 1)
                for n in ada_behind(("glu", l, 1)):
                    pool.wait_ge(empty["d"], Dn[("adaT",) + units[n][1:]])
                G.tensor_copy(ka[64:96, :, :], lora[64:96, 3:4, :].to_broadcast([32, HA, T])).then_inc(s["pool_set"], 1)

                pool.wait_ge(s["pool_set"], 2)

                def rotate(part, rows, q, t, cos, sin, heads):
                    pool.wait_ge(s["rope_part"], part)
                    r = slice(*rows)
                    if sin is not None:
                        step(G.tensor_tensor(t, t, con_at(sin)[r, :].unsqueeze(1).to_broadcast([rows[1] - rows[0], heads, SEQ]), op=MUL))
                    step(G.tensor_tensor(q[r, :, CTX:T], q[r, :, CTX:T],
                                         con_at(cos)[r, :].unsqueeze(1).to_broadcast([rows[1] - rows[0], heads, SEQ]), op=MUL))
                    pool.wait_ge(pool_step, own[0])
                    G.tensor_tensor(q[r, :, CTX:T], q[r, :, CTX:T], t, op=ADD).then_inc(s["rope_pool"], 1)
                    pool.wait_ge(s["rope_pool"], part)

                Pd = P[:, 0:2, :].rearrange("p a (b n) -> p (a b) n", b=2)
                Pq = P[64:96, :, :].rearrange("p a (b n) -> p (a b) n", b=2)
                rotate(1, (0, 128), qd, Pd, "cos_d", None, HD)
                rotate(2, (64, 96), qa, Pq, "cos_a", "sin_a", HA)
                rotate(3, (0, 128), kd, Pd, "cos_d", None, HD)
                for c in range(KD):
                    pool.wait_ge(empty["d"], Dn[("branch", l, c, 1)])
                    G.tensor_tensor(yt[:, c, q0:T], yt[:, c, q0:T], P[:, 2, q0:T], op=ADD).then_inc(s["merge_part"], 1)
                    pool.wait_ge(s["merge_part"], c + 1)
                    pool.wait_ge(empty["d"], Dn[("branch", l, c, 2)])
                    G.tensor_tensor(yt[:, c, q0:T], yt[:, c, q0:T], P[:, 3, q0:T], op=ADD).then_inc(s["yt_ready"], 1)
                for c in range(0, KD, 2):
                    pool.wait_ge(empty["a"], A[("out", l, c)])
                    G.tensor_tensor(x[:, c, q0:T], x[:, c, q0:T], P[:, (c // 2) % 2, q0:T], op=ADD) \
                        .then_inc(s["out_part"], 1)
                    if c:
                        add_squares(s, (c - 2, c - 1), qt0, 1)
                add_squares(s, (KD - 2, KD - 1), qt0, 1)
                C = NQ // 8
                pool.wait_ge(zeroed, 16 * DEPTH)
                pool.wait_ge(s["slots_ready"], 1)
                for t in range(nt):
                    for m in range(2):
                        pool.indirect_dma_start(out=td[l][:, :], out_offset=bass.IndirectOffsetOnAxis(ap=sl[:, m, t:t + 1], axis=0),
                                                in_=tok[:, t:t + 1], in_offset=None).then_inc(s["tokens_moved"], 16)
                pool.wait_ge(s["tokens_moved"], 16 * 2 * nt)
                pool.dma_start(idx[0:C, :], td[l].rearrange("(r b) o -> r (b o)", b=NBLK)[0:C, :]).then_inc(s["tokens_moved"], 16)
                pool.wait_ge(s["tokens_moved"], 16 * 2 * nt + 16)
                pool.wait_ge(s["h2_stored"], 16 * nt)

                def gather(j, i):
                    p = j % 2
                    if not (isinstance(i, int) and 4 * i + j < 2):
                        pool.wait_ge(s["xgt_full"], i * 4 + j - 1)
                    G.tensor_copy(icol[0:C, p:p + 1], idx[0:C, bass.ds(i * 4 + j, 1)]).then_inc(s["icol_ready"], 1)
                    wait_apart(pool, s["icol_ready"], i * 4 + j + 1)
                    pool.indirect_dma_start(out=xg[0:C, p, :], out_offset=None, in_=h2d[l][:, :],
                                            in_offset=bass.IndirectOffsetOnAxis(ap=icol[0:C, p:p + 1], axis=0)) \
                        .then_inc(s[f"xg_ready{p}"], 16)

                for j in range(4):
                    gather(j, 0)
                with pool.Fori(1, NE // 4) as i:
                    for j in range(4):
                        gather(j, i)
                nx = pool.value_load(meta[l][0:1, 15:16], min_val=0, max_val=OVER)
                with pool.If(nx > 0):
                    pool.wait_ge(s["xgt_full"], NE - 1)
                    with pool.Fori(0, OVER) as j:
                        with pool.If(nx > j):
                            G.tensor_copy(icol[0:C, 0:1], idx[0:C, bass.ds(NE + j, 1)]).then_inc(s["ov_icol"], 1)
                            wait_apart(pool, s["ov_icol"], j + 1)
                            pool.indirect_dma_start(out=xg[0:C, 0, :], out_offset=None, in_=h2d[l][:, :],
                                                    in_offset=bass.IndirectOffsetOnAxis(ap=icol[0:C, 0:1], axis=0)) \
                                .then_inc(s["ov_xg"], 16)
                            wait_apart(pool, s["ov_stored"], 32 * j + 32)
                for p in range(2):
                    pool.wait_ge(s[f"y_stored{p}"], 32 * NE // 2)
                for t in range(nt):
                    p = t % 2
                    if t >= 2:
                        pool.wait_ge(full["d"], Dn[("mix", l, qt0 + t - 2, 1)])
                    for buf, m in ((xg, 0), (yy, 1)):
                        pool.indirect_dma_start(out=buf[:, p, :], out_offset=None, in_=yd[l][:, :],
                                                in_offset=bass.IndirectOffsetOnAxis(ap=sl[:, m, t:t + 1], axis=0)) \
                            .then_inc(s[f"yg_ready{p}"], 16)

            add_squares(S[1], range(KD), 2, 2)

        @block.sync
        def _(sp):
            Dn = number["d"]
            sp.dma_start(silc[:, 16:32], a["cvec"]).then_inc(loaded, 16)
            sp.dma_start(vec, a["vecs"]).then_inc(loaded, 16)
            sp.dma_start(con[:, :], a["con"]).then_inc(loaded, 16)
            sp.dma_start(fing[:, :], a["final_g"]).then_inc(loaded, 16)
            sp.dma_start(rcon, a["rcon"]).then_inc(loaded, 16)

            def load(n):
                kind, l, i = units[n]
                slot, src = ring[:, n % NRING, :], a["out_w" if kind == "out" else kind][l, i]
                if n >= NRING:
                    b, e = unit_end[units[n - NRING]]
                    sp.wait_ge(full[b], e)
                sp.dma_start(slot[:, 0:src.shape[1]], src).then_inc(ring_ready[n % NRING], 16)

            def expert(l, j, i, e):
                s = S[l]
                if not (isinstance(i, int) and i == 0):
                    sp.wait_ge(s["gu_full"], i * 4 + j - 3)
                for m, n_ in enumerate(("w_gate", "w_up")):
                    sp.dma_start(gu[j][:, 2048 * m:2048 * m + 2048].unsqueeze(1),
                                 a[n_][l][bass.ds(e, 1)].rearrange("e p n -> p e n")).then_inc(s[f"gu_ready{j}"], 16)
                if not (isinstance(i, int) and i == 0):
                    sp.wait_ge(s["y_full"], i * 4 + j - 3)
                sp.dma_start(wd[:, j:j + 1, :], a["w_down"][l][bass.ds(e, 1)].rearrange("e p n -> p e n")) \
                    .then_inc(s[f"wd_ready{j}"], 16)

            n = 0
            for l in range(DEPTH):
                s = S[l]
                while n < len(units) and (l == 1 or n < first_of_layer1):
                    load(n)
                    n += 1
                    if n == NRING and l == 0:
                        sp.dma_start(x, a["x"]).then_inc(x_loaded, 16)
                        sp.dma_start(wr, a["router"][0]).then_inc(router_loaded, 16)
                b, e = unit_end[("out", l, 1)]
                sp.wait_ge(full[b], e)
                last = {m % NRING: unit_end[units[m]] for m in range(n - NRING, n)}
                for j in range(4):
                    if j in last:
                        sp.wait_ge(full[last[j][0]], last[j][1])
                    expert(l, j, 0, j)
                if l == 0:
                    sp.wait_ge(full["d"], Dn[("router", 0)])
                    sp.dma_start(wr, a["router"][1]).then_inc(router_loaded, 16)
                with sp.Fori(1, NE // 4) as i:
                    for j in range(4):
                        expert(l, j, i, i * 4 + j)
                sp.wait_ge(s["slots_ready"], 1)
                nx = sp.value_load(meta[l][0:1, 15:16], min_val=0, max_val=OVER)
                with sp.If(nx > 0):
                    sp.wait_ge(s["gu_full"], NE - 3)
                    sp.wait_ge(s["y_full"], NE - 3)
                    with sp.Fori(0, OVER) as j:
                        with sp.If(nx > j):
                            e = sp.value_load(meta[l][0:1, bass.ds(j, 1)], min_val=0, max_val=NE - 1)
                            for m, n_ in enumerate(("w_gate", "w_up")):
                                sp.dma_start(gu[0][:, 2048 * m:2048 * m + 2048].unsqueeze(1),
                                             a[n_][l][bass.ds(e, 1)].rearrange("e p n -> p e n")).then_inc(s["ov_w"], 16)
                            sp.dma_start(wd[:, 0:1, :], a["w_down"][l][bass.ds(e, 1)].rearrange("e p n -> p e n")) \
                                .then_inc(s["ov_w"], 16)
                            wait_apart(sp, s["ov_stored"], 32 * j + 32)
                sp.wait_ge(s["gu_full"], NE)
            sp.wait_ge(out_ready, 1)
            sp.dma_start(a["out"].rearrange("(k p) t -> p k t", p=128), h[:, :, CTX:T]).then_inc(out_stored, 16)
            sp.wait_ge(out_stored, 16)


def tables():
    con = np.zeros((128, NC), np.float32)
    con[:, 0:128] = np.eye(128)
    con[:, 128:130] = np.arange(128)[:, None] % 32 == np.arange(2)
    tok = np.arange(SEQ)
    row, colm = (tok // GRID_W).astype(np.float32), (tok % GRID_W).astype(np.float32)
    for dim, c, s_, rows in ((2 * DH // 2, "cos_d", "sin_d", None), (ROPE, "cos_a", "sin_a", 64)):
        n = dim // 4
        inv = (np.float32(ROPE_BASE) ** (-np.arange(n, dtype=np.float32) / np.float32(n))).astype(np.float32)
        ang = np.concatenate([row[:, None] * inv, colm[:, None] * inv], -1).astype(np.float32)
        cos, sin = np.cos(ang).T, np.sin(ang).T
        if rows is None:
            con[:, CON[c][0]:CON[c][1]] = np.concatenate([cos] * 4)
            con[:, CON[s_][0]:CON[s_][1]] = np.concatenate([sin, -sin] * 2)
        else:
            con[rows:rows + 32, CON[c][0]:CON[c][1]] = np.concatenate([cos] * 2)
            con[rows:rows + 32, CON[s_][0]:CON[s_][1]] = np.concatenate([-sin, sin])
    r = np.zeros((128, NRC), np.float32)
    r[:, 0:128] = np.triu(np.ones((128, 128)), 1)
    for n_, v in (("desc4", np.arange(NG, 0, -1)), ("desc32", np.arange(NE, 0, -1)), ("expert", np.arange(NE)),
                  ("nth", np.arange(OVER))):
        r[:, RCON[n_][0]:RCON[n_][1]] = v
    r[:, RCON["token"][0]:RCON["token"][1]] = np.arange(128)[:, None] + 128 * np.arange(4)
    return con, r


def kernel(x, c, ctx, c_ctx, w_ada, b_ada, norm1_g, w_in, q_norm_g, w_uq, kv_norm_g, w_ukv, conv_w, conv_b,
           conv_ln_g, conv_ln_b, lam_q1, lam_k1, lam_q2, lam_k2, diff_subln_g, w_o_mla, w_o_conv, w_o_diff, w_out,
           norm2_g, w_rg, b_rg, w_re, b_re, w_gate, w_up, w_down, final_g):
    import concourse.bacc as bacc
    from concourse.bass_utils import run_bass_kernel_spmd as run

    L = DEPTH
    A = np.asarray

    def rows(w, k):
        w = A(w)
        return w.reshape(L, k, 128, w.shape[-1]).transpose(0, 2, 1, 3)

    def flat(w, lead):
        w = np.ascontiguousarray(w)
        return w.reshape(w.shape[:lead] + (-1,))

    def part(v):
        v = A(v)
        return v.reshape(L, -1, 128).transpose(0, 2, 1)

    def alike(v):
        v = A(v)
        return np.broadcast_to(v[:, None, :], (L, 128, v.shape[-1]))

    win = rows(w_in, KD)
    o_glu, o_q = LW, LW + 2 * CC
    o_k, o_v, o_g = o_q + HD * 2 * DH, o_q + 2 * HD * 2 * DH, o_q + 3 * HD * 2 * DH
    glu = win[..., o_glu:o_q].reshape(L, 128, KD, 2, 2, 2, 128)
    gates = win[..., o_g:].reshape(L, 128, KD, 3, KD, 128)
    wo = np.concatenate([rows(w, 4) for w in (w_o_mla, w_o_conv, w_o_diff)], 2).reshape(L, 128, 12, KD, 128)
    con, rcon = tables()
    vecs = np.concatenate([part(norm1_g), part(norm2_g), part(b_ada), part(q_norm_g), part(kv_norm_g),
                           A(conv_w).reshape(L, CW, CT, 128).transpose(0, 3, 2, 1).reshape(L, 128, CT * CW),
                           part(conv_b), part(conv_ln_g), part(conv_ln_b), part(diff_subln_g),
                           alike(lam_q1), alike(lam_k1), alike(lam_q2), alike(lam_k2), alike(b_rg), alike(b_re)], 2)
    arrays = {
        "cvec": np.stack([A(c)[0], A(c_ctx)], 1).reshape(KD, 128, 2).transpose(1, 0, 2).reshape(128, 2 * KD),
        "vecs": vecs.transpose(1, 0, 2),
        "con": con, "rcon": rcon,
        "final_g": A(final_g).reshape(KD, 128).T,
        "x": np.concatenate([A(ctx)[0], A(x)[0]], 0).T.reshape(KD, 128, T).transpose(1, 0, 2),
        "router": np.concatenate([rows(w_rg, KD), rows(w_re, KD)], 3),
        "ada": flat(rows(w_ada, KD).reshape(L, 128, KD, NADA, 512).transpose(0, 3, 1, 2, 4), 3),
        "lora": flat(win[:, None, :, :, 0:LW], 3),
        "glu": flat(glu.transpose(0, 4, 1, 2, 5, 3, 6), 3),
        "dq": flat(win[:, None, :, :, o_q:o_k], 3),
        "dk": flat(win[:, None, :, :, o_k:o_v], 3),
        "dv": flat(win[:, None, :, :, o_v:o_g], 3),
        "ukv": np.concatenate([flat(rows(w_uq, 2), 2), A(w_ukv)], 2)[:, None],
        "merge": np.concatenate([flat(gates.transpose(0, 4, 1, 2, 3, 5), 3), flat(wo.transpose(0, 3, 1, 2, 4), 3)], 3),
        "out_w": flat(rows(w_out, KD).reshape(L, 128, KD, 2, 512).transpose(0, 3, 1, 2, 4), 3),
        "w_gate": A(w_gate).reshape(L, NE, KD, 128, FF).transpose(0, 1, 3, 2, 4).reshape(L, NE, 128, KD * FF),
        "w_up": A(w_up).reshape(L, NE, KD, 128, FF).transpose(0, 1, 3, 2, 4).reshape(L, NE, 128, KD * FF),
        "w_down": A(w_down).reshape(L, NE, 2, 128, D).transpose(0, 1, 3, 2, 4).reshape(L, NE, 128, 2 * D),
    }
    nc = bacc.Bacc("TRN2", target_bir_lowering=False, num_devices=1)
    aps, given = {}, {}
    for name, v in arrays.items():
        v = np.ascontiguousarray(v)
        given[f"{name}_in"] = v
        aps[name] = nc.dram_tensor(f"{name}_in", v.shape, mybir.dt.float32, kind="ExternalInput").ap()
    out = nc.dram_tensor("result", (D, SEQ), mybir.dt.float32, kind="ExternalOutput").ap()
    build(nc, dict(aps, out=out))
    r = run(nc, [given], core_ids=[0])
    return np.ascontiguousarray(r.results[0]["result"].T).reshape(1, SEQ, D)
```

```python
import math
from contextlib import ExitStack

import numpy as np
import concourse.bass as bass
from concourse import mybir

D = 1024
KD = D // 128
SEQ, CTX = 256, 256
T = CTX + SEQ
DEPTH = 2
GRID_W = 64
ROPE_BASE = 10000.0
EPS = 1e-6
HA, NOPE, ROPE, VA = 8, 64, 32, 64
QL, KVL = 256, 128
CC, CW = 512, 31
HD, DH = 4, 64
NG, EG, FF = 4, 8, 256
NE = NG * EG
CT = CC // 128
PAD = CW // 2
UP = 256 + 2 * PAD
LW = QL + KVL + ROPE
SLOT = 4096
NRING = 3
NADA = 12
OVER = 15
NBLK = 48
SCALE_A = 1.0 / math.sqrt(NOPE + ROPE)
SCALE_D = 1.0 / math.sqrt(DH)
ROUND = 12582912.0

VEC = {}
_at = 0
for _n, _w in (("norm1_g", KD), ("norm2_g", KD), ("b_ada", 48), ("q_g", 2), ("kv_g", 1), ("conv_w", CT * CW),
               ("conv_b", CT), ("ln_g", CT), ("ln_b", CT), ("sub_g", 1), ("lams", 4 * DH), ("b_r", NG + NE)):
    VEC[_n] = (_at, _at + _w)
    _at += _w
NV = _at

CON = {}
_at = 0
for _n, _w in (("ident", 128), ("pick", 2), ("cos_d", SEQ), ("sin_d", SEQ), ("cos_a", SEQ), ("sin_a", SEQ)):
    CON[_n] = (_at, _at + _w)
    _at += _w
NC = _at
RCON = {}
_at = 0
for _n, _w in (("tri", 128), ("desc4", NG), ("desc32", NE), ("expert", NE), ("nth", OVER), ("token", 4)):
    RCON[_n] = (_at, _at + _w)
    _at += _w
NRC = _at


def build(nc, a):
    f32, i32 = mybir.dt.float32, mybir.dt.int32
    ALU, ACT, AX = mybir.AluOpType, mybir.ActivationFunctionType, mybir.AxisListType
    MUL, ADD, SUB = ALU.mult, ALU.add, ALU.subtract
    ctx = ExitStack()

    def sb(name, shape, dt=f32):
        return ctx.enter_context(nc.sbuf_tensor(name, shape, dt))

    def sem(name):
        return ctx.enter_context(nc.semaphore(name))

    def grid(ap, n):
        return ap.rearrange("p (n m) -> p n m", n=n)

    with ctx:
        x = grid(sb("x", [128, KD * T])[:, :], KD)
        h = grid(sb("h", [128, KD * T])[:, :], KD)
        arena = sb("arena", [128, 20720])
        ring = grid(sb("ring", [128, NRING * SLOT])[:, :], NRING)
        qa = grid(arena[:, 0:4096], HA)
        oa = grid(arena[:, 0:4096], HA)[:, 0:8:2, :]
        va = grid(arena[:, 4096:6144], 4)
        qd = grid(arena[:, 6144:8192], HD)
        kd = grid(arena[:, 8192:10240], HD)
        vd = grid(arena[:, 10240:12288], 4)
        ka = grid(arena[:, 12288:16384], HA)
        gt8 = grid(arena[:, 12288:16384], KD)
        up = arena[:, 16384:16384 + CT * 2 * UP].rearrange("p (c s u) -> p c s u", c=CT, s=2)
        cv = grid(arena[:, 18672:20720], CT)
        lora = grid(sb("lora", [128, 4 * T])[:, :], 4)
        yt_more = grid(sb("yt_more", [128, 3 * T])[:, :], 3)
        yt = [arena[:, 16384 + T * c:16384 + T * c + T] for c in range(4)] + [yt_more[:, c] for c in range(3)] + [lora[:, 3]]
        P = grid(sb("P", [128, 4 * 512])[:, :], 4)
        PT = grid(sb("PT", [128, 2 * 512])[:, :], 2)
        con = sb("con", [128, NC])
        vec = grid(sb("vec", [128, 2 * NV])[:, :], 2)
        ones = sb("ones", [128, 128])
        fing = sb("fing", [128, KD])
        silc = sb("silc", [128, 2 * KD * 2])
        silz = sb("silz", [128, KD * 32])[:, :]
        ada = [grid(sb(f"ada{l}", [128, 96])[:, :], 48) for l in range(2)]
        mod = [grid(sb(f"mod{l}", [128, 3 * KD * 2])[:, :], 3 * KD) for l in range(2)]
        st = sb("st", [128, 64])
        am = sb("am", [128, 96])
        small = sb("small", [128, 16])
        wr = grid(sb("wr", [128, KD * (NG + NE)])[:, :], KD)
        wd = grid(arena[:, 0:8192], 4)
        yg = grid(arena[:, 0:8192], 8)
        gu = [ring[:, 0, 0:4096], ring[:, 1, 0:4096], ring[:, 2, 0:4096], arena[:, 8192:12288]]
        m0 = 12288
        xg = grid(arena[:, m0:m0 + 2048], 2)
        yy = grid(arena[:, m0 + 2048:m0 + 4096], 2)
        stage = grid(arena[:, m0:m0 + 4096], 4)
        xgt = grid(arena[:, m0 + 4096:m0 + 5120], 2)
        gt = grid(arena[:, m0 + 5120:m0 + 5632], 2)
        hid = grid(arena[:, m0 + 5632:m0 + 6144], 2)
        hidt = grid(arena[:, m0 + 6144:m0 + 6400], 2)
        rt = sb("routing", [128, 1824])[:, :]
        rat = [0]

        def rtile(n, dt=f32):
            rat[0] += n
            assert rat[0] <= 1824, rat[0]
            t = rt[:, rat[0] - n:rat[0]]
            return t if dt == f32 else t.bitcast(dt)

        rcon = rtile(NRC)
        lg = grid(rtile(4 * 36), 4)
        g4 = [grid(rtile(16), 4) for _ in range(3)]
        bigs = rtile(8 * 128)
        big = [grid(bigs[:, 128 * n_:128 * n_ + 128], 4) for n_ in range(8)]
        col = [rtile(4) for _ in range(10)]
        c32 = [rtile(32) for _ in range(6)]
        cmp15 = grid(bigs[:, 0:OVER * NE], OVER)
        ov15 = rtile(16)
        icol = rtile(4, i32)
        sl = grid(rtile(8, i32), 2)
        tok = rtile(4, i32)
        meta = [rtile(16, i32) for _ in range(2)]
        idx = rtile(NBLK, i32)
        zero = rtile(NBLK, i32)

        PS = [ctx.enter_context(nc.psum_tensor(f"bank{i}", [128, 512], f32)) for i in range(8)]
        BANK = {"a": PS[0], "d": PS[1]}

        CAP = [T // 8, SEQ // 8]
        h2d = [nc.dram_tensor(f"h2_{l}", [8 * CAP[l], D], f32).ap() for l in range(2)]
        yd = [nc.dram_tensor(f"y_{l}", [CAP[l] * NBLK, D], f32).ap() for l in range(2)]
        td = [nc.dram_tensor(f"tok_{l}", [CAP[l] * NBLK, 1], i32).ap() for l in range(2)]

        full = {"a": sem("act_tile_full"), "d": sem("dve_tile_full")}
        empty = {"a": sem("act_tile_empty"), "d": sem("dve_tile_empty")}
        number = {"a": {}, "d": {}}
        ring_ready = [sem(f"ring_ready{s}") for s in range(NRING)]
        unit_end = {}
        loaded = sem("inputs_loaded")
        x_loaded, router_loaded, table_zero = sem("x_loaded"), sem("router_loaded"), sem("table_zero")
        hid_half, zeroed = sem("hid_half"), sem("zeroed")
        y_zeroed = sem("y_zeroed")
        passed = sem("waits_passed")
        lam_sums, lam_exps = sem("lam_sums"), sem("lam_exps")
        consts_set = sem("consts_set")
        silc_tanh, silc_ready = sem("silc_tanh"), sem("silc_ready")
        dve_step, pool_step = sem("dve_step"), sem("pool_step")
        out_ready, out_stored = sem("out_ready"), sem("out_stored")
        NAMES = ["sq_ready", "stat_ready", "recip_ready", "modded", "shifted",
                 "conv_v", "conv_sq", "conv_scaled", "conv_act", "conv_out",
                 "rope_part", "rope_pool", "kr_ready", "pool_set", "scores", "scores_max", "exp_ready",
                 "probs_ready", "pt_full", "pt_ready", "pv_full", "attn_out", "merge_part", "yt_ready", "g1_ready", "out_part",
                 "h2_stored", "gexp_in", "gexp", "mask_ready", "slots_ready", "tokens_moved", "icol_ready",
                 "xg_ready0", "xg_ready1", "xgt_full", "xgt_ready", "gu_ready0", "gu_ready1", "gu_ready2", "gu_ready3",
                 "wd_ready0", "wd_ready1", "wd_ready2", "wd_ready3", "gu_full", "gtanh", "hid_ready", "ht_full", "hidt_ready", "ssq",
                 "y_full", "y_act", "y_stored0", "y_stored1", "yg_ready0", "yg_ready1", "weights_ready",
                 "ov_w", "ov_icol", "ov_xg", "ov_pe", "ov_act", "ov_dve", "ov_stored"]
        S = [{n: sem(f"{n}_{l}") for n in NAMES} for l in range(DEPTH)]

        rstd = PT[:, 0, :]

        def sqt(k):
            return P[:, 3, :] if k == 0 else (lora[:, 0, :], lora[:, 1, :], P[:, 2, :])[k % 3]

        def dprob(u):
            return P[:, 2 * (u % 2):2 * (u % 2) + 2, :]

        def attn_units(l):
            tiles = range(0 if l == 0 else 2, 4)
            seen = [CTX if t < CTX // 128 else T for t in range(4)]
            return ([(i, t, seen[t]) for i in range(HA) for t in tiles],
                    [(i, t, seen[t]) for i in range(HD) for t in tiles])

        GATES, ALL = KD * KD, KD * KD + 4 * KD

        MERGE = (1, 0, 2)

        def merge_range(l, g):
            if l == 0:
                n = [3, 3, 2] * 8 + [4] * 8 + [8] * 8 + [4] * 8
            else:
                n = [4] * 14 + [8, 12, 20] + [16] * 4 + [12, 12, 8]
            return sum(n[:g]), sum(n[:g + 1])

        def merge_done(l, r0, r1):
            done = []
            for r_ in range(r0, r1):
                b, r = divmod(r_, ALL)
                if r < GATES and r % KD == KD - 1:
                    done.append(("gate", b, r // KD))
                if r >= GATES and r % 4 == 3:
                    done.append(("branch", b, (r - GATES) // 4))
                for at, unit_, after in ((GATES // 2, "mg", 0), (GATES, "mg", 1), (ALL, "mo", 0)):
                    if r == at - 1:
                        done.append(("ada", 0, (f"mg{2 * b + after}" if unit_ == "mg" else f"mo{b}", l, 0)))
                    if (r_ - KD) % ALL == at - 1 and r_ >= KD:
                        b_ = (r_ - KD) // ALL
                        done.append(("adaT", 0, (f"mg{2 * b_ + after}" if unit_ == "mg" else f"mo{b_}", l, 0)))
            return done

        def wait_apart(eng, sm, value):
            eng.wait_ge(sm, value)
            eng.sem_inc(passed, 1)

        def con_at(n):
            return con[:, CON[n][0]:CON[n][1]]

        def vec_at(l, n):
            return vec[:, l, VEC[n][0]:VEC[n][1]]

        def rcon_at(n):
            return rcon[:, RCON[n][0]:RCON[n][1]]

        ident = con_at("ident")

        units = [("ada", 0, u) for u in range(4)]
        more = [("ada", 0, u) for u in range(4, NADA)] + [("ada", 1, u) for u in range(NADA)]
        for l in range(DEPTH):
            for kind, n in (("lora", 1), ("glu", 2), ("dq", 1), ("ukv", 1), ("dk", 1), ("dv", 1), ("mg0", 1), ("mg1", 1), ("mo0", 1), ("mg2", 1),
                            ("mg3", 1), ("mo1", 1), ("mg4", 1), ("mo2", 1), ("mg5", 1), ("out", 2)):
                for i in range(n):
                    units.append((kind, l, i))
                    if kind not in ("mg0", "mg1", "mg4", "mo2"):
                        units += more[:1]
                        del more[:1]
        assert not more
        unit_no = {u: i for i, u in enumerate(units)}
        first_of_layer1 = unit_no[("lora", 1, 0)]

        def ada_behind(key):
            n = 0 if key is None else unit_no[key] + 1
            out_ = []
            while n < len(units) and units[n][0] == "ada":
                out_.append(n)
                n += 1
            return out_

        def ada_tmp(n):
            before = [k_[0] for k_ in units[:n] if k_[0] != "ada"]
            if not before or before[-1] in ("lora", "glu"):
                return ka[:, n % 4, :]
            return PT[:, 1, :] if before[-1] in ("dq", "ukv", "dk", "dv") else lora[:, 2, :]

        block = ctx.enter_context(nc.Block())

        @block.tensor
        def _(pe):
            made = {}

            def begin(b, name):
                n = len(number[b]) + 1
                made["a"], made["d"] = int(b == "a"), int(b == "d")
                assert (name not in number[b])
                number[b][name] = n
                if n > 1:
                    pe.wait_ge(empty[b], n - 1)
                return BANK[b]

            def end(b, ins):
                ins.then_inc(full[b], 1)

            def unit(key):
                n = unit_no[key]
                pe.wait_ge(ring_ready[n % NRING], 16 * (n // NRING + 1))
                return ring[:, n % NRING, :]

            def mm(out, w, rhs, start, stop):
                return nc.tensor.matmul(out, w, rhs, start=start, stop=stop)

            def ada_units(after):
                for n in ada_behind(after):
                    ada_unit(units[n])

            def ada_unit(key):
                _, la, u = key
                w = grid(unit(key)[:, 0:4096], KD)
                ps = begin("d", ("ada", la, u))
                for k in range(KD):
                    g = 32 * (k % 4)
                    last = mm(ps[g:g + 32, :], silz[:, 32 * k:32 * k + 32], w[:, k, :], k < 4, k >= 4)
                end("d", last)
                used(key)

            def ada_finish(key):
                for n in ada_behind(key):
                    _, la, u = units[n]
                    ps = begin("d", ("adaT", la, u))
                    pe.wait_ge(empty["d"], number["d"][("ada", la, u)])
                    for m in range(4):
                        last = mm(ps[:, 2 * m:2 * m + 2], ada_tmp(n)[:, 128 * m:128 * m + 128],
                                  con_at("pick")[:, 0:2], True, True)
                    end("d", last)

            def used(key, b=None):
                b = b or max("ad", key=lambda n_: made[n_])
                unit_end[key] = (b, len(number[b]))

            def column_tile(b, name, w, q0, cols=128, kk=KD, src=None):
                ps = begin(b, name)
                for k in range(kk):
                    rhs = src[k][:, q0:T] if isinstance(src, list) else src[:, k, q0:T]
                    last = mm(ps[0:cols, 0:T - q0], w(k), rhs, k == 0, k == kk - 1)
                end(b, last)

            def row_stats(name, parts):
                ps = begin("a", name)
                for c, (src, t) in enumerate(parts):
                    for j, s_ in enumerate(src):
                        last = mm(ps[:, c:c + 1], s_[:, t * 128:t * 128 + 128], ones[:, 0:1],
                                  j == 0, j == len(src) - 1)
                end("a", last)

            def spread(name, cols, q0=0):
                ps = begin("d", name)
                for t, c in cols:
                    last = mm(ps[:, t * 128:t * 128 + 128], st[:, c:c + 1].to_broadcast([128, 128]), ident, True, True)
                end("d", last)

            def norm_sums(l, which, t0, n, early):
                s = S[l]
                ps = begin("a", (which, l))
                order = [4, 5, 6, 7] if early else [5, 6, 7, 4]
                for k in order:
                    if k == 4:
                        pe.wait_ge(s["ssq"], 4 * (n + 1))
                    else:
                        pe.wait_ge(s["sq_ready"], n * KD + k + 1)
                    src = P[:, 3] if k == 4 else sqt(k)
                    last = mm(ps[:, t0 * 128:T], ones[:, :], src[:, t0 * 128:T], k == order[0], k == order[-1])
                end("a", last)

            pe.wait_ge(loaded, 16 * 5)
            pe.wait_ge(consts_set, 2)
            pe.wait_ge(silc_ready, 1)
            for n in ada_behind(None):
                ada_unit(units[n])
            ada_finish(None)

            for l in range(DEPTH):
                s = S[l]
                q0 = 0 if l == 0 else CTX
                qt0 = q0 // 128
                norm_sums(l, "n1", 0, 0, False)
                pe.wait_ge(s["shifted"], 2 * KD)
                w = grid(unit(("lora", l, 0))[:, 0:KD * LW], KD)
                for i, (b, c0, cols, qq) in enumerate((("a", 0, 128, q0), ("d", 128, 128, q0),
                                                      ("a", 256, 128, 0), ("d", 384, 32, 0))):
                    column_tile(b, ("lora", l, i), lambda k: w[:, k, c0:c0 + cols], qq, cols, KD, h)
                used(("lora", l, 0))
                ada_units(("lora", l, 0))
                for j in range(2):
                    w = unit(("glu", l, j))[:, 0:4096].rearrange("p (k n m) -> p k n m", k=KD, n=4)
                    for i in range(2):
                        column_tile("a", ("gluG", l, 2 * j + i), lambda k: w[:, k, 2 * i + 1, :], q0, 128, KD, h)
                        if i == 0:
                            ada_finish(("glu", l, 0) if j else ("lora", l, 0))
                        column_tile("d", ("gluA", l, 2 * j + i), lambda k: w[:, k, 2 * i, :], q0, 128, KD, h)
                    used(("glu", l, j))
                    ada_units(("glu", l, j))
                    if j == 0:
                        pe.wait_ge(s["stat_ready"], 1)
                        row_stats(("loraS", l), [([P[:, 0], P[:, 1]], t) for t in range(qt0, 4)]
                                  + [([P[:, 2]], t) for t in range(4)])
                pe.wait_ge(s["recip_ready"], 2)
                spread(("loraQ", l), [(t, 8 + t - qt0) for t in range(qt0, 4)])
                spread(("loraK", l), [(t, 8 + 4 - qt0 + t) for t in range(4)])
                w = grid(unit(("dq", l, 0))[:, 0:4096], KD)
                for i in range(HD):
                    column_tile("ad"[i % 2], ("dq", l, i), lambda k: w[:, k, 128 * i:128 * i + 128], q0, 128, KD, h)
                    if i == 0:
                        ada_finish(("glu", l, 1))
                used(("dq", l, 0))
                ada_units(("dq", l, 0))
                pe.wait_ge(empty["d"], number["d"][("loraK", l)])
                w = unit(("ukv", l, 0))
                wq, wkv = grid(w[:, 0:1536], 2), w[:, 1536:2560]
                for i in range(HA):
                    column_tile("ad"[i % 2], ("uq", l, i), lambda k: wq[:, k, 96 * i:96 * i + 96], q0, 96, 2, lora)
                    if i == 0:
                        ada_finish(("dq", l, 0))
                for i in range(HA):
                    column_tile("ad"[i % 2], ("uk", l, i), lambda k: wkv[:, 128 * i:128 * i + 64], 0, 64, 1, lora[:, 2:3])
                for t in range(4):
                    b = "ad"[t % 2]
                    ps = begin(b, ("uv", l, t))
                    end(b, mm(ps[:, :], lora[:, 2, t * 128:t * 128 + 128],
                              wkv.rearrange("p (h n) -> p h n", h=HA)[:, :, NOPE:], True, True))
                used(("ukv", l, 0))
                ada_units(("ukv", l, 0))
                w = grid(unit(("dk", l, 0))[:, 0:4096], KD)
                for i in range(HD):
                    column_tile("ad"[i % 2], ("dk", l, i), lambda k: w[:, k, 128 * i:128 * i + 128], 0, 128, KD, h)
                    if i == 0:
                        ada_finish(("ukv", l, 0))
                used(("dk", l, 0))
                ada_units(("dk", l, 0))
                w = grid(unit(("dv", l, 0))[:, 0:4096], KD)
                for t in range(4):
                    b = "ad"[t % 2]
                    ps = begin(b, ("dv", l, t))
                    for k in range(KD):
                        last = mm(ps[:, :], h[:, k, t * 128:t * 128 + 128], w[:, k, :], k == 0, k == KD - 1)
                    end(b, last)
                    if t == 0:
                        ada_finish(("dk", l, 0))
                used(("dv", l, 0))
                ada_units(("dv", l, 0))
                ada_finish(("dv", l, 0))
                def conv_norm(u):
                    if u == 0:
                        pe.wait_ge(s["conv_v"], 1)
                        row_stats(("lnM", l), [([cv[:, c] for c in range(CT)], t) for t in range(qt0, 4)])
                    elif u == 2:
                        pe.wait_ge(empty["a"], number["a"][("lnM", l)])
                        spread(("lnMb", l), [(t, 16 + t - qt0) for t in range(qt0, 4)])
                    elif u == 8 + l:
                        pe.wait_ge(s["conv_sq"], CT)
                        row_stats(("lnV", l), [([lora[:, c] for c in range(CT)], t) for t in range(qt0, 4)])
                    elif u == 10 + l:
                        pe.wait_ge(s["recip_ready"], 3)
                        spread(("lnVb", l), [(t, 24 + t - qt0) for t in range(qt0, 4)])

                def gate_step(b, c, k):
                    if c % 4 == 0 and k == 0:
                        unit((f"mg{2 * b + c // 4}", l, 0))
                    if k == 0:
                        begin("a", ("gate", l, c, b))
                    w = ring[:, unit_no[(f"mg{2 * b + c // 4}", l, 0)] % NRING, :].rearrange("p (c k m) -> p c k m", c=4, k=KD)
                    ins = mm(PS[0][:, 0:T - q0], w[:, c % 4, k, :], h[:, k, q0:T], k == 0, k == KD - 1)
                    if k == KD - 1:
                        end("a", ins)
                        if c % 4 == 3:
                            used((f"mg{2 * b + c // 4}", l, 0), "a")

                def branch_step(b, c, k):
                    if c == 0 and k == 0:
                        unit((f"mo{b}", l, 0))
                        if b == 0:
                            pe.wait_ge(s["conv_out"], CT)
                        elif b == 1:
                            pe.wait_ge(s["attn_out"], len(AU))
                    if k == 0:
                        begin("d", ("branch", l, c, b))
                    w = ring[:, unit_no[(f"mo{b}", l, 0)] % NRING, :].rearrange("p (c k m) -> p c k m", c=KD, k=4)
                    ins = mm(PS[1][:, 0:T - q0], w[:, c, k, :], (oa, cv, qd)[MERGE[b]][:, k, q0:T], k == 0, k == 3)
                    if k == 3:
                        end("d", ins)
                        if c == KD - 1:
                            used((f"mo{b}", l, 0), "d")

                def merge_steps(g):
                    for r_ in range(*merge_range(l, g)):
                        b, r = divmod(r_, ALL)
                        if r < GATES:
                            gate_step(b, r // KD, r % KD)
                        else:
                            branch_step(b, (r - GATES) // 4, r % 4)
                        for what, _, key in merge_done(l, r_, r_ + 1):
                            if what == "ada":
                                ada_units(key)
                            elif what == "adaT":
                                ada_finish(key)

                AU, DU = attn_units(l)
                n_all = len(AU) + len(DU)
                for b in "ad":
                    pe.wait_ge(empty[b], len(number[b]))
                pe.wait_ge(s["rope_pool"], 3)
                pe.wait_ge(s["pool_set"], 2)

                def scores_a(u):
                    i, t, nk = AU[u]
                    if u >= 4:
                        pe.wait_ge(s["exp_ready"], u - 3)
                    mm(PS[2 + u % 4][:, 0:nk], qa[0:96, i, t * 128:t * 128 + 128], ka[0:96, i, 0:nk], True, True) \
                        .then_inc(s["scores"], 1)

                def scores_d(u):
                    i, t, nk = DU[u]
                    g = len(AU) + 2 * u
                    pe.wait_ge(s["exp_ready"], len(AU) if u < 2 else g - 2)
                    for m in range(2):
                        mm(PS[2 + 2 * (u % 2) + m][:, 0:nk], qd[64 * m:64 * m + 64, i, t * 128:t * 128 + 128],
                           kd[64 * m:64 * m + 64, i, 0:nk], True, True).then_inc(s["scores"], 1)

                def turn(g, src, nk):
                    pe.wait_ge(s["probs_ready"], g + 1)
                    if g >= 1:
                        pe.wait_ge(s["pt_ready"], g)
                    for kt in range(nk // 128):
                        last = nc.tensor.transpose(PS[6][:, kt * 128:kt * 128 + 128],
                                                   src[:, kt * 128:kt * 128 + 128], ident)
                    last.then_inc(s["pt_full"], 1)

                def values(g, lhs, out, nk):
                    pe.wait_ge(s["pt_ready"], g + 1)
                    if g >= 1:
                        pe.wait_ge(s["attn_out"], g)
                    for kt in range(nk // 128):
                        last = mm(out, lhs(kt), PT[:, g % 2, kt * 128:kt * 128 + 128], kt == 0, kt == nk // 128 - 1)
                    last.then_inc(s["pv_full"], 1)

                def values_a(u):
                    i, t, nk = AU[u]
                    r = 64 * (i % 2)
                    values(u, lambda kt: va[:, kt, 64 * i:64 * i + 64], PS[7][r:r + 64, 0:128], nk)

                def values_d(u):
                    i, t, nk = DU[u]
                    values(len(AU) + u, lambda kt: vd[:, kt, 128 * i:128 * i + 128], PS[7][:, 0:128], nk)

                scores_a(0)
                scores_a(1)
                conv_norm(0)
                for u in range(len(AU)):
                    turn(u, P[:, u % 4], AU[u][2])
                    if u + 2 < len(AU):
                        scores_a(u + 2)
                    if u >= 1:
                        values_a(u - 1)
                    merge_steps(u)
                    if u:
                        conv_norm(u)
                scores_d(0)
                scores_d(1)
                values_a(len(AU) - 1)
                for u in range(len(DU)):
                    turn(len(AU) + u, dprob(u)[:, 0], DU[u][2])
                    if u + 2 < len(DU):
                        scores_d(u + 2)
                    if u >= 1:
                        values_d(u - 1)
                    merge_steps(len(AU) + u)
                values_d(len(DU) - 1)
                for k in range(KD):
                    gate_step(2, 0, k)
                pe.wait_ge(s["stat_ready"], 1 + HD)
                row_stats(("dn", l), [([P[:, i]], t) for i in range(HD) for t in range(qt0, 4)])
                for k in range(KD):
                    gate_step(2, 1, k)
                pe.wait_ge(s["recip_ready"], 4)
                for i in range(HD):
                    spread(("dnb", l, i), [(t, 32 + i * (4 - qt0) + t - qt0) for t in range(qt0, 4)])
                ada_finish(("mo1", l, 0))
                pe.wait_ge(empty["d"], number["d"][("dnb", l, HD - 1)])
                for c in range(KD):
                    if c >= 2:
                        for k in range(KD):
                            gate_step(2, c, k)
                    for k in range(4):
                        branch_step(2, c, k)
                ada_units(("mg5", l, 0))
                pe.wait_ge(s["yt_ready"], KD)
                for c in range(KD):
                    if c % 4 == 0:
                        w = unit(("out", l, c // 4))[:, 0:4096].rearrange("p (k n m) -> p k n m", k=KD, n=4)
                    column_tile("ad"[c % 2], ("out", l, c), lambda k: w[:, k, c % 4, :], q0, 128, KD, yt)
                    if c % 4 == 0:
                        ada_finish(("mg5", l, 0) if c == 0 else ("out", l, 0))
                    if c % 4 == 3:
                        used(("out", l, c // 4))
                        ada_units(("out", l, c // 4))
                ada_finish(("out", l, 1))
                norm_sums(l, "n2", qt0, 1, True)
                pe.wait_ge(router_loaded, 16 * (l + 1))
                ps = begin("d", ("router", l))
                for k in range(KD):
                    pe.wait_ge(s["shifted"], 2 * KD + (2 if l == 0 else 1) * (k + 1))
                    for t in range(qt0, 4):
                        last = mm(ps[:, (t - qt0) * 36:(t - qt0) * 36 + 36], h[:, k, t * 128:t * 128 + 128],
                                  wr[:, k, :], (k, t) == (0, qt0), (k, t) == (KD - 1, 3))
                end("d", last)
                def h2_turn(tiles):
                    for t in tiles:
                        for half in range(2):
                            ps = begin("a", ("h2", l, t, half))
                            for k in range(4):
                                last = nc.tensor.transpose(ps[:, k * 128:k * 128 + 128],
                                                           h[:, 4 * half + k, t * 128:t * 128 + 128], ident)
                            end("a", last)

                h2_turn(range(qt0, qt0 + 2))
                TT = 4 - qt0
                pe.wait_ge(s["mask_ready"], 1)
                ps = begin("d", ("rank", l))
                for j in range(TT):
                    for t in range(j, TT + 1):
                        last = mm(ps[:, t * 32:t * 32 + 32], ones[:, :] if j < t else rcon_at("tri"), big[4][:, j, :],
                                  j == t == 0, (j, t) == (TT - 1, TT))
                end("d", last)
                h2_turn(range(qt0 + 2, 4))

                C = (T - q0) // 8

                def gather_turn(par, full_sem):
                    for k in range(KD):
                        last = nc.tensor.transpose(PS[2 + par][:, k * C:k * C + C], xg[0:C, par, k * 128:k * 128 + 128],
                                                   ident[0:C, 0:C])
                    last.then_inc(full_sem, 1)

                def up_products(par, slot, full_sem):
                    w = slot.rearrange("p (g k m) -> p g k m", g=2, k=KD)
                    for k in range(KD):
                        for g in range(2):
                            last = mm(PS[4 + par][64 * g:64 * g + C, 0:FF], xgt[:, par, k * C:k * C + C], w[:, g, k, :],
                                      k == 0, k == KD - 1)
                    last.then_inc(full_sem, 1)

                def hidden_turn(par, full_sem):
                    for k in range(2):
                        last = nc.tensor.transpose(PS[0][:, k * C:k * C + C], hid[0:C, par, k * 128:k * 128 + 128],
                                                   ident[0:C, 0:C])
                    last.then_inc(full_sem, 1)

                def down_products(par, slot, full_sem):
                    w = grid(slot, 2)
                    for k in range(2):
                        for n in range(2):
                            last = mm(PS[6 + par][64 * n:64 * n + C, :], hidt[:, par, k * C:k * C + C],
                                      w[:, k, n * 512:n * 512 + 512], k == 0, k == 1)
                    last.then_inc(full_sem, 1)

                def do_turn(j, i):
                    wait_apart(pe, s[f"xg_ready{j % 2}"], i * 32 + 16 * (j // 2 + 1))
                    if not (isinstance(i, int) and 4 * i + j < 2):
                        wait_apart(pe, s["xgt_ready"], i * 4 + j - 1)
                    gather_turn(j % 2, s["xgt_full"])

                def do_up(j, i):
                    pe.wait_ge(s[f"gu_ready{j}"], i * 32 + 32)
                    pe.wait_ge(s["xgt_ready"], i * 4 + j + 1)
                    if not (isinstance(i, int) and 4 * i + j < 2):
                        pe.wait_ge(s["hid_ready"], i * 4 + j - 1)
                    up_products(j % 2, gu[j], s["gu_full"])

                def do_hidden(j, i):
                    wait_apart(pe, s["hid_ready"], i * 4 + j + 1)
                    if not (isinstance(i, int) and 4 * i + j < 1):
                        wait_apart(pe, s["hidt_ready"], i * 4 + j)
                    hidden_turn(j % 2, s["ht_full"])

                def do_down(j, i):
                    pe.wait_ge(s[f"wd_ready{j}"], i * 16 + 16)
                    pe.wait_ge(s["hidt_ready"], i * 4 + j + 1)
                    if not (isinstance(i, int) and 4 * i + j < 2):
                        pe.wait_ge(s["y_act"], i * 4 + j - 1)
                    down_products(j % 2, wd[:, j, :], s["y_full"])

                def group(i, first, last):
                    for j in range(4):
                        do_up(j, i)
                        if not (last and j == 3):
                            jn, inn = (j + 1, i) if j < 3 else (0, i + 1)
                            do_turn(jn, inn)
                        if not (first and j == 0):
                            jp, ip = (j - 1, i) if j > 0 else (3, i - 1)
                            do_down(jp, ip)
                        do_hidden(j, i)

                do_turn(0, 0)
                group(0, True, False)
                with pe.Fori(1, NE // 4 - 1) as i:
                    group(i, False, False)
                group(NE // 4 - 1, False, True)
                do_down(3, NE // 4 - 1)
                nx = pe.value_load(meta[l][0:1, 15:16], min_val=0, max_val=OVER)
                with pe.If(nx > 0):
                    pe.wait_ge(s["y_act"], NE)
                    def extra(j):
                        wait_apart(pe, s["ov_xg"], 16 * j + 16)
                        gather_turn(0, s["ov_pe"])
                        pe.wait_ge(s["ov_w"], 48 * j + 48)
                        pe.wait_ge(s["ov_act"], 3 * j + 1)
                        up_products(0, gu[0], s["ov_pe"])
                        wait_apart(pe, s["ov_dve"], 3 * j + 2)
                        hidden_turn(0, s["ov_pe"])
                        pe.wait_ge(s["ov_dve"], 3 * j + 3)
                        down_products(0, wd[:, 0, :], s["ov_pe"])

                    extra(0)
                    with pe.If(nx > 1):
                        with pe.Fori(1, OVER) as j:
                            with pe.If(nx > j):
                                extra(j)
                pe.wait_ge(s["weights_ready"], 1)
                for t in range(qt0, 4):
                    pe.wait_ge(s[f"yg_ready{(t - qt0) // (TT // 2)}"], 16 * TT)
                    for half in range(2):
                        ps = begin("d", ("mix", l, t, half))
                        for k in range(4):
                            for m in range(2):
                                n = 2 * (t - qt0) + m
                                c = (4 * half + k) * 128
                                last = mm(ps[:, k * 128:k * 128 + 128], yg[:, n, c:c + 128],
                                          bigs[:, 128 * n:128 * n + 128], m == 0, m == 1)
                        end("d", last)
            s = S[1]
            norm_sums(1, "nf", 2, 2, False)

        @block.scalar
        def _(act):
            A, Dn = number["a"], number["d"]
            own = [0]

            def f(out, in_, fn, **kw):
                return nc.scalar.activation(out, in_, fn, **kw)

            eps = small[:, 0:1]

            def take(key):
                act.wait_ge(full["a"], A[key])

            def give(ins):
                ins.then_inc(empty["a"], 1)

            def square(s, k, t0, seen):
                if k >= 4:
                    act.wait_ge(s["ssq"], seen + k - 3)
                f(sqt(k)[:, t0 * 128:T], x[:, k, t0 * 128:T], ACT.Square).then_inc(s["sq_ready"], 1)

            def root(key, c0, n, scale, psc=0, done=True):
                ins = f(st[:, c0:c0 + n], PS[0][:, psc:psc + n], ACT.Sqrt, scale=scale, bias=eps)
                if done:
                    give(ins)

            def norm_root(key, t0):
                take(key)
                give(f(rstd[:, t0 * 128:T], PS[0][:, t0 * 128:T], ACT.Sqrt, scale=1.0 / D, bias=eps))

            def shifts(s, l, segs, which, base):
                for k in range(KD):
                    act.wait_ge(s["modded"], base + k + 1)
                    for v, t0, t1 in segs:
                        f(h[:, k, t0:t1], h[:, k, t0:t1], ACT.Identity, scale=mod[l][:, which * KD + k, v:v + 1],
                          bias=ada[l][:, 3 * KD * which + k, v:v + 1]).then_inc(s["shifted"], 1)

            BOTH = [(1, 0, CTX), (0, CTX, T)]
            act.wait_ge(loaded, 16 * 5)
            f(silc[:, 0:16], silc[:, 16:32], ACT.Tanh, scale=0.5).then_inc(silc_tanh, 1)
            act.wait_ge(lam_sums, 1)
            f(small[:, 5:9], small[:, 1:5], ACT.Exp).then_inc(lam_exps, 1)
            act.wait_ge(consts_set, 2)
            act.wait_ge(x_loaded, 16)
            for l in range(DEPTH):
                s = S[l]
                q0 = 0 if l == 0 else CTX
                qt0, NQ = q0 // 128, T - q0
                nt = 4 - qt0
                SEGS = BOTH if l == 0 else BOTH[1:]
                if l == 1:
                    act.wait_ge(empty["d"], Dn[("mix", 0, 3, 1)])
                for k in range(KD):
                    square(s, k, 0, 0)
                norm_root(("n1", l), 0)
                shifts(s, l, BOTH, 0, 0)
                for i, p in ((0, 0), (2, 2)):
                    take(("lora", l, i))
                    t0 = q0 if i == 0 else 0
                    f(lora[:, i, t0:T], PS[0][:, 0:T - t0], ACT.Copy)
                    give(f(P[:, p, t0:T], PS[0][:, 0:T - t0], ACT.Square))
                    if i == 0:
                        act.wait_ge(empty["d"], Dn[("lora", l, 1)])
                        f(P[:, 1, q0:T], lora[:, 1, q0:T], ACT.Square)
                f(small[:, 15:16], small[:, 15:16], ACT.Copy).then_inc(s["stat_ready"], 1)
                for j in range(CT):
                    take(("gluG", l, j))
                    if j >= 2:
                        act.wait_ge(empty["d"], Dn[("gluA", l, j - 2)])
                    give(f(PT[:, j % 2, q0:T], PS[0][:, 0:NQ], ACT.Tanh, scale=0.5))
                    if j == 1:
                        take(("loraS", l))
                        root(None, 8, nt, 1.0 / QL, 0, False)
                        root(None, 8 + nt, 4, 1.0 / KVL, nt)
                for i in range(0, HD, 2):
                    take(("dq", l, i))
                    give(f(qd[:, i, q0:T], PS[0][:, 0:NQ], ACT.Copy))
                act.wait_ge(y_zeroed, 16 * DEPTH)
                for i in range(0, HA, 2):
                    take(("uq", l, i))
                    give(f(qa[0:96, i, q0:T], PS[0][0:96, 0:NQ], ACT.Copy))
                for i in range(0, HA, 2):
                    take(("uk", l, i))
                    give(f(ka[0:64, i, :], PS[0][0:64, :], ACT.Copy))
                for t in range(0, 4, 2):
                    take(("uv", l, t))
                    give(f(va[:, t, :], PS[0][:, :], ACT.Copy))
                for i in range(0, HD, 2):
                    take(("dk", l, i))
                    give(f(kd[:, i, :], PS[0][:, :], ACT.Copy))
                for t in range(0, 4, 2):
                    take(("dv", l, t))
                    give(f(vd[:, t, :], PS[0][:, :], ACT.Copy))
                def conv_norm(u):
                    if u == 0:
                        take(("lnM", l))
                        give(f(st[:, 16:16 + nt], PS[0][:, 0:nt], ACT.Copy, scale=1.0 / CC))
                    elif u == 4:
                        act.wait_ge(empty["d"], Dn[("lnMb", l)])
                        for c in range(CT):
                            f(lora[:, c, q0:T], cv[:, c, q0:T], ACT.Square).then_inc(s["conv_sq"], 1)
                    elif u == 8 + l:
                        take(("lnV", l))
                        root(None, 24, nt, 1.0 / CC)
                    elif u == 12:
                        for c in range(CT):
                            if c < CT - 1:
                                act.wait_ge(s["conv_scaled"], c + 1)
                            else:
                                act.wait_ge(empty["d"], Dn[("lnVb", l)])
                            f(cv[:, c, q0:T], cv[:, c, q0:T], ACT.Identity, scale=0.5,
                              bias=vec_at(l, "ln_b")[:, c:c + 1]).then_inc(s["conv_act"], 1)
                            act.wait_ge(s["conv_act"], 2 * c + 1)
                            f(lora[:, c, q0:T], cv[:, c, q0:T], ACT.Tanh).then_inc(s["conv_act"], 1)

                AU, DU = attn_units(l)
                nA = len(AU)

                def exp_a(u):
                    i, t, nk = AU[u]
                    c = 8 * (u % 8)
                    act.wait_ge(s["scores_max"], u + 1)
                    if u >= 4:
                        act.wait_ge(s["pt_full"], u - 3)
                    f(P[:, u % 4, 0:nk], PS[2 + u % 4][:, 0:nk], ACT.Exp, scale=SCALE_A, bias=am[:, c + 2:c + 3],
                      accum_out=am[:, c + 4:c + 5]).then_inc(s["exp_ready"], 1)

                def exp_d(u):
                    i, t, nk = DU[u]
                    c = 8 * ((nA + u) % 8)
                    act.wait_ge(s["scores_max"], nA + u + 1)
                    act.wait_ge(s["pt_full"], nA + max(u - 1, 0))
                    for m in range(2):
                        f(dprob(u)[:, m, 0:nk], PS[2 + 2 * (u % 2) + m][:, 0:nk], ACT.Exp, scale=SCALE_D,
                          bias=am[:, c + 2 + m:c + 3 + m], accum_out=am[:, c + 4 + m:c + 5 + m]) \
                            .then_inc(s["exp_ready"], 1)

                def pt_copy(g, nk):
                    act.wait_ge(s["pt_full"], g + 1)
                    if g >= 2:
                        act.wait_ge(s["pv_full"], g - 1)
                    f(PT[:, g % 2, 0:nk], PS[6][:, 0:nk], ACT.Copy).then_inc(s["pt_ready"], 1)

                def gate(b, c):
                    take(("gate", l, c, b))
                    if b == 0 and c == 0:
                        act.wait_ge(s["conv_v"], 1)
                    if b == 0 and c == KD - 1:
                        act.wait_ge(s["conv_out"], CT)
                    if b == 2:
                        act.wait_ge(s["merge_part"], c + 1)
                    give(f(yt[c][:, q0:T] if b == 0 else gt8[:, c, q0:T], PS[0][:, 0:NQ], ACT.Tanh, scale=0.5))

                def gates(g):
                    for what, b, c in merge_done(l, *merge_range(l, g)):
                        if what == "gate":
                            gate(b, c)

                exp_a(0)
                exp_a(1)
                conv_norm(0)
                for u in range(nA):
                    pt_copy(u, AU[u][2])
                    if u + 2 < nA:
                        exp_a(u + 2)
                    gates(u)
                    if u:
                        conv_norm(u)
                exp_d(0)
                exp_d(1)
                for u in range(len(DU)):
                    pt_copy(nA + u, DU[u][2])
                    if u + 2 < len(DU):
                        exp_d(u + 2)
                    gates(nA + u)
                act.wait_ge(s["attn_out"], nA + len(DU))
                for i in range(HD):
                    f(P[:, i, q0:T], qd[:, i, q0:T], ACT.Square).then_inc(s["stat_ready"], 1)
                gate(2, 0)
                take(("dn", l))
                root(None, 32, HD * nt, 1.0 / (2 * DH))
                for c in range(1, KD):
                    gate(2, c)
                act.wait_ge(s["g1_ready"], 1)

                def square_pair(c):
                    act.wait_ge(s["out_part"], c // 2 + 1)
                    square(s, c, qt0, 4)
                    act.wait_ge(empty["d"], Dn[("out", l, c + 1)])
                    square(s, c + 1, qt0, 4)

                for c in range(0, KD, 2):
                    take(("out", l, c))
                    j = (c // 2) % 2
                    if c >= 4:
                        act.wait_ge(s["out_part"], c // 2 - 1)
                    for v, t0, t1 in SEGS:
                        ins = f(P[:, j, t0:t1], PS[0][:, t0 - q0:t1 - q0], ACT.Copy,
                                scale=mod[l][:, 2 * KD + c, v:v + 1])
                    give(ins)
                    if c:
                        square_pair(c - 2)
                square_pair(KD - 2)
                norm_root(("n2", l), qt0)
                shifts(s, l, SEGS, 1, KD)
                def h2_store(tiles):
                    for t in tiles:
                        for half in range(2):
                            take(("h2", l, qt0 + t, half))
                            give(f(stage[:, t, 512 * half:512 * half + 512], PS[0][:, :], ACT.Copy))
                        act.wait_ge(empty["a"], A[("h2", l, qt0 + t, 1)])
                        act.dma_start(h2d[l][t * 128:t * 128 + 128, :], stage[:, t, :]).then_inc(s["h2_stored"], 16)

                h2_store(range(0, 2))
                act.wait_ge(s["gexp_in"], 1)
                f(g4[1][:, 0:nt, :], g4[0][:, 0:nt, :], ACT.Exp)
                f(col[5][:, 0:nt], col[4][:, 0:nt], ACT.Exp).then_inc(s["gexp"], 1)
                h2_store(range(2, nt))
                C = NQ // 8
                yrow = yd[l].rearrange("(r b) d -> r b d", b=NBLK)

                def xgt_copy(j, i):
                    act.wait_ge(s["xgt_full"], i * 4 + j + 1)
                    if not (isinstance(i, int) and 4 * i + j < 2):
                        act.wait_ge(s["gu_full"], i * 4 + j - 1)
                    f(xgt[:, j % 2, 0:KD * C], PS[2 + j % 2][:, 0:KD * C], ACT.Copy).then_inc(s["xgt_ready"], 1)

                def gate_tanh(j, i):
                    act.wait_ge(s["gu_full"], i * 4 + j + 1)
                    if not (isinstance(i, int) and 4 * i + j < 2):
                        act.wait_ge(s["hid_ready"], i * 4 + j - 1)
                    f(gt[0:C, j % 2, :], PS[4 + j % 2][0:C, 0:FF], ACT.Tanh, scale=0.5).then_inc(s["gtanh"], 1)

                def y_out(j, i):
                    p = j % 2
                    act.wait_ge(s["y_full"], i * 4 + j + 1)
                    if not (isinstance(i, int) and 4 * i + j < 2):
                        act.wait_ge(s[f"y_stored{p}"], i * 64 + 32 * (j // 2))
                    f(yy[0:64 + C, p, 0:512], PS[6 + p][0:64 + C, :], ACT.Copy).then_inc(s["y_act"], 1)
                    act.wait_ge(s["y_act"], i * 4 + j + 1)
                    for n in range(2):
                        act.dma_start(yrow[0:C, bass.ds(i * 4 + j, 1), n * 512:n * 512 + 512],
                                      yy[64 * n:64 * n + C, p:p + 1, 0:512]).then_inc(s[f"y_stored{p}"], 16)

                def group(i, first, last):
                    for j in range(4):
                        gate_tanh(j, i)
                        if not (last and j == 3):
                            xgt_copy((j + 1) % 4, i + (j + 1) // 4)
                        if not (first and j == 0):
                            y_out((j - 1) % 4, i - (j == 0))

                xgt_copy(0, 0)
                group(0, True, False)
                with act.Fori(1, NE // 4 - 1) as i:
                    group(i, False, False)
                group(NE // 4 - 1, False, True)
                y_out(3, NE // 4 - 1)
                nx = act.value_load(meta[l][0:1, 15:16], min_val=0, max_val=OVER)
                with act.If(nx > 0):
                    act.wait_ge(s["y_stored0"], 32 * NE // 2)
                    def extra(j):
                        act.wait_ge(s["ov_pe"], 4 * j + 1)
                        f(xgt[:, 0, 0:KD * C], PS[2][:, 0:KD * C], ACT.Copy).then_inc(s["ov_act"], 1)
                        act.wait_ge(s["ov_pe"], 4 * j + 2)
                        f(gt[0:C, 0, :], PS[4][0:C, 0:FF], ACT.Tanh, scale=0.5).then_inc(s["ov_act"], 1)
                        act.wait_ge(s["ov_pe"], 4 * j + 4)
                        f(yy[0:64 + C, 0, 0:512], PS[6][0:64 + C, :], ACT.Copy).then_inc(s["ov_act"], 1)
                        act.wait_ge(s["ov_act"], 3 * j + 3)
                        for n in range(2):
                            act.dma_start(yrow[0:C, bass.ds(NE + j, 1), n * 512:n * 512 + 512],
                                          yy[64 * n:64 * n + C, 0:1, 0:512]).then_inc(s["ov_stored"], 16)
                        wait_apart(act, s["ov_stored"], 32 * j + 32)

                    extra(0)
                    with act.If(nx > 1):
                        with act.Fori(1, OVER) as j:
                            with act.If(nx > j):
                                extra(j)
            act.wait_ge(empty["d"], Dn[("mix", 1, 3, 1)])
            for k in range(KD):
                square(S[1], k, 2, 8)
            norm_root(("nf", 1), 2)

        @block.vector
        def _(dve):
            A, Dn = number["a"], number["d"]
            own = [0]
            V = nc.vector

            def step(ins):
                own[0] += 1
                ins.then_inc(dve_step, 1)
                dve.wait_ge(dve_step, own[0])

            def stt(out, in0, sc, in1, op0=MUL, op1=MUL):
                return V.scalar_tensor_tensor(out, in0, sc, in1, op0=op0, op1=op1)

            def take(key):
                dve.wait_ge(full["d"], Dn[key])

            def give(ins):
                ins.then_inc(empty["d"], 1)

            def ada_raw(key):
                for n in ada_behind(key):
                    take(units[n])
                    give(V.tensor_copy(ada_tmp(n), PS[1][:, :]))

            def ada_finish(key):
                for n in ada_behind(key):
                    ada_evac(units[n])

            def ada_evac(key):
                _, la, u = key
                take(("adaT", la, u))
                give(V.tensor_tensor(ada[la][:, 4 * u:4 * u + 4, :], grid(PS[1][:, 0:8], 4),
                                     vec_at(la, "b_ada")[:, 4 * u:4 * u + 4].unsqueeze(2).to_broadcast([128, 4, 2]), op=ADD))

            def scales(l, which):
                dve.wait_ge(empty["d"], max(Dn[("adaT", l, u)] for u in {0: (0, 1, 2, 3), 1: (8, 9), 2: (4, 5)}[which]))
                if which == 2:
                    V.tensor_scalar(mod[l][:, 16:24, :], ada[l][:, 16:24, :], 0.5, None, MUL).then_inc(S[l]["g1_ready"], 1)
                    dve.wait_ge(S[l]["g1_ready"], 1)
                    return
                c0 = (KD, 4 * KD)[which]
                g = vec_at(l, ("norm1_g", "norm2_g")[which]).unsqueeze(2).to_broadcast([128, KD, 2])
                step(stt(mod[l][:, which * KD:which * KD + KD, :], ada[l][:, c0:c0 + KD, :], 1.0, g, ADD, MUL))

            def recip(s, c0, n, key):
                dve.wait_ge(empty["a"], A[key])
                V.reciprocal(st[:, c0:c0 + n], st[:, c0:c0 + n]).then_inc(s["recip_ready"], 1)

            def norm_rstd(s, key, t0, nth):
                dve.wait_ge(empty["a"], A[key])
                V.reciprocal(rstd[:, t0 * 128:T], rstd[:, t0 * 128:T]).then_inc(s["recip_ready"], 1)
                dve.wait_ge(s["recip_ready"], nth)

            def norm_apply(s, t0):
                for k in range(KD):
                    V.tensor_tensor(h[:, k, t0 * 128:T], x[:, k, t0 * 128:T], rstd[:, t0 * 128:T], op=MUL) \
                        .then_inc(s["modded"], 1)

            BOTH = [(1, 0, CTX), (0, CTX, T)]
            V.memset(ones[:, :], 1.0).then_inc(consts_set, 1)
            step(V.memset(silz, 0.0))
            step(V.memset(small[:, :], 0.0))
            V.memset(small[:, 0:1], EPS).then_inc(consts_set, 1)
            dve.wait_ge(loaded, 16 * 5)
            for l in range(DEPTH):
                lam = vec_at(l, "lams")
                for m in range(2):
                    step(V.tensor_tensor(am[:, 0:DH], lam[:, 2 * m * DH:2 * m * DH + DH],
                                         lam[:, 2 * m * DH + DH:2 * m * DH + 2 * DH], op=MUL))
                    ins = V.reduce_sum(small[:, 1 + 2 * l + m:2 + 2 * l + m], am[:, 0:DH], AX.X)
                    if (l, m) == (1, 1):
                        ins.then_inc(lam_sums, 1)
                    else:
                        step(ins)
            dve.wait_ge(silc_tanh, 1)
            step(stt(silc[:, 0:16], silc[:, 0:16], 1.0, silc[:, 16:32], ADD, MUL))
            V.tensor_scalar(silz.rearrange("p (k n) -> p k n", k=KD)[:, :, 0:2], silc[:, 0:16].rearrange("p (k n) -> p k n", k=KD),
                            0.5, None, MUL).then_inc(silc_ready, 1)
            dve.wait_ge(lam_exps, 1)
            for l in range(DEPTH):
                lam_init = 0.8 - 0.6 * math.exp(-0.3 * l)
                step(V.tensor_tensor(small[:, 9 + l:10 + l], small[:, 6 + 2 * l:7 + 2 * l], small[:, 5 + 2 * l:6 + 2 * l], op=SUB))
                step(V.tensor_scalar(small[:, 9 + l:10 + l], small[:, 9 + l:10 + l], -lam_init, None, ADD))
                step(V.tensor_scalar(vec_at(l, "sub_g"), vec_at(l, "sub_g"), 1.0 - lam_init, None, MUL))
                step(V.tensor_scalar(vec_at(l, "conv_w"), vec_at(l, "conv_w"), 0.5, None, MUL))
                step(V.tensor_scalar(vec_at(l, "ln_b"), vec_at(l, "ln_b"), 0.5, None, MUL))
            step(V.tensor_copy(tok, rcon_at("token")))
            V.memset(zero, 0).then_inc(table_zero, 1)
            ada_raw(None)
            ada_finish(None)
            dve.wait_ge(x_loaded, 16)
            for l in range(DEPTH):
                s = S[l]
                q0 = 0 if l == 0 else CTX
                qt0, NQ = q0 // 128, T - q0
                nt = 4 - qt0
                SEGS = BOTH if l == 0 else BOTH[1:]
                seqs = slice(0 if l == 0 else 1, 2)
                scales(l, 0)
                norm_rstd(s, ("n1", l), 0, 1)
                norm_apply(s, 0)
                take(("lora", l, 1))
                give(V.tensor_copy(lora[:, 1, q0:T], PS[1][:, 0:NQ]))
                take(("lora", l, 3))
                give(V.tensor_copy(lora[64:96, 3, :], PS[1][0:32, :]))
                ada_raw(("lora", l, 0))
                dve.wait_ge(s["pool_set"], 1)
                for j in range(CT):
                    if j % 2 == 0:
                        ada_finish(("glu", l, 0) if j else ("lora", l, 0))
                    take(("gluA", l, j))
                    dve.wait_ge(empty["a"], A[("gluG", l, j)])
                    give(stt(up[:, j, seqs, PAD:PAD + 256], PT[:, j % 2, q0:T].rearrange("p (s u) -> p s u", u=256), 1.0,
                             PS[1][:, 0:NQ].rearrange("p (s u) -> p s u", u=256), ADD, MUL))
                    if j % 2 == 1:
                        ada_raw(("glu", l, j // 2))
                last_glu = Dn[("gluA", l, CT - 1)]
                recip(s, 8, nt + 4, ("loraS", l))
                take(("loraQ", l))
                stt(lora[:, 0, q0:T], lora[:, 0, q0:T], vec_at(l, "q_g")[:, 0:1], PS[1][:, q0:T])
                give(stt(lora[:, 1, q0:T], lora[:, 1, q0:T], vec_at(l, "q_g")[:, 1:2], PS[1][:, q0:T]))
                take(("loraK", l))
                give(stt(lora[:, 2, :], lora[:, 2, :], vec_at(l, "kv_g"), PS[1][:, :]))
                kr, krt = lora[64:96, 3, CTX:T], PT[64:96, 0, 0:SEQ]
                swap = [(r + 16) % 32 for r in range(32)]
                dve.wait_ge(empty["d"], last_glu)
                V.stream_shuffle(krt, kr, swap).then_inc(dve_step, 1)
                own[0] += 1
                dve.wait_ge(dve_step, own[0])
                step(V.tensor_tensor(krt, krt, con_at("sin_a")[64:96, :], op=MUL))
                step(V.tensor_tensor(kr, kr, con_at("cos_a")[64:96, :], op=MUL))
                V.tensor_tensor(kr, kr, krt, op=ADD).then_inc(s["kr_ready"], 1)

                conv_at = [0]
                base = own[0]

                def conv(n):
                    for o in range(conv_at[0], min(conv_at[0] + n, CW * CT)):
                        tap, c = divmod(o, CT)
                        w_ = vec_at(l, "conv_w")[:, c * CW + tap:c * CW + tap + 1]
                        src = up[:, c, seqs, tap:tap + 256]
                        dst = cv[:, c, q0:T].rearrange("p (s u) -> p s u", u=256)
                        if tap == 0:
                            ins = V.tensor_scalar(dst, src, w_, vec_at(l, "conv_b")[:, c:c + 1], MUL, ADD)
                        else:
                            dve.wait_ge(dve_step, conv_done[o - CT])
                            ins = stt(dst, src, w_, dst, MUL, ADD)
                        own[0] += 1
                        conv_done[o] = own[0]
                        ins.then_inc(dve_step, 1)
                    conv_at[0] = min(conv_at[0] + n, CW * CT)

                conv_done = {}

                def swapped_sin(dst, src, nth, wait):
                    dve.wait_ge(s["rope_pool"], wait) if wait else dve.wait_ge(full["a"], A[("loraS", l)])
                    for o_, i_ in ((0, 1), (1, 0), (2, 3), (3, 2)):
                        ins = V.tensor_tensor(dst[32 * o_:32 * o_ + 32], src[32 * i_:32 * i_ + 32, :, CTX:T],
                                              con_at("sin_d")[32 * i_:32 * i_ + 32, :].unsqueeze(1).to_broadcast([32, HD, SEQ]),
                                              op=MUL)
                    ins.then_inc(s["rope_part"], 1)

                Pd = P[:, 0:2, :].rearrange("p a (b n) -> p (a b) n", b=2)
                Pq = P[64:96, :, :].rearrange("p a (b n) -> p (a b) n", b=2)
                few, many = (4, 16)
                conv(few)
                for i in range(1, HD, 2):
                    if i == 1:
                        ada_finish(("glu", l, 1))
                    take(("dq", l, i))
                    give(V.tensor_copy(qd[:, i, q0:T], PS[1][:, 0:NQ]))
                    conv(many - 4)
                ada_raw(("dq", l, 0))
                dve.wait_ge(empty["d"], Dn[("dq", l, HD - 1)])
                dve.wait_ge(empty["a"], A[("dq", l, HD - 2)])
                swapped_sin(Pd, qd, 1, 0)
                dve.wait_ge(y_zeroed, 16 * DEPTH)
                ada_finish(("dq", l, 0))
                for i in range(1, HA, 2):
                    take(("uq", l, i))
                    give(V.tensor_copy(qa[0:96, i, q0:T], PS[1][0:96, 0:NQ]))
                for i in range(1, HA, 2):
                    take(("uk", l, i))
                    give(V.tensor_copy(ka[0:64, i, :], PS[1][0:64, :]))
                for t in range(1, 4, 2):
                    take(("uv", l, t))
                    give(V.tensor_copy(va[:, t, :], PS[1][:, :]))
                ada_raw(("ukv", l, 0))
                dve.wait_ge(empty["a"], A[("uq", l, HA - 2)])
                dve.wait_ge(empty["d"], Dn[("uq", l, HA - 1)])
                dve.wait_ge(s["rope_pool"], 1)
                V.stream_shuffle(Pq, qa[64:96, :, CTX:T], swap).then_inc(s["rope_part"], 1)
                for i in range(1, HD, 2):
                    conv(many + 4)
                    if i == 1:
                        ada_finish(("ukv", l, 0))
                    take(("dk", l, i))
                    give(V.tensor_copy(kd[:, i, :], PS[1][:, :]))
                ada_raw(("dk", l, 0))
                dve.wait_ge(empty["d"], Dn[("dk", l, HD - 1)])
                dve.wait_ge(empty["a"], A[("dk", l, HD - 2)])
                swapped_sin(Pd, kd, 3, 2)
                for t in range(1, 4, 2):
                    conv(many)
                    if t == 1:
                        ada_finish(("dk", l, 0))
                    take(("dv", l, t))
                    give(V.tensor_copy(vd[:, t, :], PS[1][:, :]))
                ada_raw(("dv", l, 0))
                ada_finish(("dv", l, 0))
                conv(CW * CT)
                dve.wait_ge(dve_step, own[0])
                V.memset(small[:, 14:15], 0.0).then_inc(s["conv_v"], 1)
                def conv_norm(u):
                    if u == 2:
                        take(("lnMb", l))
                        for c in range(CT):
                            ins = V.tensor_tensor(cv[:, c, q0:T], cv[:, c, q0:T], PS[1][:, q0:T], op=SUB)
                        give(ins)
                    elif u == 9 + l:
                        recip(s, 24, nt, ("lnV", l))
                    elif u == 11 + l:
                        take(("lnVb", l))
                        for c in range(CT):
                            ins = stt(cv[:, c, q0:T], cv[:, c, q0:T], vec_at(l, "ln_g")[:, c:c + 1], PS[1][:, q0:T])
                            if c < CT - 1:
                                ins.then_inc(s["conv_scaled"], 1)
                            else:
                                give(ins)
                    elif u == 13:
                        for c in range(CT):
                            dve.wait_ge(s["conv_act"], 2 * c + 2)
                            stt(cv[:, c, q0:T], lora[:, c, q0:T], 1.0, cv[:, c, q0:T], ADD, MUL).then_inc(s["conv_out"], 1)

                AU, DU = attn_units(l)
                nA = len(AU)
                nlam = small[:, 9 + l:10 + l]

                def peak(g, banks, nk, scale, tiles):
                    c = 8 * (g % 8)
                    for m, b in enumerate(banks):
                        dve.wait_ge(s["scores"], tiles + m + 1)
                        ins = V.reduce_max(am[:, c + m:c + m + 1], PS[b][:, 0:nk], AX.X)
                    step(ins)
                    n = len(banks)
                    V.tensor_scalar(am[:, c + 2:c + 2 + n], am[:, c:c + n], -scale, None, MUL).then_inc(s["scores_max"], 1)

                def peak_a(u):
                    peak(u, [2 + u % 4], AU[u][2], SCALE_A, u)

                def peak_d(u):
                    peak(nA + u, [2 + 2 * (u % 2), 3 + 2 * (u % 2)], DU[u][2], SCALE_D, nA + 2 * u)

                def probs_a(u):
                    c, nk = 8 * (u % 8), AU[u][2]
                    dve.wait_ge(s["exp_ready"], u + 1)
                    step(V.reciprocal(am[:, c + 6:c + 7], am[:, c + 4:c + 5]))
                    V.tensor_scalar(P[:, u % 4, 0:nk], P[:, u % 4, 0:nk], am[:, c + 6:c + 7], None, MUL) \
                        .then_inc(s["probs_ready"], 1)

                def probs_d(u):
                    c, nk = 8 * ((nA + u) % 8), DU[u][2]
                    p0, p1 = dprob(u)[:, 0, 0:nk], dprob(u)[:, 1, 0:nk]
                    dve.wait_ge(s["exp_ready"], nA + 2 * u + 2)
                    step(V.reciprocal(am[:, c + 6:c + 8], am[:, c + 4:c + 6]))
                    step(V.tensor_scalar(p1, p1, am[:, c + 7:c + 8], nlam, MUL, MUL))
                    stt(p0, p0, am[:, c + 6:c + 7], p1, MUL, ADD).then_inc(s["probs_ready"], 1)

                def out_copy(g, out, ps):
                    dve.wait_ge(s["pv_full"], g + 1)
                    V.tensor_copy(out, ps).then_inc(s["attn_out"], 1)

                def out_a(u):
                    i, t, nk = AU[u]
                    r = 64 * (i % 2)
                    out_copy(u, oa[r:r + 64, i // 2, t * 128:t * 128 + 128], PS[7][r:r + 64, 0:128])

                def out_d(u):
                    i, t, nk = DU[u]
                    out_copy(nA + u, qd[:, i, t * 128:t * 128 + 128], PS[7][:, 0:128])

                def branch(b, c):
                    take(("branch", l, c, b))
                    dve.wait_ge(empty["a"], A[("gate", l, c, b)])
                    out = yt[c][:, q0:T] if b == 0 else gt8[:, c, q0:T]
                    give(stt(out, out, 1.0, PS[1][:, 0:NQ], ADD, MUL))

                def merge_tiles(g):
                    for what, b, c in merge_done(l, *merge_range(l, g)):
                        if what == "branch":
                            branch(b, c)
                        elif what == "ada":
                            ada_raw(c)
                        elif what == "adaT":
                            ada_finish(c)

                peak_a(0)
                peak_a(1)
                probs_a(0)
                for u in range(nA):
                    if u + 2 < nA:
                        peak_a(u + 2)
                    if u + 1 < nA:
                        probs_a(u + 1)
                    if u >= 1:
                        out_a(u - 1)
                    merge_tiles(u)
                    conv_norm(u)
                peak_d(0)
                peak_d(1)
                probs_d(0)
                out_a(nA - 1)
                for u in range(len(DU)):
                    if u + 2 < len(DU):
                        peak_d(u + 2)
                    if u + 1 < len(DU):
                        probs_d(u + 1)
                    if u >= 1:
                        out_d(u - 1)
                    merge_tiles(nA + u)
                out_d(len(DU) - 1)
                recip(s, 32, HD * nt, ("dn", l))
                for i in range(HD):
                    take(("dnb", l, i))
                    give(stt(qd[:, i, q0:T], qd[:, i, q0:T], vec_at(l, "sub_g"), PS[1][:, q0:T]))
                ada_finish(("mo1", l, 0))
                for c in range(KD):
                    branch(2, c)
                ada_raw(("mg5", l, 0))
                ada_finish(("mg5", l, 0))
                scales(l, 2)
                for c in range(1, KD, 2):
                    take(("out", l, c))
                    for v, t0, t1 in SEGS:
                        ins = stt(x[:, c, t0:t1], PS[1][:, t0 - q0:t1 - q0], mod[l][:, 2 * KD + c, v:v + 1],
                                  x[:, c, t0:t1], MUL, ADD)
                    give(ins)
                    if c % 4 == 3:
                        ada_raw(("out", l, c // 4))
                        ada_finish(("out", l, c // 4))
                scales(l, 1)
                norm_rstd(s, ("n2", l), qt0, 5)
                norm_apply(s, qt0)
                take(("router", l))
                give(V.tensor_tensor(lg[:, 0:nt, :], grid(PS[1][:, 0:36 * nt], nt),
                                     vec_at(l, "b_r").unsqueeze(1).to_broadcast([128, nt, NG + NE]), op=ADD))
                dve.wait_ge(empty["d"], Dn[("router", l)])

                def over(c, n):
                    return c[:, 0:nt].unsqueeze(2).to_broadcast([128, nt, n])

                def row(r, n):
                    return r.unsqueeze(1).to_broadcast([128, nt, n])

                def first_max(values, n, desc, top, tmp, hot, best):
                    step(V.reduce_max(best[:, 0:nt], values, AX.X))
                    step(V.tensor_tensor(tmp, values, over(best, n), op=ALU.is_equal))
                    step(V.tensor_tensor(tmp, tmp, row(desc, n), op=MUL))
                    step(V.reduce_max(top[:, 0:nt], tmp, AX.X))
                    step(V.tensor_tensor(hot, tmp, over(top, n), op=ALU.is_equal))

                B = [b_[:, 0:nt, :] for b_ in big]
                glog = lg[:, 0:nt, 0:NG]
                g0, g1_, g2_ = (g_[:, 0:nt, :] for g_ in g4)
                first_max(glog, NG, rcon_at("desc4"), col[1], g1_, g2_, col[0])
                step(V.tensor_tensor(g0, glog, over(col[0], NG), op=SUB))
                step(V.tensor_scalar(g2_, g2_, -1.0, 3.0e38, ADD, MUL))
                for t in range(nt):
                    ins = V.tensor_tensor(B[0][:, t, :].rearrange("p (g e) -> p g e", g=NG),
                                          lg[:, t, NG:].rearrange("p (g e) -> p g e", g=NG),
                                          g4[2][:, t, :].unsqueeze(2).to_broadcast([128, NG, EG]), op=ADD)
                step(ins)
                first_max(B[0], NE, rcon_at("desc32"), col[1], B[1], B[2], col[2])
                step(V.scalar_tensor_tensor(B[0], B[2], -3.1e38, B[0], op0=MUL, op1=ADD))
                first_max(B[0], NE, rcon_at("desc32"), col[1], B[1], B[3], col[3])
                V.tensor_tensor(col[4][:, 0:nt], col[3][:, 0:nt], col[2][:, 0:nt], op=SUB).then_inc(s["gexp_in"], 1)
                V.tensor_tensor(B[4], B[2], B[3], op=ADD).then_inc(s["mask_ready"], 1)
                dve.wait_ge(s["gexp"], 1)
                step(V.reduce_sum(col[6][:, 0:nt], g1_, AX.X))
                step(stt(col[7][:, 0:nt], col[5][:, 0:nt], 1.0, col[6][:, 0:nt], ADD, MUL))
                step(V.reciprocal(col[7][:, 0:nt], col[7][:, 0:nt]))
                step(V.tensor_scalar(col[8][:, 0:nt], col[7][:, 0:nt], 0.5, None, MUL))
                step(V.tensor_tensor(col[9][:, 0:nt], col[8][:, 0:nt], col[5][:, 0:nt], op=MUL))
                C = NQ // 8
                half_up = 1.0 / (2 * C) - 0.5
                extra, cum, cum2, dvec = c32[0], c32[1], c32[2], c32[3]
                take(("rank", l))
                step(V.tensor_copy(B[5], grid(PS[1][:, 0:32 * nt], nt)))
                step(V.tensor_scalar(extra, PS[1][:, 32 * nt:32 * nt + 32], 1.0 / C, half_up - 1.0 / C, MUL, ADD))
                step(V.tensor_scalar(extra, extra, ROUND, None, ADD))
                step(V.tensor_scalar(extra, extra, -ROUND, 0.0, ADD, ALU.max))
                give(V.tensor_copy(cum, extra))
                dve.wait_ge(empty["d"], Dn[("rank", l)])
                for sh in (1, 2, 4, 8, 16):
                    step(V.tensor_copy(cum2[:, 0:sh], cum[:, 0:sh]))
                    step(V.tensor_tensor(cum2[:, sh:NE], cum[:, sh:NE], cum[:, 0:NE - sh], op=ADD))
                    cum, cum2 = cum2, cum
                step(V.tensor_tensor(dvec, cum, extra, op=SUB))
                step(stt(dvec, dvec, float(NE - 1), rcon_at("expert"), ADD, SUB))
                step(V.tensor_scalar(B[6], B[5], 1.0 / C, half_up, MUL, ADD))
                step(V.tensor_scalar(B[6], B[6], ROUND, None, ADD))
                step(V.tensor_scalar(B[6], B[6], -ROUND, None, ADD))
                step(V.tensor_scalar(B[7], B[6], 1.0, None, ALU.is_ge))
                step(V.tensor_tensor(B[1], B[6], row(dvec, NE), op=ADD))
                step(V.tensor_tensor(B[1], B[1], B[7], op=MUL))
                step(V.tensor_tensor(B[1], B[1], row(rcon_at("expert"), NE), op=ADD))
                step(stt(B[1], B[5], float(NBLK), B[1], MUL, ADD))
                step(stt(B[1], B[6], float(-NBLK * C), B[1], MUL, ADD))
                for m in range(2):
                    step(V.tensor_tensor(B[7], B[1], B[2 + m], op=MUL))
                    step(V.reduce_sum(col[0][:, 0:nt], B[7], AX.X))
                    step(V.tensor_copy(sl[:, m, 0:nt], col[0][:, 0:nt]))
                step(V.tensor_tensor(cmp15, cum.unsqueeze(1).to_broadcast([128, OVER, NE]),
                                     rcon_at("nth").unsqueeze(2).to_broadcast([128, OVER, NE]), op=ALU.is_le))
                step(V.reduce_sum(ov15[:, 0:OVER], cmp15, AX.X))
                step(V.tensor_copy(ov15[:, OVER:OVER + 1], cum[:, NE - 1:NE]))
                V.tensor_copy(meta[l], ov15).then_inc(s["slots_ready"], 1)
                for n in range(2 * nt):
                    ins = V.tensor_scalar(bigs[:, 128 * n:128 * n + 128], ident, col[8 + n % 2][:, n // 2:n // 2 + 1], None, MUL)
                ins.then_inc(s["weights_ready"], 1)

                def hidden(j, i):
                    p = j % 2
                    dve.wait_ge(s["gtanh"], i * 4 + j + 1)
                    if not (isinstance(i, int) and 4 * i + j < 2):
                        dve.wait_ge(s["ht_full"], i * 4 + j - 1)
                    stt(hid[0:C, p, :], gt[0:C, p, :], 1.0, PS[4 + p][0:C, 0:FF], ADD, MUL).then_inc(hid_half, 1)
                    dve.wait_ge(hid_half, 32 * l + i * 4 + j + 1)
                    V.tensor_tensor(hid[0:C, p, :], hid[0:C, p, :], PS[4 + p][64:64 + C, 0:FF], op=MUL) \
                        .then_inc(s["hid_ready"], 1)

                def hidden_copy(j, i):
                    p = j % 2
                    dve.wait_ge(s["ht_full"], i * 4 + j + 1)
                    if not (isinstance(i, int) and 4 * i + j < 2):
                        dve.wait_ge(s["y_full"], i * 4 + j - 1)
                    V.tensor_copy(hidt[:, p, 0:2 * C], PS[0][:, 0:2 * C]).then_inc(s["hidt_ready"], 1)

                def group(i):
                    for j in range(4):
                        hidden(j, i)
                        hidden_copy(j, i)

                group(0)
                with dve.Fori(1, NE // 4) as i:
                    group(i)
                nx = dve.value_load(meta[l][0:1, 15:16], min_val=0, max_val=OVER)
                with dve.If(nx > 0):
                    def extra(j):
                        dve.wait_ge(s["ov_act"], 3 * j + 2)
                        stt(hid[0:C, 0, :], gt[0:C, 0, :], 1.0, PS[4][0:C, 0:FF], ADD, MUL).then_inc(s["ov_dve"], 1)
                        dve.wait_ge(s["ov_dve"], 3 * j + 1)
                        V.tensor_tensor(hid[0:C, 0, :], hid[0:C, 0, :], PS[4][64:64 + C, 0:FF], op=MUL) \
                            .then_inc(s["ov_dve"], 1)
                        dve.wait_ge(s["ov_pe"], 4 * j + 3)
                        V.tensor_copy(hidt[:, 0, 0:2 * C], PS[0][:, 0:2 * C]).then_inc(s["ov_dve"], 1)

                    extra(0)
                    with dve.If(nx > 1):
                        with dve.Fori(1, OVER) as j:
                            with dve.If(nx > j):
                                extra(j)
                for t in range(nt):
                    v = 1 if qt0 + t < 2 else 0
                    for half in range(2):
                        take(("mix", l, qt0 + t, half))
                        for k in range(4):
                            xs = x[:, 4 * half + k, (qt0 + t) * 128:(qt0 + t) * 128 + 128]
                            ins = stt(xs, PS[1][:, k * 128:k * 128 + 128], ada[l][:, 5 * KD + 4 * half + k, v:v + 1],
                                      xs, MUL, ADD)
                        give(ins)
            s = S[1]
            norm_rstd(s, ("nf", 1), 2, 6)
            for k in range(KD):
                ins = stt(h[:, k, CTX:T], x[:, k, CTX:T], fing[:, k:k + 1], rstd[:, CTX:T])
            ins.then_inc(out_ready, 1)

        @block.gpsimd
        def _(pool):
            A, Dn = number["a"], number["d"]
            own = [0]
            G = nc.gpsimd

            def step(ins):
                own[0] += 1
                ins.then_inc(pool_step, 1)
                pool.wait_ge(pool_step, own[0])

            def add_squares(s, ks, t0, n):
                for k in ks:
                    if k == 0 or k > 4:
                        continue
                    pool.wait_ge(s["sq_ready"], n * KD + k + 1)
                    if k > 1:
                        pool.wait_ge(s["ssq"], n * 4 + k - 1)
                    G.tensor_tensor(P[:, 3, t0 * 128:T], P[:, 3, t0 * 128:T], sqt(k)[:, t0 * 128:T], op=ADD) \
                        .then_inc(s["ssq"], 1)

            pool.wait_ge(table_zero, 1)
            for l in range(DEPTH):
                pool.dma_start(td[l].rearrange("(r b) o -> r (b o)", b=NBLK), zero[0:CAP[l], :]).then_inc(zeroed, 16)
            for l in range(DEPTH):
                s = S[l]
                q0 = 0 if l == 0 else CTX
                qt0, NQ = q0 // 128, T - q0
                nt = 4 - qt0
                if l == 1:
                    pool.wait_ge(empty["d"], Dn[("mix", 0, 3, 1)])
                G.memset(arena[:, 16384:16384 + CT * 2 * UP], 0.0).then_inc(s["pool_set"], 1)
                add_squares(s, range(KD), 0, 0)
                pool.wait_ge(s["pool_set"], 1)
                if l == 0:
                    G.memset(arena[:, 0:D], 0.0).then_inc(pool_step, 1)
                    own[0] += 1
                    pool.wait_ge(pool_step, own[0])
                    pool.wait_ge(empty["d"], Dn[("lora", 0, 1)])
                    for ll in range(DEPTH):
                        pool.dma_start(yd[ll].rearrange("(r b) d -> r b d", b=NBLK)[:, NE:, :],
                                       arena[0:CAP[ll], 0:D].unsqueeze(1).to_broadcast([CAP[ll], NBLK - NE, D])) \
                            .then_inc(y_zeroed, 16)
                pool.wait_ge(s["kr_ready"], 1)
                for n in ada_behind(("glu", l, 1)):
                    pool.wait_ge(empty["d"], Dn[("adaT",) + units[n][1:]])
                G.tensor_copy(ka[64:96, :, :], lora[64:96, 3:4, :].to_broadcast([32, HA, T])).then_inc(s["pool_set"], 1)

                pool.wait_ge(s["pool_set"], 2)

                def rotate(part, rows, q, t, cos, sin, heads):
                    pool.wait_ge(s["rope_part"], part)
                    r = slice(*rows)
                    if sin is not None:
                        step(G.tensor_tensor(t, t, con_at(sin)[r, :].unsqueeze(1).to_broadcast([rows[1] - rows[0], heads, SEQ]), op=MUL))
                    step(G.tensor_tensor(q[r, :, CTX:T], q[r, :, CTX:T],
                                         con_at(cos)[r, :].unsqueeze(1).to_broadcast([rows[1] - rows[0], heads, SEQ]), op=MUL))
                    pool.wait_ge(pool_step, own[0])
                    G.tensor_tensor(q[r, :, CTX:T], q[r, :, CTX:T], t, op=ADD).then_inc(s["rope_pool"], 1)
                    pool.wait_ge(s["rope_pool"], part)

                Pd = P[:, 0:2, :].rearrange("p a (b n) -> p (a b) n", b=2)
                Pq = P[64:96, :, :].rearrange("p a (b n) -> p (a b) n", b=2)
                rotate(1, (0, 128), qd, Pd, "cos_d", None, HD)
                rotate(2, (64, 96), qa, Pq, "cos_a", "sin_a", HA)
                rotate(3, (0, 128), kd, Pd, "cos_d", None, HD)
                for b, done in ((1, "merge_part"), (2, "yt_ready")):
                    for c in range(KD):
                        pool.wait_ge(empty["d"], Dn[("branch", l, c, b)])
                        G.tensor_tensor(yt[c][:, q0:T], yt[c][:, q0:T], gt8[:, c, q0:T], op=ADD).then_inc(s[done], 1)
                    pool.wait_ge(s[done], KD)
                for c in range(0, KD, 2):
                    pool.wait_ge(empty["a"], A[("out", l, c)])
                    G.tensor_tensor(x[:, c, q0:T], x[:, c, q0:T], P[:, (c // 2) % 2, q0:T], op=ADD) \
                        .then_inc(s["out_part"], 1)
                    if c:
                        add_squares(s, (c - 2, c - 1), qt0, 1)
                add_squares(s, (KD - 2, KD - 1), qt0, 1)
                C = NQ // 8
                pool.wait_ge(zeroed, 16 * DEPTH)
                pool.wait_ge(s["slots_ready"], 1)
                for t in range(nt):
                    for m in range(2):
                        pool.indirect_dma_start(out=td[l][:, :], out_offset=bass.IndirectOffsetOnAxis(ap=sl[:, m, t:t + 1], axis=0),
                                                in_=tok[:, t:t + 1], in_offset=None).then_inc(s["tokens_moved"], 16)
                pool.wait_ge(s["tokens_moved"], 16 * 2 * nt)
                pool.dma_start(idx[0:C, :], td[l].rearrange("(r b) o -> r (b o)", b=NBLK)[0:C, :]).then_inc(s["tokens_moved"], 16)
                pool.wait_ge(s["tokens_moved"], 16 * 2 * nt + 16)
                pool.wait_ge(s["h2_stored"], 16 * nt)

                def gather(j, i):
                    p = j % 2
                    if not (isinstance(i, int) and 4 * i + j < 2):
                        pool.wait_ge(s["xgt_full"], i * 4 + j - 1)
                    G.tensor_copy(icol[0:C, p:p + 1], idx[0:C, bass.ds(i * 4 + j, 1)]).then_inc(s["icol_ready"], 1)
                    wait_apart(pool, s["icol_ready"], i * 4 + j + 1)
                    pool.indirect_dma_start(out=xg[0:C, p, :], out_offset=None, in_=h2d[l][:, :],
                                            in_offset=bass.IndirectOffsetOnAxis(ap=icol[0:C, p:p + 1], axis=0)) \
                        .then_inc(s[f"xg_ready{p}"], 16)

                for j in range(4):
                    gather(j, 0)
                with pool.Fori(1, NE // 4) as i:
                    for j in range(4):
                        gather(j, i)
                nx = pool.value_load(meta[l][0:1, 15:16], min_val=0, max_val=OVER)
                with pool.If(nx > 0):
                    pool.wait_ge(s["xgt_full"], NE - 1)
                    def extra(j):
                        G.tensor_copy(icol[0:C, 0:1], idx[0:C, bass.ds(NE + j, 1)]).then_inc(s["ov_icol"], 1)
                        wait_apart(pool, s["ov_icol"], j + 1)
                        pool.indirect_dma_start(out=xg[0:C, 0, :], out_offset=None, in_=h2d[l][:, :],
                                                in_offset=bass.IndirectOffsetOnAxis(ap=icol[0:C, 0:1], axis=0)) \
                            .then_inc(s["ov_xg"], 16)
                        wait_apart(pool, s["ov_stored"], 32 * j + 32)

                    extra(0)
                    with pool.If(nx > 1):
                        with pool.Fori(1, OVER) as j:
                            with pool.If(nx > j):
                                extra(j)
                for p in range(2):
                    pool.wait_ge(s[f"y_stored{p}"], 32 * NE // 2)
                for t in range(nt):
                    p = t // (nt // 2)
                    for m in range(2):
                        pool.indirect_dma_start(out=yg[:, 2 * t + m, :], out_offset=None, in_=yd[l][:, :],
                                                in_offset=bass.IndirectOffsetOnAxis(ap=sl[:, m, t:t + 1], axis=0)) \
                            .then_inc(s[f"yg_ready{p}"], 16)

            add_squares(S[1], range(KD), 2, 2)

        @block.sync
        def _(sp):
            Dn = number["d"]
            sp.dma_start(silc[:, 16:32], a["cvec"]).then_inc(loaded, 16)
            sp.dma_start(vec, a["vecs"]).then_inc(loaded, 16)
            sp.dma_start(con[:, :], a["con"]).then_inc(loaded, 16)
            sp.dma_start(fing[:, :], a["final_g"]).then_inc(loaded, 16)
            sp.dma_start(rcon, a["rcon"]).then_inc(loaded, 16)

            def load(n):
                kind, l, i = units[n]
                slot, src = ring[:, n % NRING, :], a["out_w" if kind == "out" else kind[:2] if kind[:2] in ("mg", "mo") else kind]\
                    [l, int(kind[2]) if kind[:2] in ("mg", "mo") else i]
                if n >= NRING:
                    b, e = unit_end[units[n - NRING]]
                    sp.wait_ge(full[b], e)
                sp.dma_start(slot[:, 0:src.shape[1]], src).then_inc(ring_ready[n % NRING], 16)

            def expert(l, j, i, e):
                s = S[l]
                if not (isinstance(i, int) and i == 0):
                    sp.wait_ge(s["gu_full"], i * 4 + j - 3)
                for m, n_ in enumerate(("w_gate", "w_up")):
                    sp.dma_start(gu[j][:, 2048 * m:2048 * m + 2048].unsqueeze(1),
                                 a[n_][l][bass.ds(e, 1)].rearrange("e p n -> p e n")).then_inc(s[f"gu_ready{j}"], 16)
                if not (isinstance(i, int) and i == 0):
                    sp.wait_ge(s["y_full"], i * 4 + j - 3)
                sp.dma_start(wd[:, j:j + 1, :], a["w_down"][l][bass.ds(e, 1)].rearrange("e p n -> p e n")) \
                    .then_inc(s[f"wd_ready{j}"], 16)

            n = 0
            for l in range(DEPTH):
                s = S[l]
                while n < len(units) and (l == 1 or n < first_of_layer1):
                    load(n)
                    n += 1
                    if n == NRING and l == 0:
                        sp.dma_start(x, a["x"]).then_inc(x_loaded, 16)
                        sp.dma_start(wr, a["router"][0]).then_inc(router_loaded, 16)
                b, e = unit_end[("out", l, 1)]
                sp.wait_ge(full[b], e)
                last = {m % NRING: unit_end[units[m]] for m in range(n - NRING, n)}
                for j in range(4):
                    if j in last:
                        sp.wait_ge(full[last[j][0]], last[j][1])
                    expert(l, j, 0, j)
                if l == 0:
                    sp.wait_ge(full["d"], Dn[("router", 0)])
                    sp.dma_start(wr, a["router"][1]).then_inc(router_loaded, 16)
                with sp.Fori(1, NE // 4) as i:
                    for j in range(4):
                        expert(l, j, i, i * 4 + j)
                sp.wait_ge(s["slots_ready"], 1)
                nx = sp.value_load(meta[l][0:1, 15:16], min_val=0, max_val=OVER)
                with sp.If(nx > 0):
                    sp.wait_ge(s["gu_full"], NE - 3)
                    sp.wait_ge(s["y_full"], NE - 3)
                    def extra(j):
                        e = sp.value_load(meta[l][0:1, bass.ds(j, 1)], min_val=0, max_val=NE - 1)
                        for m, n_ in enumerate(("w_gate", "w_up")):
                            sp.dma_start(gu[0][:, 2048 * m:2048 * m + 2048].unsqueeze(1),
                                         a[n_][l][bass.ds(e, 1)].rearrange("e p n -> p e n")).then_inc(s["ov_w"], 16)
                        sp.dma_start(wd[:, 0:1, :], a["w_down"][l][bass.ds(e, 1)].rearrange("e p n -> p e n")) \
                            .then_inc(s["ov_w"], 16)
                        wait_apart(sp, s["ov_stored"], 32 * j + 32)

                    extra(0)
                    with sp.If(nx > 1):
                        with sp.Fori(1, OVER) as j:
                            with sp.If(nx > j):
                                extra(j)
                sp.wait_ge(s["gu_full"], NE)
                for p in range(2):
                    sp.wait_ge(s[f"yg_ready{p}"], 32 * (2 if l == 0 else 1))
            sp.wait_ge(out_ready, 1)
            sp.dma_start(a["out"].rearrange("(k p) t -> p k t", p=128), h[:, :, CTX:T]).then_inc(out_stored, 16)
            sp.wait_ge(out_stored, 16)


def tables():
    con = np.zeros((128, NC), np.float32)
    con[:, 0:128] = np.eye(128)
    con[:, 128:130] = np.arange(128)[:, None] % 32 == np.arange(2)
    tok = np.arange(SEQ)
    row, colm = (tok // GRID_W).astype(np.float32), (tok % GRID_W).astype(np.float32)
    for dim, c, s_, rows in ((2 * DH // 2, "cos_d", "sin_d", None), (ROPE, "cos_a", "sin_a", 64)):
        n = dim // 4
        inv = (np.float32(ROPE_BASE) ** (-np.arange(n, dtype=np.float32) / np.float32(n))).astype(np.float32)
        ang = np.concatenate([row[:, None] * inv, colm[:, None] * inv], -1).astype(np.float32)
        cos, sin = np.cos(ang).T, np.sin(ang).T
        if rows is None:
            con[:, CON[c][0]:CON[c][1]] = np.concatenate([cos] * 4)
            con[:, CON[s_][0]:CON[s_][1]] = np.concatenate([sin, -sin] * 2)
        else:
            con[rows:rows + 32, CON[c][0]:CON[c][1]] = np.concatenate([cos] * 2)
            con[rows:rows + 32, CON[s_][0]:CON[s_][1]] = np.concatenate([-sin, sin])
    r = np.zeros((128, NRC), np.float32)
    r[:, 0:128] = np.triu(np.ones((128, 128)), 1)
    for n_, v in (("desc4", np.arange(NG, 0, -1)), ("desc32", np.arange(NE, 0, -1)), ("expert", np.arange(NE)),
                  ("nth", np.arange(OVER))):
        r[:, RCON[n_][0]:RCON[n_][1]] = v
    r[:, RCON["token"][0]:RCON["token"][1]] = np.arange(128)[:, None] + 128 * np.arange(4)
    return con, r


def kernel(x, c, ctx, c_ctx, w_ada, b_ada, norm1_g, w_in, q_norm_g, w_uq, kv_norm_g, w_ukv, conv_w, conv_b,
           conv_ln_g, conv_ln_b, lam_q1, lam_k1, lam_q2, lam_k2, diff_subln_g, w_o_mla, w_o_conv, w_o_diff, w_out,
           norm2_g, w_rg, b_rg, w_re, b_re, w_gate, w_up, w_down, final_g):
    import concourse.bacc as bacc
    from concourse.bass_utils import run_bass_kernel_spmd as run

    L = DEPTH
    A = np.asarray

    def rows(w, k):
        w = A(w)
        return w.reshape(L, k, 128, w.shape[-1]).transpose(0, 2, 1, 3)

    def flat(w, lead):
        w = np.ascontiguousarray(w)
        return w.reshape(w.shape[:lead] + (-1,))

    def part(v):
        v = A(v)
        return v.reshape(L, -1, 128).transpose(0, 2, 1)

    def alike(v):
        v = A(v)
        return np.broadcast_to(v[:, None, :], (L, 128, v.shape[-1]))

    win = rows(w_in, KD)
    o_glu, o_q = LW, LW + 2 * CC
    o_k, o_v, o_g = o_q + HD * 2 * DH, o_q + 2 * HD * 2 * DH, o_q + 3 * HD * 2 * DH
    glu = win[..., o_glu:o_q].reshape(L, 128, KD, 2, 2, 2, 128)
    gates = win[..., o_g:].reshape(L, 128, KD, 3, KD, 128)
    wo = np.concatenate([rows(w, 4) for w in (w_o_mla, w_o_conv, w_o_diff)], 2).reshape(L, 128, 12, KD, 128)
    con, rcon = tables()
    vecs = np.concatenate([part(norm1_g), part(norm2_g), part(b_ada), part(q_norm_g), part(kv_norm_g),
                           A(conv_w).reshape(L, CW, CT, 128).transpose(0, 3, 2, 1).reshape(L, 128, CT * CW),
                           part(conv_b), part(conv_ln_g), part(conv_ln_b), part(diff_subln_g),
                           alike(lam_q1), alike(lam_k1), alike(lam_q2), alike(lam_k2), alike(b_rg), alike(b_re)], 2)
    arrays = {
        "cvec": np.stack([A(c)[0], A(c_ctx)], 1).reshape(KD, 128, 2).transpose(1, 0, 2).reshape(128, 2 * KD),
        "vecs": vecs.transpose(1, 0, 2),
        "con": con, "rcon": rcon,
        "final_g": A(final_g).reshape(KD, 128).T,
        "x": np.concatenate([A(ctx)[0], A(x)[0]], 0).T.reshape(KD, 128, T).transpose(1, 0, 2),
        "router": np.concatenate([rows(w_rg, KD), rows(w_re, KD)], 3),
        "ada": flat(rows(w_ada, KD).reshape(L, 128, KD, NADA, 512).transpose(0, 3, 1, 2, 4), 3),
        "lora": flat(win[:, None, :, :, 0:LW], 3),
        "glu": flat(glu.transpose(0, 4, 1, 2, 5, 3, 6), 3),
        "dq": flat(win[:, None, :, :, o_q:o_k], 3),
        "dk": flat(win[:, None, :, :, o_k:o_v], 3),
        "dv": flat(win[:, None, :, :, o_v:o_g], 3),
        "ukv": np.concatenate([flat(rows(w_uq, 2), 2), A(w_ukv)], 2)[:, None],
        "mg": flat(gates.transpose(0, 3, 4, 1, 2, 5)[:, [1, 0, 2]].reshape(L, 6, 4, 128, KD, 128)
                   .transpose(0, 1, 3, 2, 4, 5), 3),
        "mo": flat(wo.reshape(L, 128, 3, 4, KD, 128).transpose(0, 2, 1, 4, 3, 5)[:, [1, 0, 2]], 3),
        "out_w": flat(rows(w_out, KD).reshape(L, 128, KD, 2, 512).transpose(0, 3, 1, 2, 4), 3),
        "w_gate": A(w_gate).reshape(L, NE, KD, 128, FF).transpose(0, 1, 3, 2, 4).reshape(L, NE, 128, KD * FF),
        "w_up": A(w_up).reshape(L, NE, KD, 128, FF).transpose(0, 1, 3, 2, 4).reshape(L, NE, 128, KD * FF),
        "w_down": A(w_down).reshape(L, NE, 2, 128, D).transpose(0, 1, 3, 2, 4).reshape(L, NE, 128, 2 * D),
    }
    nc = bacc.Bacc("TRN2", target_bir_lowering=False, num_devices=1)
    aps, given = {}, {}
    for name, v in arrays.items():
        v = np.ascontiguousarray(v)
        given[f"{name}_in"] = v
        aps[name] = nc.dram_tensor(f"{name}_in", v.shape, mybir.dt.float32, kind="ExternalInput").ap()
    out = nc.dram_tensor("result", (D, SEQ), mybir.dt.float32, kind="ExternalOutput").ap()
    build(nc, dict(aps, out=out))
    r = run(nc, [given], core_ids=[0])
    return np.ascontiguousarray(r.results[0]["result"].T).reshape(1, SEQ, D)
```
